# Optimizing a Trainium2 kernel written in Bass

```python
import jax, jax.numpy as jnp
from jax import lax
import numpy as np

D_MODEL = 1024
BATCH = 1
SEQ = 256
DEPTH = 2

N_META = 16
BLOCK = 128
WINDOW = 128
HEAD_DIM = 64
N_Q_HEADS = D_MODEL // HEAD_DIM
N_KV_HEADS = 4
Q_PER_KV = N_Q_HEADS // N_KV_HEADS
QKV_DIM = (N_Q_HEADS + 2 * N_KV_HEADS) * HEAD_DIM
RWKV_HEAD = 64
RWKV_HEADS = D_MODEL // RWKV_HEAD
DECAY_LORA = max(32, int(round(1.8 * D_MODEL ** 0.5 / 32)) * 32)
AAA_LORA = max(32, int(round(1.8 * D_MODEL ** 0.5 / 32)) * 32)
GATE_LORA = max(32, int(round(0.6 * D_MODEL ** 0.8 / 32)) * 32)
N_MIX = 6
D_FF = 7 * D_MODEL // 2
N_EXPERTS = 8
TOP_K = 2
N_ATTN = (DEPTH + 1) // 2
N_RWKV = DEPTH // 2
NORM_EPS = 1e-5
GN_EPS = 64e-5

kernel_name = 'hybrid_swa_sink_rwkv7_moe_meta'

def rmsnorm(x, g, eps=NORM_EPS):
    xf = x.astype(jnp.float32)
    y = xf * lax.rsqrt(jnp.mean(xf * xf, axis=-1, keepdims=True) + eps)
    return (y * g.astype(jnp.float32)).astype(x.dtype)

def swiglu(h, w_gate, w_up, w_down):
    return (jax.nn.silu(h @ w_gate) * (h @ w_up)) @ w_down

def swa_sink_attention(h, w_qkv, q_gain, k_gain, sinks, w_o):
    B, T, _ = h.shape
    pad = BLOCK - N_META
    Tp = T + pad
    nb = Tp // BLOCK
    qkv = jnp.pad(h @ w_qkv, ((0, 0), (pad, 0), (0, 0)))
    q, k, v = jnp.split(qkv, [N_Q_HEADS * HEAD_DIM, (N_Q_HEADS + N_KV_HEADS) * HEAD_DIM], axis=-1)
    q = rmsnorm(q.reshape(B, Tp, N_Q_HEADS, HEAD_DIM), q_gain)
    k = rmsnorm(k.reshape(B, Tp, N_KV_HEADS, HEAD_DIM), k_gain)
    v = v.reshape(B, Tp, N_KV_HEADS, HEAD_DIM)
    qb = q.reshape(B, nb, BLOCK, N_KV_HEADS, Q_PER_KV, HEAD_DIM)
    kb = k.reshape(B, nb, BLOCK, N_KV_HEADS, HEAD_DIM)
    vb = v.reshape(B, nb, BLOCK, N_KV_HEADS, HEAD_DIM)

    def with_prev(t):
        prev = jnp.pad(t, ((0, 0), (1, 0), (0, 0), (0, 0), (0, 0)))[:, :-1]
        return jnp.concatenate([prev, t], axis=2)

    k_band, v_band = with_prev(kb), with_prev(vb)
    k_meta, v_meta = k[:, pad:BLOCK], v[:, pad:BLOCK]
    scale = HEAD_DIM ** -0.5
    s_band = jnp.einsum('bnqkgd,bnjkd->bnkgqj', qb, k_band, preferred_element_type=jnp.float32) * scale
    s_meta = jnp.einsum('bnqkgd,bmkd->bnkgqm', qb, k_meta, preferred_element_type=jnp.float32) * scale

    q_pos = jnp.arange(nb)[:, None] * BLOCK + jnp.arange(BLOCK)[None, :]
    k_pos = (jnp.arange(nb)[:, None] - 1) * BLOCK + jnp.arange(2 * BLOCK)[None, :]
    diff = q_pos[:, :, None] - k_pos[:, None, :]
    band_ok = (k_pos[:, None, :] >= BLOCK) & (diff >= 0) & (diff < WINDOW)
    meta_pos = pad + jnp.arange(N_META)
    meta_ok = meta_pos[None, None, :] <= q_pos[:, :, None]
    s_band = jnp.where(band_ok[None, :, None, None], s_band, -jnp.inf)
    s_meta = jnp.where(meta_ok[None, :, None, None], s_meta, -jnp.inf)
    sink = jnp.broadcast_to(sinks.astype(jnp.float32).reshape(1, 1, N_KV_HEADS, Q_PER_KV, 1, 1),
                            s_meta.shape[:-1] + (1,))
    p = jax.nn.softmax(jnp.concatenate([s_meta, s_band, sink], axis=-1), axis=-1)
    p_meta = p[..., :N_META].astype(v.dtype)
    p_band = p[..., N_META:N_META + 2 * BLOCK].astype(v.dtype)
    o = (jnp.einsum('bnkgqm,bmkd->bnqkgd', p_meta, v_meta)
         + jnp.einsum('bnkgqj,bnjkd->bnqkgd', p_band, v_band))
    o = o.reshape(B, Tp, N_Q_HEADS * HEAD_DIM)[:, pad:]
    return o @ w_o

def rwkv7_time_mix(h, mix, w0, w1, w2, a0, a1, a2, g1, g2, k_k, k_a, r_k,
                   w_r, w_k, w_v, w_o, gn_w, gn_b):
    B, T, D = h.shape
    H, N = RWKV_HEADS, RWKV_HEAD
    xx = jnp.pad(h, ((0, 0), (1, 0), (0, 0)))[:, :-1] - h
    xr, xw, xk, xv, xa, xg = [h + xx * mix[i] for i in range(N_MIX)]
    r = xr @ w_r
    k = xk @ w_k
    v = xv @ w_v
    w = -jax.nn.softplus(-(w0 + jnp.tanh(xw @ w1) @ w2)) - 0.5
    a = jax.nn.sigmoid(a0 + (xa @ a1) @ a2)
    g = jax.nn.sigmoid(xg @ g1) @ g2
    kk = (k * k_k).astype(jnp.float32).reshape(B, T, H, N)
    kk = kk / jnp.maximum(jnp.linalg.norm(kk, axis=-1, keepdims=True), 1e-12)
    k = k * (1 + (a - 1) * k_a)

    to_h = lambda t: t.astype(jnp.float32).reshape(B, T, H, N)
    r_h, k_h, v_h, a_h = to_h(r), to_h(k), to_h(v), to_h(a)
    decay = jnp.exp(-jnp.exp(to_h(w)))
    aa = -kk
    bb = kk * a_h

    def step(S, inp):
        r_t, w_t, k_t, v_t, a_t, b_t = inp
        sa = jnp.einsum('bhvk,bhk->bhv', S, a_t)
        S = S * w_t[:, :, None, :] + sa[..., None] * b_t[:, :, None, :] + v_t[..., None] * k_t[:, :, None, :]
        return S, jnp.einsum('bhvk,bhk->bhv', S, r_t)

    xs = tuple(jnp.swapaxes(t, 0, 1) for t in (r_h, decay, k_h, v_h, aa, bb))
    S0 = jnp.zeros((B, H, N, N), jnp.float32)
    _, out = lax.scan(step, S0, xs)
    out = jnp.swapaxes(out, 0, 1)
    mu = jnp.mean(out, axis=-1, keepdims=True)
    var = jnp.mean(jnp.square(out - mu), axis=-1, keepdims=True)
    out = (out - mu) * lax.rsqrt(var + GN_EPS) * gn_w.astype(jnp.float32).reshape(H, N) \
        + gn_b.astype(jnp.float32).reshape(H, N)
    bonus = jnp.sum(r_h * k_h * r_k.astype(jnp.float32), axis=-1, keepdims=True) * v_h
    y = (out + bonus).reshape(B, T, D).astype(h.dtype)
    return (y * g) @ w_o

def moe_swiglu(h, w_router, w_gate, w_up, w_down):
    probs = jax.nn.softmax((h @ w_router).astype(jnp.float32), axis=-1)
    top_p, top_i = lax.top_k(probs, TOP_K)
    top_p = top_p / jnp.sum(top_p, axis=-1, keepdims=True)
    gates = jnp.sum(jax.nn.one_hot(top_i, N_EXPERTS, dtype=jnp.float32) * top_p[..., None], axis=-2)
    y = jnp.zeros(h.shape, jnp.float32)
    for e in range(N_EXPERTS):
        y = y + gates[..., e:e + 1] * swiglu(h, w_gate[e], w_up[e], w_down[e]).astype(jnp.float32)
    return y.astype(h.dtype)

def setup_inputs(seed: int = 0) -> dict:
    key = jax.random.key(seed)
    ks = iter(jax.random.split(key, 48))
    nrm = lambda shape, scale: jax.random.normal(next(ks), shape, jnp.float32) * scale
    gain = lambda shape: 1.0 + nrm(shape, 0.02)
    D, F, E = D_MODEL, D_FF, N_EXPERTS
    NA, NR = N_ATTN, N_RWKV
    ND, NM = N_ATTN, N_RWKV
    return {
        'x': nrm((BATCH, SEQ, D), 1.0),
        'meta_tokens': nrm((N_META, D), 1.0),
        'mixer_norm': gain((DEPTH, D)),
        'ffn_norm': gain((DEPTH, D)),
        'attn_w_qkv': nrm((NA, D, QKV_DIM), D ** -0.5),
        'attn_q_norm': gain((NA, HEAD_DIM)),
        'attn_k_norm': gain((NA, HEAD_DIM)),
        'attn_sinks': nrm((NA, N_Q_HEADS), 0.5),
        'attn_w_o': nrm((NA, N_Q_HEADS * HEAD_DIM, D), (N_Q_HEADS * HEAD_DIM) ** -0.5),
        'rwkv_mix': jax.random.uniform(next(ks), (NR, N_MIX, D), jnp.float32),
        'rwkv_w0': jax.random.uniform(next(ks), (NR, D), jnp.float32, -2.0, 2.0),
        'rwkv_w1': nrm((NR, D, DECAY_LORA), D ** -0.5),
        'rwkv_w2': nrm((NR, DECAY_LORA, D), DECAY_LORA ** -0.5),
        'rwkv_a0': nrm((NR, D), 0.1),
        'rwkv_a1': nrm((NR, D, AAA_LORA), D ** -0.5),
        'rwkv_a2': nrm((NR, AAA_LORA, D), AAA_LORA ** -0.5),
        'rwkv_g1': nrm((NR, D, GATE_LORA), D ** -0.5),
        'rwkv_g2': nrm((NR, GATE_LORA, D), GATE_LORA ** -0.5),
        'rwkv_k_k': 0.85 + nrm((NR, D), 0.02),
        'rwkv_k_a': gain((NR, D)),
        'rwkv_r_k': nrm((NR, RWKV_HEADS, RWKV_HEAD), 0.1),
        'rwkv_w_r': nrm((NR, D, D), D ** -0.5),
        'rwkv_w_k': nrm((NR, D, D), D ** -0.5),
        'rwkv_w_v': nrm((NR, D, D), D ** -0.5),
        'rwkv_w_o': nrm((NR, D, D), D ** -0.5),
        'rwkv_gn_w': gain((NR, D)),
        'rwkv_gn_b': nrm((NR, D), 0.02),
        'ffn_w_gate': nrm((ND, D, F), D ** -0.5),
        'ffn_w_up': nrm((ND, D, F), D ** -0.5),
        'ffn_w_down': nrm((ND, F, D), F ** -0.5),
        'moe_router': nrm((NM, D, E), D ** -0.5),
        'moe_w_gate': nrm((NM, E, D, F), D ** -0.5),
        'moe_w_up': nrm((NM, E, D, F), D ** -0.5),
        'moe_w_down': nrm((NM, E, F, D), F ** -0.5),
    }

def reference(x, meta_tokens, mixer_norm, ffn_norm,
              attn_w_qkv, attn_q_norm, attn_k_norm, attn_sinks, attn_w_o,
              rwkv_mix, rwkv_w0, rwkv_w1, rwkv_w2, rwkv_a0, rwkv_a1, rwkv_a2,
              rwkv_g1, rwkv_g2, rwkv_k_k, rwkv_k_a, rwkv_r_k,
              rwkv_w_r, rwkv_w_k, rwkv_w_v, rwkv_w_o, rwkv_gn_w, rwkv_gn_b,
              ffn_w_gate, ffn_w_up, ffn_w_down,
              moe_router, moe_w_gate, moe_w_up, moe_w_down):
    B = x.shape[0]
    meta = jnp.broadcast_to(meta_tokens.astype(x.dtype)[None], (B, N_META, x.shape[-1]))
    h = jnp.concatenate([meta, x], axis=1)
    for i in range(DEPTH):
        j = i // 2
        u = rmsnorm(h, mixer_norm[i])
        if i % 2 == 0:
            h = h + swa_sink_attention(u, attn_w_qkv[j], attn_q_norm[j], attn_k_norm[j],
                                       attn_sinks[j], attn_w_o[j])
        else:
            h = h + rwkv7_time_mix(u, rwkv_mix[j], rwkv_w0[j], rwkv_w1[j], rwkv_w2[j],
                                   rwkv_a0[j], rwkv_a1[j], rwkv_a2[j], rwkv_g1[j], rwkv_g2[j],
                                   rwkv_k_k[j], rwkv_k_a[j], rwkv_r_k[j],
                                   rwkv_w_r[j], rwkv_w_k[j], rwkv_w_v[j], rwkv_w_o[j],
                                   rwkv_gn_w[j], rwkv_gn_b[j])
        u = rmsnorm(h, ffn_norm[i])
        if i % 2 == 0:
            h = h + swiglu(u, ffn_w_gate[j], ffn_w_up[j], ffn_w_down[j])
        else:
            h = h + moe_swiglu(u, moe_router[j], moe_w_gate[j], moe_w_up[j], moe_w_down[j])
    return h[:, N_META:]


_drawn_inputs = setup_inputs


def setup_inputs(seed=0):
    import zlib

    import numpy as np

    out = dict(_drawn_inputs(seed))
    spreads = {}
    factors = {'attn_q_norm': 3.126,
     'attn_k_norm': 3.024,
     'attn_sinks': 25.624,
     'rwkv_k_k': 40.047,
     'rwkv_k_a': 2.688,
     'rwkv_gn_w': 2.906}
    for name, (base, spread) in spreads.items():
        noise = np.random.default_rng([zlib.crc32(name.encode()), seed]).standard_normal(out[name].shape)
        drawn = base * np.exp(spread * noise) if base else spread * noise
        out[name] = __import__('jax').numpy.asarray(drawn.astype(out[name].dtype))
    for name, factor in factors.items():
        out[name] = (out[name] * factor).astype(out[name].dtype)
    return out
```

```python
import math
from contextlib import ExitStack

import concourse.bass as bass
from concourse import mybir

F32 = mybir.dt.float32
F32R = mybir.dt.float32r
I32 = mybir.dt.int32
ALU = mybir.AluOpType
ACT = mybir.ActivationFunctionType
AX = mybir.AxisListType.X

P = 128
D = 1024
KC = D // P
META = 16
SEQ = 256
T = META + SEQ
HEADS, KVH, HD = 16, 4, 64
PAIRS = HEADS // 2
FF = 3584
BLK = 512
FB = FF // BLK
QB = BLK // P
EXPERTS = 8
EPS, GN_EPS = 1e-5, 64e-5
CH = 64
PAD = CH - META
NCH = (PAD + T) // CH
TP = NCH * CH
LORA, GLORA = 64, 160
DECAY = math.exp(-0.5)
NEG = -1e30
R_MIXN, R_FFNN, R_MIX, R_W0, R_A0, R_KK, R_KA, R_RK, R_GNW, R_GNB, NROW = 0, 2, 4, 10, 11, 12, 13, 14, 15, 16, 17


class Own:

    def __init__(self, eng):
        self.eng, self.count, self.base, self.last = eng, {}, {}, None

    def done(self, ins, sem):
        ins.then_inc(sem, 1)
        k = id(sem)
        self.count[k] = self.count.get(k, 0) + 1
        self.last = (sem, k)
        return ins

    def settle(self):
        sem, k = self.last
        self.eng.wait_ge(sem, self.base.get(k, 0) + self.count[k])

    def at(self, **_):
        return None

    def body(self, bases):
        self.saved = dict(self.count)
        for sem, b in bases.items():
            self.base[id(sem)] = b
            self.count[id(sem)] = 0

    def end(self, totals):
        for sem, v in totals.items():
            self.base[id(sem)] = v
            self.count[id(sem)] = 0


def build(nc, x, meta_tokens, mixer_norm, ffn_norm, attn_w_qkv, attn_q_norm, attn_k_norm, attn_sinks, attn_w_o,
          rwkv_mix, rwkv_w0, rwkv_w1, rwkv_w2, rwkv_a0, rwkv_a1, rwkv_a2, rwkv_g1, rwkv_g2, rwkv_k_k, rwkv_k_a,
          rwkv_r_k, rwkv_w_r, rwkv_w_k, rwkv_w_v, rwkv_w_o, rwkv_gn_w, rwkv_gn_b, ffn_w_gate, ffn_w_up, ffn_w_down,
          moe_router, moe_w_gate, moe_w_up, moe_w_down, out):
    ctx = ExitStack()
    with ctx:
        def sb(name, shape, dt=F32):
            return ctx.enter_context(nc.sbuf_tensor(name, shape, dt))

        def sem(name):
            return ctx.enter_context(nc.semaphore(name))

        ident = sb("ident", [P, P])
        ones = sb("ones", [P, P])
        headones = sb("headones", [P, P])
        levelmask = sb("levelmask", [P, 5, P])
        level1T = sb("level1T", [P, P])
        causal = sb("causal", [P, 2, P])
        reset = sb("reset", [P, TP])
        slotno = sb("slotno", [P, P])
        before = sb("before", [P, P])
        expno = sb("expno", [P, 2, EXPERTS])
        expno8 = sb("expno8", [P, 2, EXPERTS])
        SEG = [(0, META + P), (META + P, T), (META + P + T, META)]
        NSC = 2 * META + P + T
        attmask = sb("attmask", [P, NSC])
        par = sb("par", [P, KC, NROW])
        one_minus_ka = sb("one_minus_ka", [P, KC])
        qgain = sb("qgain", [P, 1])
        kgain = sb("kgain", [P, 1])
        sinkrow = sb("sinkrow", [1, HEADS])
        sink = sb("sink", [P, HEADS])
        router = sb("router", [P, KC, EXPERTS])
        stat = sb("stat", [P, 2, 8, 6])
        chunkdecay = sb("chunkdecay", [P, PAIRS, NCH])
        route = sb("route", [P, 16, 2, EXPERTS])
        rcol = sb("rcol", [P, 8, 2])
        ranks = sb("ranks", [P, 3, EXPERTS])
        npass_i = sb("npass_i", [P, 1], I32)
        normcol = sb("normcol", [P, 3, 2])

        ARENA = 50048
        RAW = KC * T + 2 * KC * BLK
        SPLIT = 26752
        HALF = KC * BLK // 2
        NRAW, NRING = 7, 4
        with nc.sbuf_tensor("under_raw", [P, RAW], F32), nc.sbuf_tensor("raw_w", [P, NRAW, HALF], F32) as raw_w, \
                nc.sbuf_tensor("under_split", [P, SPLIT - RAW - NRAW * HALF], F32), \
                nc.sbuf_tensor("wsplit", [P, NRING, 2, HALF], F32R) as wsplit, \
                nc.sbuf_tensor("xsplit", [P, 2, 2, KC, P], F32R) as xsplit, \
                nc.sbuf_tensor("hsplit", [P, 2, 2, QB, P], F32R) as hsplit:
            pass
        arena = sb("arena", [P, ARENA])

        def area(off, *dims):
            n = 1
            for d in dims:
                n *= d
            assert off + n <= ARENA, (off, dims)
            v = arena[:, off:off + n]
            if len(dims) == 2:
                v = v.rearrange("p (a b) -> p a b", a=dims[0])
            elif len(dims) == 3:
                v = v.rearrange("p (a b c) -> p a b c", a=dims[0], b=dims[1])
            elif len(dims) == 4:
                v = v.rearrange("p (a b c d) -> p a b c d", a=dims[0], b=dims[1], c=dims[2])
            return v

        hT = area(0, KC, T)
        SLOT0 = KC * T
        SLOT = KC * BLK
        NSLOT = 6
        slot = [area(SLOT0 + s * SLOT, SLOT) for s in range(NSLOT)]
        slot_k = [area(SLOT0 + s * SLOT, KC, BLK) for s in range(NSLOT)]
        slot_d = [area(SLOT0 + s * SLOT, QB, D) for s in range(NSLOT)]
        UT = SLOT0 + NSLOT * SLOT
        uT = area(UT, KC, T + 1)
        A0 = UT + KC * (T + 1)
        qT = area(A0, KC, T)
        kz = area(A0 + 2176, KVH, 2, T)
        vdup = area(A0 + 4352, 3, KVH, P)
        oT = area(A0 + 5888, KC, T)
        scores = area(A0 + 8064, 2, 2, NSC)
        PTW = 512 + 256 + 512 + 32
        pT = area(A0 + 9792, 2, PTW)
        raw = area(A0 + 12416, 2, T)
        rsq = area(A0 + 12960, 2, T)
        rstd2 = area(A0 + 13504, 2, T)
        sq = area(A0 + 14048, KC, T)
        std = area(A0 + 16224, T)
        rstd = area(A0 + 16496, T)
        wkdup = area(A0 + 16768, KC, KVH, 2, HD)
        xtok = area(A0, 2, D)
        mtok = area(A0 + 2048, D)
        prow = area(A0 + 3072, D)
        hid = area(A0, FF // P, T)
        sgate = area(A0 + 7616, QB, T)
        ARR = ARENA - (6 * PAIRS * TP + 2 * PAIRS * SEQ)
        r_a, kk_a, k_a, b_a, v_a, w_a = [area(ARR + n * PAIRS * TP, PAIRS, TP) for n in range(6)]
        g_a = area(ARR + 6 * PAIRS * TP, PAIRS, SEQ)
        bonus = area(ARR + 6 * PAIRS * TP + PAIRS * SEQ, PAIRS, SEQ)
        X4 = SLOT0 + 4 * SLOT
        xx = area(X4, KC, T)
        xm = [area(X4 + 2176 * (1 + n), KC, T) for n in range(2)]
        th_w, th_a, sg_a, sg_b = [area(X4 + 6528 + n * T, T) for n in range(4)]
        assert X4 + 6528 + 4 * T <= UT
        tmp1 = area(UT, KC, T)
        tmp2 = xx
        cum = area(A0, 2, TP)
        expo = area(A0 + 2 * TP, 3, TP)
        assert A0 + 5 * TP <= ARR
        wk = SLOT0 + 2 * SLOT
        ARt = area(wk, PAIRS, 2, P)
        Bt, Kt, Vt, Bs, Ks, Vs = [area(wk + 2048 + n * 1024, PAIRS, P) for n in range(6)]
        NA = area(wk + 8192, PAIRS, 2, P)
        KA = area(wk + 10240, PAIRS, 2, P)
        X, XT, Y, RHS, U, S = [area(wk + 12288 + n * 1024, PAIRS, P) for n in range(6)]
        assert wk + 18432 <= ARR
        gn_std = area(UT, PAIRS, SEQ)
        gn_sq = area(ARR + 4096, PAIRS, SEQ)
        gainrow = area(ARR + 6144, D)
        assert UT + 2048 <= ARR
        utok = area(0, 2, D)
        hbuf = area(SLOT0, 2, BLK)
        silu = area(SLOT0 + 1024, 2, BLK)
        ye = area(SLOT0 + 2048, D)
        sel = area(SLOT0 + 3072, 2, 2, P)
        selg = area(SLOT0 + 3584, 2, 2, P)
        selT = area(SLOT0 + 4096, 2, 2, P)
        utT = area(SLOT0 + 4608, KC, SEQ)
        acc = area(RAW + NRAW * HALF, 2, D)
        assert RAW + NRAW * HALF + 2 * D <= SPLIT and SPLIT + 2 * (NRING * HALF + KC * 2 * P + QB * 2 * P) <= ARENA

        ps = ctx.enter_context(nc.psum_tensor("ps", [P, 8, 512], F32))

        ld_x, ld_meta, ld_par, ld_small, ld_gain = [sem(n) for n in ("ld_x", "ld_meta", "ld_par", "ld_small", "ld_gain")]
        slot_in = [sem(f"slot_in{s}") for s in range(NSLOT)]
        pool_own, ident_ok, consts_ok, kw_ok, kz_zero, pads_zero, work_zero = [sem(n) for n in (
            "pool_own", "ident_ok", "consts_ok", "kw_ok", "kz_zero", "pads_zero", "work_zero")]
        act_own, dve_own = sem("act_own"), sem("dve_own")
        in_tr, in_x, in_rest = sem("in_tr"), sem("in_x"), sem("in_rest")
        norm_sq, norm_ss, norm_std, norm_u = [sem(n) for n in ("norm_sq", "norm_ss", "norm_std", "norm_u")]
        qk_mm, qk_sq, qk_ss, qk_std, qk_n, v_mm, v_cp = [sem(n) for n in (
            "qk_mm", "qk_sq", "qk_ss", "qk_std", "qk_n", "v_mm", "v_cp")]
        sc_mm, sc_rd, sc_max, sc_exp, p_ok, pt_mm, pt_a, pt_d, pv_mm, o_cp = [sem(n) for n in (
            "sc_mm", "sc_rd", "sc_max", "sc_exp", "p_ok", "pt_mm", "pt_a", "pt_d", "pv_mm", "o_cp")]
        wo_mm, wo_add = sem("wo_mm"), sem("wo_add")
        gate_mm, up_mm, ffn_silu, ffn_mul, down_mm, down_add = [sem(n) for n in (
            "gate_mm", "up_mm", "ffn_silu", "ffn_mul", "down_mm", "down_add")]
        mix_ok, mix_used, lora_h, l2_mm, l2_ev, pr_mm, pr_ev = [sem(n) for n in (
            "mix_ok", "mix_used", "lora_h", "l2_mm", "l2_ev", "pr_mm", "pr_ev")]
        kk_ok, kk_sq, kk_ss, kk_ev, kk_nrm, kk_done, rk_ok, rk_mm, rk_ev = [sem(n) for n in (
            "kk_ok", "kk_sq", "kk_ss", "kk_ev", "kk_nrm", "kk_done", "rk_ok", "rk_mm", "rk_ev")]
        cum_ok, prev_ok, dec_exp, dec_done = [sem(n) for n in ("cum_ok", "prev_ok", "dec_exp", "dec_done")]
        bd_ar, bd_b, bd_kv, ap_mm, ap_ev, tr_mm, tr_ev = [sem(n) for n in (
            "bd_ar", "bd_b", "bd_kv", "ap_mm", "ap_ev", "tr_mm", "tr_ev")]
        y_mm, y_ev, x_mm, x_ok, rhs_mm, rhs_ev, u_mm, u_ev, ot_mm, ot_ev, s_mm, s_ok, rec_own = [sem(n) for n in (
            "y_mm", "y_ev", "x_mm", "x_ok", "rhs_mm", "rhs_ev", "u_mm", "u_ev", "ot_mm", "ot_ev", "s_mm", "s_ok", "rec_own")]
        ht_mm, ht_cp, gn_mm, gn_x, gn_sqd, gn_var, gn_sd, y_ok, wo2_mm, acc_ok = [sem(n) for n in (
            "ht_mm", "ht_cp", "gn_mm", "gn_x", "gn_sqd", "gn_var", "gn_sd", "y_ok", "wo2_mm", "acc_ok")]
        n4_ss, n4_std, utok_ok, utT_mm, utT_cp, lg_mm, lg_sub, lg_exp, mask_ok, rank_mm, npass_ok = [sem(n) for n in (
            "n4_ss", "n4_std", "utok_ok", "utT_mm", "utT_cp", "lg_mm", "lg_sub", "lg_exp", "mask_ok", "rank_mm", "npass_ok")]
        sel_ok, xg_mm, xg_hi, xg_ev, st_mm, st_ev = [sem(n) for n in ("sel_ok", "xg_mm", "xg_hi", "xg_ev", "st_mm", "st_ev")]
        raw_in = [sem(f"raw_in{n}") for n in range(NRAW)]
        w_hi, w_lo, w_used, et_hi = sem("w_hi"), sem("w_lo"), sem("w_used"), sem("et_hi")
        et_mm, e_silu, e_h, et_ev, ye_ev, es_mm, es_add = [sem(n) for n in (
            "et_mm", "e_silu", "e_h", "et_ev", "ye_ev", "es_mm", "es_add")]
        acc_done, out_sem = sem("acc_done"), sem("out_sem")

        block = ctx.enter_context(nc.Block())

        NB2 = 2 * FB
        TILES = []
        for j in range(2):
            TILES += [(0, j * FB), (1, j * FB)]
            for f in range(1, FB):
                TILES += [(0, j * FB + f), (1, j * FB + f), (2, j * FB + f - 1)]
            TILES.append((2, j * FB + FB - 1))
        NHALF = 2 * len(TILES)
        assert NHALF % NRAW == 0 and NHALF % NRING == 0
        NLV = 5

        @block.sync
        def _(sp):
            def cols(w, n):
                return w.rearrange("(k p) n -> p k n", p=P)[:, :, n * BLK:(n + 1) * BLK]

            def load(s, dst, src):
                sp.dma_start(dst, src).then_inc(slot_in[s], 16)

            wqkv, wo = attn_w_qkv[0], attn_w_o[0]
            wg, wu, wd = ffn_w_gate[0], ffn_w_up[0], ffn_w_down[0]
            sp.dma_start(xtok, x[0].rearrange("(t p) d -> p t d", p=P)).then_inc(ld_x, 16)
            sp.dma_start(mtok[0:META, :], meta_tokens[:, :]).then_inc(ld_meta, 16)
            for row, src in ((R_MIXN, mixer_norm), (R_FFNN, ffn_norm), (R_MIX, rwkv_mix[0]), (R_W0, rwkv_w0),
                             (R_A0, rwkv_a0), (R_KK, rwkv_k_k), (R_KA, rwkv_k_a),
                             (R_RK, rwkv_r_k.rearrange("o h n -> o (h n)")), (R_GNW, rwkv_gn_w), (R_GNB, rwkv_gn_b)):
                sp.dma_start(prow[row:row + src.shape[0], :], src).then_inc(ld_par, 16)
            load(0, slot_k[0], cols(wqkv, 0))
            for half in range(2):
                rows = slice(half * HD, (half + 1) * HD)
                sp.dma_start(qgain[rows, :], attn_q_norm.rearrange("o (n u) -> (o n) u", u=1)).then_inc(ld_small, 16)
                sp.dma_start(kgain[rows, :], attn_k_norm.rearrange("o (n u) -> (o n) u", u=1)).then_inc(ld_small, 16)
            sp.dma_start(sinkrow[:, :], attn_sinks[:, :]).then_inc(ld_small, 16)
            load(1, slot_k[1], cols(wqkv, 1))
            load(2, slot_k[2], cols(wqkv, 2))
            load(3, slot_k[3], cols(wo, 0))
            load(4, slot_k[4], cols(wo, 1))
            load(5, slot_k[5], cols(wg, 0))
            sp.dma_start(router[:, :, :], moe_router[0].rearrange("(k p) e -> p k e", p=P)).then_inc(ld_small, 16)
            sp.wait_ge(qk_mm, 4)
            load(0, slot_k[0], cols(wu, 0))
            wd_v = wd.rearrange("(r k p) n -> r p k n", p=P, k=FB)
            dk = [slot_k[1 + r][:, 0:FB, :] for r in range(4)]
            for r, (s_, n) in enumerate(((qk_mm, 8), (v_mm, 3), (wo_mm, 4), (wo_mm, 8))):
                sp.wait_ge(s_, n)
                load(1 + r, dk[r], wd_v[r, :, :, 0:BLK])
            with sp.Fori(1, FB) as f:
                sp.wait_ge(gate_mm, f * QB)
                load(5, slot_k[5], wg.rearrange("(k p) n -> p k n", p=P)[:, :, bass.ds(f * BLK, BLK)])
                sp.wait_ge(up_mm, f * QB)
                load(0, slot_k[0], wu.rearrange("(k p) n -> p k n", p=P)[:, :, bass.ds(f * BLK, BLK)])
            sp.wait_ge(up_mm, FB * QB)
            for off, w in ((0, rwkv_w1), (KC * LORA, rwkv_a1), (2 * KC * LORA, rwkv_g1)):
                n = w.shape[2]
                sp.dma_start(slot[0][:, off:off + KC * n].rearrange("p (k n) -> p k n", k=KC),
                             w[0].rearrange("(k p) n -> p k n", p=P)).then_inc(slot_in[0], 16)
            for r in range(4):
                sp.wait_ge(down_mm, r + 1)
                load(1 + r, dk[r], wd_v[r, :, :, BLK:D])
            sp.wait_ge(down_mm, 5)
            for rows, off, src in ((slice(0, 64), 0, rwkv_w2[0]), (slice(64, 128), 0, rwkv_a2[0]),
                                   (slice(0, 128), D, rwkv_g2[0, 0:P]), (slice(0, GLORA - P), 2 * D, rwkv_g2[0, P:GLORA])):
                sp.dma_start(slot[1][rows, off:off + D], src).then_inc(slot_in[1], 16)
            sp.wait_ge(down_mm, 6)
            load(2, slot_k[2], cols(rwkv_w_k[0], 0))
            sp.wait_ge(down_mm, 7)
            load(3, slot_k[3], cols(rwkv_w_k[0], 1))
            sp.wait_ge(mix_used, 3)
            load(0, slot_k[0], cols(rwkv_w_r[0], 0))
            sp.wait_ge(l2_mm, 24)
            load(1, slot_k[1], cols(rwkv_w_r[0], 1))
            for s, w, n, used in ((2, rwkv_w_v, 0, 4), (3, rwkv_w_v, 1, 8), (0, rwkv_w_o, 0, 12), (1, rwkv_w_o, 1, 16)):
                sp.wait_ge(pr_mm, used)
                load(s, slot_k[s], cols(w[0], n))
            we_g = moe_w_gate[0].rearrange("e (k p) n -> e p k n", p=P)
            we_u = moe_w_up[0].rearrange("e (k p) n -> e p k n", p=P)
            we_d = moe_w_down[0].rearrange("e (f k p) n -> e f p k n", p=P, k=QB)

            def expert_tiles(i, it):
                for n_, (kind, q) in enumerate(TILES):
                    e, f = 2 * i + q // FB, q % FB
                    for h in range(2):
                        m = 2 * n_ + h
                        sp.wait_ge(w_lo, it * NHALF + m + 1)
                        if kind < 2:
                            dst = raw_w[:, m % NRAW, :].rearrange("p (k n) -> p k n", k=KC // 2)
                            src = (we_g, we_u)[kind][e, :, h * (KC // 2):(h + 1) * (KC // 2), f * BLK:(f + 1) * BLK]
                        else:
                            dst = raw_w[:, m % NRAW, :].rearrange("p (k n) -> p k n", k=QB // 2)
                            src = we_d[e, f, :, h * (QB // 2):(h + 1) * (QB // 2), :]
                        sp.dma_start(dst, src).then_inc(raw_in[m % NRAW], 16)

            sp.wait_ge(ot_ev, 4 * NCH)
            sp.wait_ge(s_ok, 2 * NCH + 2)
            sp.dma_start(gainrow, ffn_norm[1:2, :].to_broadcast([P, D])).then_inc(ld_gain, 16)
            with sp.Fori(0, EXPERTS // 2) as i:
                expert_tiles(i, i)
            sp.wait_ge(npass_ok, 1)
            n = sp.value_load(npass_i[0:1, 0:1], min_val=1, max_val=2)
            with sp.If(n > 1):
                with sp.Fori(0, EXPERTS // 2) as i:
                    expert_tiles(i, i + EXPERTS // 2)
            sp.wait_ge(acc_done, 1)
            sp.dma_start(out[0].rearrange("(t p) d -> p t d", p=P), acc).then_inc(out_sem, 16)
            sp.wait_ge(out_sem, 16)

        @block.gpsimd
        def _(pool):
            g = nc.gpsimd
            own = Own(pool)

            def one(ins, s_=pool_own):
                own.done(ins, s_)
                own.settle()

            def keep(v, pattern, base, mult, op=ALU.is_ge, fill=0.0):
                one(g.affine_select(out=v, in_=v, pattern=pattern, compare_op=op, fill=fill, base=base,
                                    channel_multiplier=mult))

            def fill(v, value):
                one(g.memset(v, value))

            fill(ident[:, :], 0.0)
            one(g.affine_select(out=ident[:, :], in_=ident[:, :], pattern=[[-1, P]], compare_op=ALU.not_equal, fill=1.0,
                                base=0, channel_multiplier=1), ident_ok)
            fill(ones[:, :], 1.0)
            pool.wait_ge(in_x, 4)
            pool.wait_ge(in_rest, 3)
            one(g.memset(kz[:, :, :, :], 0.0), kz_zero)
            fill(uT[:, :, 0:1], 0.0)
            fill(attmask[:, :], 0.0)
            keep(attmask[:, META:META + P], [[-1, P]], 0, 1, fill=NEG)
            a = SEG[1][0] + META
            keep(attmask[:, a:a + P], [[1, P]], -1, -1, fill=NEG)
            keep(attmask[:, a + P:a + 2 * P], [[-1, P]], 0, 1, fill=NEG)
            keep(attmask[:, SEG[2][0]:NSC], [[-1, META]], 0, 1, fill=NEG)
            fill(headones[:, :], 1.0)
            hv = headones[:, :].rearrange("p (h i) -> p h i", h=2)
            keep(hv, [[-CH, 2], [0, CH]], 0, 1)
            keep(hv, [[CH, 2], [0, CH]], CH - 1, -1)
            for j in range(2):
                v = causal[:, j, :].rearrange("p (h i) -> p h i", h=2)
                fill(v, 1.0)
                keep(v, [[-CH, 2], [0, CH]], 0, 1)
                keep(v, [[CH, 2], [1, CH]], j - 1, -1)
            fill(levelmask[:, :, :], 0.0)
            for l in range(2, 7):
                b = 1 << (l - 1)
                v = levelmask[:, l - 2, :].rearrange("p (j x i) -> p j x i", x=2, i=b)[:, :, 0, :]
                fill(v, 1.0)
                keep(v, [[-2 * b, P // (2 * b)], [0, b]], -b, 1)
                keep(v, [[2 * b, P // (2 * b)], [0, b]], 2 * b - 1, -1)
            fill(level1T[:, :], 0.0)
            v = level1T[:, :].rearrange("p (j x) -> p j x", x=2)[:, :, 1]
            fill(v, 1.0)
            keep(v, [[-2, P // 2]], 0, 1, op=ALU.is_equal)
            fill(reset[:, :], 1.0)
            fill(reset[:, :].rearrange("p (c i) -> p c i", c=NCH)[:, :, 0], 0.0)
            fill(before[:, :], 1.0)
            keep(before[:, :], [[1, P]], -1, -1)
            for v, pattern, base in ((slotno[:, :], [[1, P]], 0), (expno[:, :, :], [[0, 2], [1, EXPERTS]], 0)):
                one(g.iota(v, pattern=pattern, base=base, channel_multiplier=0, allow_small_or_imprecise_dtypes=True))
            one(g.iota(expno8[:, :, :], pattern=[[0, 2], [1, EXPERTS]], base=EXPERTS, channel_multiplier=0,
                       allow_small_or_imprecise_dtypes=True), consts_ok)
            pool.wait_ge(slot_in[2], 16)
            for h in range(2):
                one(g.tensor_copy(wkdup[:, :, :, h, :], slot_k[2][:, :, 0:256].rearrange("p k (g d) -> p k g d", g=KVH)), kw_ok)
            pool.wait_ge(norm_u, 3)
            for arr in (r_a, kk_a, k_a, b_a, v_a, w_a):
                fill(arr[:, :, 0:PAD], 0.0)
            fill(th_w[HD:P, :], 0.0)
            fill(th_a[0:HD, :], 0.0)
            for lo in (32, 64, 96):
                fill(sg_b[lo:lo + 32, :], 0.0)
            pool.wait_ge(down_mm, 5)
            for lo in (32, 64, 96):
                one(g.memset(slot[1][lo:lo + 32, 2 * D:3 * D], 0.0), pads_zero)
            pool.wait_ge(dec_done, PAIRS)
            pool.wait_ge(rk_ev, PAIRS)
            pool.wait_ge(pr_ev, 24)
            for v in (ARt[:, :, :, :], Bt[:, :, :], Kt[:, :, :], Vt[:, :, :]):
                one(g.memset(v, 0.0), work_zero)
            with pool.Fori(0, NCH) as c:
                for n, (dst, src) in enumerate(((Kt, k_a), (Vt, v_a))):
                    for h in range(2):
                        rows = slice(h * CH, (h + 1) * CH)
                        g.tensor_copy(dst[rows, :, rows], src[rows, :, bass.ds(c * CH, CH)]).then_inc(bd_kv, 1)
                        pool.wait_ge(bd_kv, c * 4 + (2 * n + h + 1))
                pool.wait_ge(tr_mm, 6 * (c + 1))

        @block.tensor
        def _(pe):
            mm, tr = nc.tensor.matmul, nc.tensor.transpose

            pe.wait_ge(ident_ok, 1)
            pe.wait_ge(ld_x, 16)
            for t in range(2):
                for half in range(2):
                    for c in range(4):
                        k = half * 4 + c
                        last = tr(ps[:, 2 * t + half, c * P:(c + 1) * P], xtok[:, t, k * P:(k + 1) * P], ident[:, :])
                    last.then_inc(in_tr, 1)
            pe.wait_ge(ld_meta, 16)
            for k in range(KC):
                last = tr(ps[:, 4, k * META:(k + 1) * META], mtok[0:META, k * P:(k + 1) * P], ident[0:META, 0:META])
            last.then_inc(in_tr, 1)
            pe.wait_ge(ld_par, 160)
            for k in range(KC):
                last = tr(ps[:, 5, k * NROW:(k + 1) * NROW], prow[0:NROW, k * P:(k + 1) * P], ident[0:NROW, 0:NROW])
            last.then_inc(in_tr, 1)
            pe.wait_ge(ld_small, 16 * 6)
            pe.wait_ge(pool_own, 2)
            mm(ps[:, 6, 0:HEADS], ones[0:1, :], sinkrow[:, :], start=True, stop=True).then_inc(in_tr, 1)

            def norm(n):
                pe.wait_ge(norm_sq, n)
                for k in range(KC):
                    last = mm(ps[:, 7, 0:T], ones[:, :], sq[:, k, :], start=(k == 0), stop=(k == KC - 1))
                last.then_inc(norm_ss, 1)

            norm(1)
            pe.wait_ge(norm_u, 1)
            pe.wait_ge(consts_ok, 1)

            def head_ss(m):
                pe.wait_ge(qk_sq, m + 1)
                if m >= 2:
                    pe.wait_ge(qk_std, m - 1)
                mm(ps[:, 3 + m % 2, 0:T], headones[:, :], rsq[:, m % 2, :], start=True, stop=True).then_inc(qk_ss, 1)

            for m in range(KC + KVH):
                if m in (0, 4, 8):
                    pe.wait_ge(slot_in[m // 4], 16)
                if m == KC:
                    pe.wait_ge(kw_ok, 2)
                if m >= 3:
                    pe.wait_ge(qk_sq, m - 2)
                for k in range(KC):
                    if m < KC:
                        w = slot_k[m // 4][:, k, (m % 4) * P:(m % 4 + 1) * P]
                    else:
                        w = wkdup[:, k, m - KC, :, :].rearrange("p a b -> p (a b)")
                    last = mm(ps[:, m % 3, 0:T], w, uT[:, k, 1:T + 1], start=(k == 0), stop=(k == KC - 1))
                last.then_inc(qk_mm, 1)
                if m >= 1:
                    head_ss(m - 1)
            for t in range(3):
                n = P if t < 2 else META
                for k in range(KC):
                    last = mm(ps[0:n, 5 + t, 0:256], uT[:, k, 1 + t * P:1 + t * P + n], slot_k[2][:, k, 256:512],
                              start=(k == 0), stop=(k == KC - 1))
                last.then_inc(v_mm, 1)
            head_ss(KC + KVH - 1)

            def score(c):
                g = c // 2
                if c >= 1:
                    pe.wait_ge(sc_rd, c)
                mm(ps[:, 0, 0:2 * (META + P)], qT[:, c, META:META + P], kz[:, g, :, 0:META + P], start=True, stop=True)
                mm(ps[0:META, 0, 288:288 + 2 * META], qT[:, c, 0:META], kz[:, g, :, 0:META], start=True, stop=True)
                for h in range(2):
                    last = mm(ps[:, 1 + h, 0:T], qT[:, c, META + P:T], kz[:, g, h, :], start=True, stop=True)
                last.then_inc(sc_mm, 1)

            pe.wait_ge(qk_n, KC + KVH)
            pe.wait_ge(v_cp, 3)
            score(0)
            for c in range(PAIRS):
                g, b = c // 2, c % 2
                if c + 1 < PAIRS:
                    score(c + 1)
                pe.wait_ge(p_ok, c + 1)
                if c >= 1:
                    pe.wait_ge(pt_a, c)
                    pe.wait_ge(pt_d, c)
                for h in range(2):
                    p1, p2, p0 = [scores[:, b, h, o:o + n] for o, n in SEG]
                    hs = slice(h * P, (h + 1) * P)
                    tr(ps[:, 3, h * P:h * P + P], p1[:, 0:P], ident[:, :])
                    tr(ps[:, 3, 256 + h * P:256 + h * P + P], p2[:, 0:P], ident[:, :])
                    tr(ps[:, 4, h * P:h * P + P], p2[:, P:2 * P], ident[:, :])
                    tr(ps[0:META, 5, h * P:h * P + P], p1[:, P:P + META], ident[:, :])
                    tr(ps[0:META, 5, 256 + h * P:256 + h * P + P], p2[:, 2 * P:T], ident[:, :])
                    last = tr(ps[0:META, 4, 256 + h * META:256 + (h + 1) * META], p0[0:META, :], ident[0:META, 0:META])
                last.then_inc(pt_mm, 1)
                pe.wait_ge(pt_a, c + 1)
                pe.wait_ge(pt_d, c + 1)
                if c >= 1:
                    pe.wait_ge(o_cp, c)
                pt = pT[:, b, :]
                mm(ps[:, 6, 0:256], vdup[:, 0, g, :], pt[:, 0:256], start=True, stop=False)
                mm(ps[:, 6, 0:256], vdup[0:META, 1, g, :], pt[0:META, 768:1024], start=False, stop=True)
                mm(ps[:, 6, 256:512], vdup[:, 0, g, :], pt[:, 256:512], start=True, stop=False)
                mm(ps[:, 6, 256:512], vdup[:, 1, g, :], pt[:, 512:768], start=False, stop=False)
                mm(ps[:, 6, 256:512], vdup[0:META, 2, g, :], pt[0:META, 1024:1280], start=False, stop=True)
                mm(ps[:, 7, 0:2 * META], vdup[0:META, 0, g, :], pt[0:META, 1280:1312], start=True, stop=True)\
                    .then_inc(pv_mm, 1)

            pe.wait_ge(o_cp, PAIRS)
            for m in range(KC):
                if m in (0, 4):
                    pe.wait_ge(slot_in[3 + m // 4], 16)
                if m >= 4:
                    pe.wait_ge(wo_add, m - 3)
                for k in range(KC):
                    last = mm(ps[:, m % 4, 0:T], slot_k[3 + m // 4][:, k, (m % 4) * P:(m % 4 + 1) * P], oT[:, k, :],
                              start=(k == 0), stop=(k == KC - 1))
                last.then_inc(wo_mm, 1)
            norm(2)

            pe.wait_ge(norm_u, 2)
            with pe.Fori(0, FB) as f:
                for s, b0, made, free, loads in ((5, 0, gate_mm, ffn_silu, 1), (0, 4, up_mm, ffn_mul, 2)):
                    pe.wait_ge(slot_in[s], f * 16 + 16 * loads)
                    for q in range(QB):
                        pe.wait_ge(free, f * QB + (q + 1))
                        for k in range(KC):
                            last = mm(ps[:, b0 + q, 0:T], slot_k[s][:, k, q * P:(q + 1) * P], uT[:, k, 1:T + 1],
                                      start=(k == 0), stop=(k == KC - 1))
                        last.then_inc(made, 1)
            pe.wait_ge(ffn_mul, QB + FB * QB)
            with pe.Fori(0, 2) as hf:
                for r in range(4):
                    pe.wait_ge(slot_in[1 + r], hf * 16 + 32)
                    for k in range(FB):
                        for q in range(QB):
                            last = mm(ps[:, q, 0:T], slot_k[1 + r][:, k, q * P:(q + 1) * P], hid[:, r * FB + k, :],
                                      start=(r + k == 0), stop=(r == 3 and k == FB - 1))
                    last.then_inc(down_mm, 1)
                pe.wait_ge(down_add, (hf + 1) * QB)
            norm(3)

            pe.wait_ge(slot_in[0], 16 * 11)
            pe.wait_ge(mix_ok, 1)
            l1 = [slot[0][:, o:o + KC * n].rearrange("p (k n) -> p k n", k=KC)
                  for o, n in ((0, LORA), (KC * LORA, LORA), (2 * KC * LORA, GLORA))]
            for k in range(KC):
                last = mm(ps[0:LORA, 0, 0:T], l1[0][:, k, :], xm[0][:, k, :], start=(k == 0), stop=(k == KC - 1))
            last.then_inc(mix_used, 1)
            pe.wait_ge(mix_ok, 2)
            for k in range(KC):
                last = mm(ps[HD:P, 1, 0:T], l1[1][:, k, :], xm[1][:, k, :], start=(k == 0), stop=(k == KC - 1))
            last.then_inc(mix_used, 1)
            pe.wait_ge(mix_ok, 3)
            for k in range(KC):
                mm(ps[:, 2, 0:T], l1[2][:, k, 0:P], xm[0][:, k, :], start=(k == 0), stop=(k == KC - 1))
            for k in range(KC):
                last = mm(ps[0:GLORA - P, 3, 0:T], l1[2][:, k, P:GLORA], xm[0][:, k, :], start=(k == 0), stop=(k == KC - 1))
            last.then_inc(mix_used, 1)
            pe.wait_ge(slot_in[1], 16 * 7)
            pe.wait_ge(pads_zero, 3)
            for j in range(3 * KC):
                which, m = j // KC, j % KC
                if m == 0:
                    pe.wait_ge(lora_h, (1, 2, 4)[which])
                if j >= 4:
                    pe.wait_ge(l2_ev, j - 3)
                bank = ps[:, 4 + j % 4, 0:T]
                cs = slice(m * P, (m + 1) * P)
                if which < 2:
                    last = mm(bank, slot[1][:, cs], (th_w, th_a)[which], start=True, stop=True)
                else:
                    mm(bank, slot[1][:, D + m * P:D + (m + 1) * P], sg_a, start=True, stop=False)
                    last = mm(bank, slot[1][:, 2 * D + m * P:2 * D + (m + 1) * P], sg_b, start=False, stop=True)
                last.then_inc(l2_mm, 1)

            def project(j):
                which, m = j // KC, j % KC
                s = (2, 0, 2)[which] + m // 4
                if m == 0:
                    pe.wait_ge(mix_ok, 4 + which)
                if m % 4 == 0:
                    pe.wait_ge(slot_in[s], 16 * ({2: 4, 3: 4, 0: 12, 1: 8}[s] + (which == 2)))
                if j >= 4:
                    pe.wait_ge(pr_ev, j - 3)
                for k in range(KC):
                    last = mm(ps[:, j % 4, 0:T], slot_k[s][:, k, (m % 4) * P:(m % 4 + 1) * P], xm[(3 + which) % 2][:, k, :],
                              start=(k == 0), stop=(k == KC - 1))
                last.then_inc(pr_mm, 1)

            def per_head(m, src, ready, n, made, read):
                pe.wait_ge(ready, n)
                if m >= 4:
                    pe.wait_ge(read, m - 3)
                mm(ps[:, 4 + m % 4, 0:T], headones[:, :], src[:, m, :], start=True, stop=True).then_inc(made, 1)

            pe.wait_ge(lora_h, 4)
            for j in range(12):
                project(j)
            pe.wait_ge(l2_ev, 24)
            for m in range(PAIRS):
                per_head(m, tmp2, kk_sq, m + 1, kk_ss, kk_ev)
            for j in range(12, 24):
                project(j)
            for m in range(PAIRS):
                per_head(m, tmp2, rk_ok, m + 1, rk_mm, rk_ev)

            pe.wait_ge(work_zero, 4)
            with pe.Fori(0, NCH) as c:
                pe.wait_ge(bd_ar, c + 1)
                pe.wait_ge(bd_b, c + 1)
                for h in range(2):
                    for p in range(4):
                        last = mm(ps[:, 4 * h + p // 2, (p % 2) * 256:(p % 2 + 1) * 256], Bt[:, 4 * h + p, :],
                                  ARt[:, 4 * h + p, :, :], start=True, stop=True)
                    last.then_inc(ap_mm, 1)
                pe.wait_ge(bd_kv, c * 4 + 4)
                for h in range(2):
                    for p in range(4):
                        last = mm(ps[:, 4 * h + 2 + p // 2, (p % 2) * 256:(p % 2 + 1) * 256], Kt[:, 4 * h + p, :],
                                  ARt[:, 4 * h + p, :, :], start=True, stop=True)
                    last.then_inc(ap_mm, 1)
                for n, src in enumerate((Bt, Kt, Vt)):
                    for h in range(2):
                        pe.wait_ge(ap_ev, c * 4 + (1 + h if n < 2 else 3 + h))
                        for p in range(4):
                            last = tr(ps[:, 4 * h + n, p * P:(p + 1) * P], src[:, 4 * h + p, :], ident[:, :])
                        last.then_inc(tr_mm, 1)
                for h in range(2):
                    pe.wait_ge(tr_ev, c * 6 + 5 + h)
                    pe.wait_ge(s_ok, c * 2 + h + 1)
                    for p in range(4 * h, 4 * h + 4):
                        o = ps[:, 4 * h + 1, (p % 4) * P:(p % 4 + 1) * P]
                        mm(o, ARt[:, p, 0, :], S[:, p, :], start=True, stop=False)
                        last = mm(o, KA[:, p, 0, :], Vs[:, p, :], start=False, stop=True)
                    last.then_inc(rhs_mm, 1)
                for l in range(NLV):
                    for h in range(2):
                        pe.wait_ge(x_ok, c * 12 + 2 * l + h + 1)
                        for p in range(4 * h, 4 * h + 4):
                            last = mm(ps[:, 4 * h + 3, (p % 4) * P:(p % 4 + 1) * P], NA[:, p, 0, :], X[:, p, :],
                                      start=True, stop=True)
                        last.then_inc(y_mm, 1)
                    for h in range(2):
                        pe.wait_ge(y_ev, c * 10 + 2 * l + h + 1)
                        for p in range(4 * h, 4 * h + 4):
                            o = ps[:, 4 * h, (p % 4) * P:(p % 4 + 1) * P]
                            if l < NLV - 1:
                                last = mm(o, XT[:, p, :], Y[:, p, :], start=True, stop=True)
                            else:
                                last = mm(o, Y[:, p, :], XT[:, p, :], start=True, stop=True)
                        last.then_inc(x_mm, 1)
                for h in range(2):
                    pe.wait_ge(x_ok, c * 12 + 11 + h)
                    pe.wait_ge(rhs_ev, c * 2 + h + 1)
                    for p in range(4 * h, 4 * h + 4):
                        last = mm(ps[:, 4 * h + 2, (p % 4) * P:(p % 4 + 1) * P], XT[:, p, :], RHS[:, p, :], start=True, stop=True)
                    last.then_inc(u_mm, 1)
                for h in range(2):
                    pe.wait_ge(u_ev, c * 2 + h + 1)
                    for p in range(4 * h, 4 * h + 4):
                        o = ps[:, 4 * h + 1, (p % 4) * P:(p % 4 + 1) * P]
                        mm(o, S[:, p, :], ARt[:, p, 1, :], start=True, stop=False)
                        mm(o, U[:, p, :], NA[:, p, 1, :], start=False, stop=False)
                        last = mm(o, Vs[:, p, :], KA[:, p, 1, :], start=False, stop=True)
                    last.then_inc(ot_mm, 1)
                for h in range(2):
                    for p in range(4 * h, 4 * h + 4):
                        o = ps[:, 4 * h + 3, (p % 4) * P:(p % 4 + 1) * P]
                        mm(o, Bs[:, p, :], U[:, p, :], start=True, stop=False)
                        last = mm(o, Ks[:, p, :], Vs[:, p, :], start=False, stop=True)
                    last.then_inc(s_mm, 1)

            pe.wait_ge(s_ok, 2 * NCH + 2)
            pe.wait_ge(ot_ev, 4 * NCH)
            for t in range(2):
                for half in range(2):
                    for q in range(4):
                        k = 4 * half + q
                        last = tr(ps[:, 2 * t + half, q * P:(q + 1) * P], hT[:, k, META + t * P:META + (t + 1) * P], ident[:, :])
                    last.then_inc(ht_mm, 1)
            for m in range(PAIRS):
                if m >= 4:
                    pe.wait_ge(gn_x, m - 3)
                mm(ps[:, 4 + m % 4, 0:SEQ], headones[:, :], w_a[:, m, CH:TP], start=True, stop=True).then_inc(gn_mm, 1)
            pe.wait_ge(ht_cp, 4)
            for m in range(PAIRS):
                pe.wait_ge(gn_sqd, m + 1)
                if m >= 4:
                    pe.wait_ge(gn_sd, m - 3)
                mm(ps[:, m % 4, 0:SEQ], headones[:, :], gn_sq[:, m, :], start=True, stop=True).then_inc(gn_var, 1)

            pe.wait_ge(y_ok, PAIRS)
            pe.wait_ge(gn_sd, PAIRS)
            pe.wait_ge(slot_in[0], 16 * 13)
            pe.wait_ge(slot_in[1], 16 * 9)
            for t in range(2):
                for n in range(2):
                    for k in range(KC):
                        last = mm(ps[:, 2 * t + n, :], w_a[:, k, CH + t * P:CH + (t + 1) * P], slot_k[n][:, k, :],
                                  start=(k == 0), stop=(k == KC - 1))
                    last.then_inc(wo2_mm, 1)

            for m in range(KC):
                if m == 0:
                    pe.wait_ge(utok_ok, 2)
                    pe.wait_ge(gn_x, PAIRS)
                for t in range(2):
                    last = tr(ps[:, 4 + m // 2, (m % 2) * SEQ + t * P:(m % 2) * SEQ + (t + 1) * P],
                              utok[:, t, m * P:(m + 1) * P], ident[:, :])
                if m % 2:
                    last.then_inc(utT_mm, 1)
            pe.wait_ge(acc_ok, 4)
            pe.wait_ge(utT_cp, 4)
            for t in range(2):
                for k in range(KC):
                    last = mm(ps[:, 0, t * EXPERTS:(t + 1) * EXPERTS], utT[:, k, t * P:(t + 1) * P], router[:, k, :],
                              start=(k == 0), stop=(k == KC - 1))
            last.then_inc(lg_mm, 1)
            chosen = route[:, 0, :, :]
            pe.wait_ge(mask_ok, 1)
            mm(ps[:, 1, 0:8], before[:, :], chosen[:, 0, :], start=True, stop=True)
            mm(ps[:, 1, 8:16], ones[:, :], chosen[:, 0, :], start=True, stop=False)
            mm(ps[:, 1, 8:16], before[:, :], chosen[:, 1, :], start=False, stop=True)
            mm(ps[:, 1, 16:24], ones[:, :], chosen[:, 0, :], start=True, stop=False)
            mm(ps[:, 1, 16:24], ones[:, :], chosen[:, 1, :], start=False, stop=True).then_inc(rank_mm, 1)

            pe.sem_inc(w_used, NRING)
            pe.wait_ge(npass_ok, 1)
            n = pe.value_load(npass_i[0:1, 0:1], min_val=1, max_val=2)
            with pe.Fori(0, n) as pas:
                with pe.Fori(0, EXPERTS // 2) as i:
                    it = pas * 4 + i

                    def gather(j):
                        pe.wait_ge(sel_ok, it * 2 + j + 1)
                        pe.wait_ge(et_ev, it * NB2 + (1 if j == 0 else FB))
                        pe.wait_ge(es_add, it * 8 + 1)
                        for half in range(2):
                            for q in range(4):
                                k = 4 * half + q
                                for t in range(2):
                                    last = mm(ps[:, 4 + half, q * P:(q + 1) * P], utok[:, t, k * P:(k + 1) * P],
                                              sel[:, j, t, :], start=(t == 0), stop=(t == 1))
                            last.then_inc(xg_mm, 1)

                    def sel_tr(j):
                        pe.wait_ge(xg_ev, it * 4 + 2 * j + 2)
                        for t in range(2):
                            last = tr(ps[:, 5, t * P:(t + 1) * P], selg[:, j, t, :], ident[:, :])
                        last.then_inc(st_mm, 1)

                    def half_tile(m, k):
                        pe.wait_ge(w_lo, it * NHALF + (m + NRAW + 1))
                        return [wsplit[:, m % NRING, part, :].rearrange("p (k n) -> p k n", k=k) for part in range(2)]

                    def split_mm(o, x_, w_, first, last):
                        mm(o, x_[0], w_[0], start=first, stop=False)
                        mm(o, x_[0], w_[1], start=False, stop=False)
                        return mm(o, x_[1], w_[0], start=False, stop=last)

                    def gate_up(j, f, kind):
                        q = j * FB + f
                        m = 2 * TILES.index((kind, q))
                        pe.wait_ge((e_silu, e_h)[kind], it * NB2 + q + 1)
                        for h in range(2):
                            whi, wlo = half_tile(m + h, KC // 2)
                            for kk in range(KC // 2):
                                k = h * (KC // 2) + kk
                                last = split_mm(ps[:, 2 * kind + q % 2, :], (xsplit[:, j, 0, k, :], xsplit[:, j, 1, k, :]),
                                                (whi[:, kk, :], wlo[:, kk, :]), k == 0, k == KC - 1)
                            last.then_inc(w_used, 1)

                    def hidden_tr(j, f):
                        q = j * FB + f
                        pe.wait_ge(e_h, it * NB2 + q + 3)
                        pe.wait_ge(et_ev, it * NB2 + q + 1)
                        if q == FB:
                            pe.wait_ge(es_add, it * 8 + 5)
                        for k in range(QB):
                            last = tr(ps[:, 4, k * P:(k + 1) * P], hbuf[:, q % 2, k * P:(k + 1) * P], ident[:, :])
                        last.then_inc(et_mm, 1)

                    def down(j, f):
                        q = j * FB + f
                        m = 2 * TILES.index((2, q))
                        pe.wait_ge(et_ev, it * NB2 + q + 2)
                        if f == 0:
                            pe.wait_ge(ye_ev, it * 2 + j + 1)
                        for h in range(2):
                            whi, wlo = half_tile(m + h, QB // 2)
                            for kk in range(QB // 2):
                                k = h * (QB // 2) + kk
                                for n_ in range(2):
                                    cs = slice(n_ * BLK, (n_ + 1) * BLK)
                                    last = split_mm(ps[:, 6 + n_, :], (hsplit[:, q % 2, 0, k, :], hsplit[:, q % 2, 1, k, :]),
                                                    (whi[:, kk, cs], wlo[:, kk, cs]), f + k == 0, f == FB - 1 and k == QB - 1)
                            last.then_inc(w_used, 1)

                    def scatter(j):
                        pe.wait_ge(ye_ev, it * 2 + j + 2)
                        pe.wait_ge(st_ev, it * 2 + 2)
                        for o in range(4):
                            t, n_ = o // 2, o % 2
                            if o >= 2:
                                pe.wait_ge(es_add, it * 8 + (4 * j + o))
                            mm(ps[:, 5 - o % 2, :], selT[:, j, t, :], ye[:, n_ * BLK:(n_ + 1) * BLK],
                               start=True, stop=True).then_inc(es_mm, 1)

                    gather(0)
                    sel_tr(0)
                    for j in range(2):
                        gate_up(j, 0, 0)
                        if j == 1:
                            scatter(0)
                        gate_up(j, 0, 1)
                        for f in range(1, FB):
                            gate_up(j, f, 0)
                            hidden_tr(j, f - 1)
                            gate_up(j, f, 1)
                            down(j, f - 1)
                        if j == 0:
                            gather(1)
                            pe.wait_ge(xg_ev, it * 4 + 4)
                        hidden_tr(j, FB - 1)
                        if j == 0:
                            sel_tr(1)
                        down(j, FB - 1)
                    scatter(1)

        @block.scalar
        def _(act):
            A = nc.scalar.activation
            own = Own(act)
            for t in range(2):
                for half in range(2):
                    b = 2 * t + half
                    act.wait_ge(in_tr, b + 1)
                    own.done(A(hT[:, 4 * half:4 * half + 4, META + t * P:META + (t + 1) * P],
                               ps[:, b, :].rearrange("p (a b) -> p a b", a=4), ACT.Copy), in_x)

            def norm(n):
                act.wait_ge(*((in_rest, 1) if n == 1 else (wo_add, KC) if n == 2 else (down_add, KC)))
                own.settle()
                own.done(A(sq, hT, ACT.Square), norm_sq)
                act.wait_ge(norm_ss, n)
                own.done(A(std, ps[:, 7, 0:T], ACT.Sqrt, bias=epsD, scale=1.0 / D), norm_std)

            epsD, eps_q, eps_k, eps_gn = [normcol[:, 0, 0:1], normcol[:, 0, 1:2], normcol[:, 0, 0:1], normcol[:, 1, 0:1]]
            act.wait_ge(dve_own, 3)
            norm(1)

            def head_std(m):
                act.wait_ge(qk_ss, m + 1)
                if m >= 2:
                    act.wait_ge(qk_n, m - 1)
                b = ps[:, 3 + m % 2, 0:T]
                if m < KC:
                    own.done(A(rstd2[:, m % 2, :], b, ACT.Sqrt, bias=eps_q), qk_std)
                else:
                    own.done(A(rstd2[:, m % 2, :], b, ACT.Sqrt, bias=eps_k, scale=1.0 / HD), qk_std)

            for m in range(KC + KVH):
                act.wait_ge(qk_mm, m + 1)
                if m >= 2:
                    act.wait_ge(qk_ss, m - 1)
                    act.wait_ge(qk_n, m - 1)
                A(raw[:, m % 2, :], ps[:, m % 3, 0:T], ACT.Copy)
                own.done(A(rsq[:, m % 2, :], ps[:, m % 3, 0:T], ACT.Square), qk_sq)
                if m >= 1:
                    head_std(m - 1)
            for t in range(3):
                n = P if t < 2 else META
                act.wait_ge(v_mm, t + 1)
                for half in range(2):
                    last = A(vdup[0:n, t, :, half * HD:(half + 1) * HD],
                             ps[0:n, 5 + t, 0:256].rearrange("p (g d) -> p g d", g=KVH), ACT.Copy)
                own.done(last, v_cp)
            head_std(KC + KVH - 1)

            def exps(c):
                b = c % 2
                act.wait_ge(sc_max, c + 1)
                for h in range(2):
                    for s_, (o, n) in enumerate(SEG):
                        v = scores[:, b, h, o:o + n]
                        A(v, v, ACT.Exp, bias=stat[:, b, 1, 3 * h + s_:3 * h + s_ + 1],
                          accum_out=stat[:, b, 2, 3 * h + s_:3 * h + s_ + 1])
                own.done(A(stat[:, b, 4, :], stat[:, b, 3, :], ACT.Exp), sc_exp)

            def copies(c):
                b = c % 2
                act.wait_ge(pt_mm, c + 1)
                if c >= 2:
                    act.wait_ge(pv_mm, c - 1)
                own.done(A(pT[:, b, 0:512], ps[:, 3, :], ACT.Copy), pt_a)
                act.wait_ge(pv_mm, c + 1)
                for h in range(2):
                    rows = slice(h * HD, (h + 1) * HD)
                    A(oT[rows, c, 0:META], ps[rows, 7, h * META:(h + 1) * META], ACT.Copy)
                    last = A(oT[rows, c, META:T].rearrange("p (b q) -> p b q", b=2),
                             ps[rows, 6, :].rearrange("p (b h q) -> p b h q", b=2, h=2)[:, :, h, :], ACT.Copy)
                own.done(last, o_cp)

            for c in range(PAIRS):
                exps(c)
                if c >= 1:
                    copies(c - 1)
            copies(PAIRS - 1)
            norm(2)

            act.sem_inc(ffn_silu, QB)
            with act.Fori(0, FB) as f:
                for q in range(QB):
                    act.wait_ge(gate_mm, f * QB + (q + 1))
                    act.wait_ge(ffn_mul, f * QB + (q + 1))
                    A(sgate[:, q, :], ps[:, q, 0:T], ACT.Silu).then_inc(ffn_silu, 1)
            norm(3)

            act.wait_ge(pads_zero, 3)
            act.wait_ge(mix_used, 1)
            own.done(A(th_w[0:HD, :], ps[0:HD, 0, 0:T], ACT.Tanh), lora_h)
            act.wait_ge(mix_used, 2)
            own.done(A(th_a[HD:P, :], ps[HD:P, 1, 0:T], ACT.Copy), lora_h)
            act.wait_ge(mix_used, 3)
            own.done(A(sg_a, ps[:, 2, 0:T], ACT.Sigmoid), lora_h)
            own.done(A(sg_b[0:GLORA - P, :], ps[0:GLORA - P, 3, 0:T], ACT.Sigmoid), lora_h)
            for j in range(3 * KC):
                which, m = j // KC, j % KC
                act.wait_ge(l2_mm, j + 1)
                bank = ps[:, 4 + j % 4, 0:T]
                if which == 0:
                    own.done(A(w_a[:, m, PAD:TP], bank, ACT.Sigmoid, bias=par[:, m, R_W0:R_W0 + 1]), l2_ev)
                elif which == 1:
                    own.done(A(b_a[:, m, PAD:TP], bank, ACT.Sigmoid, bias=par[:, m, R_A0:R_A0 + 1]), l2_ev)
                else:
                    own.done(A(g_a[:, m, :], bank[:, META:T], ACT.Copy), l2_ev)

            def take(j):
                which, m = j // KC, j % KC
                act.wait_ge(pr_mm, j + 1)
                own.done(A((k_a, r_a, v_a)[which][:, m, PAD:TP], ps[:, j % 4, 0:T], ACT.Copy), pr_ev)

            for j in range(8):
                take(j)
            for m in range(PAIRS):
                act.wait_ge(kk_ok, m + 1)
                own.done(A(tmp2[:, m, :], kk_a[:, m, PAD:TP], ACT.Square), kk_sq)
            for j in range(8, 16):
                take(j)
            act.wait_ge(kk_ev, PAIRS)
            own.done(A(tmp1, tmp1, ACT.Sqrt), kk_nrm)
            for j in range(16, 24):
                take(j)
            for m in range(PAIRS):
                act.wait_ge(cum_ok, m + 1)
                if m >= 1:
                    act.wait_ge(dec_done, m)
                A(expo[:, 0, :], cum[:, m % 2, :], ACT.Exp, scale=-DECAY)
                A(expo[:, 1, :], cum[:, m % 2, :], ACT.Exp, scale=DECAY)
                own.done(A(expo[:, 2, :], w_a[:, m, :], ACT.Exp, scale=-DECAY), dec_exp)

            act.wait_ge(work_zero, 4)
            with act.Fori(0, NCH) as c:
                for h in range(2):
                    rows = slice(h * CH, (h + 1) * CH)
                    last = A(Bt[rows, :, rows], b_a[rows, :, bass.ds(c * CH, CH)], ACT.Copy)
                last.then_inc(bd_b, 1)
                for n, dst in enumerate((Bs, Ks, Vs)):
                    for h in range(2):
                        act.wait_ge(tr_mm, c * 6 + 2 * n + h + 1)
                        A(dst[:, 4 * h:4 * h + 4, :], ps[:, 4 * h + n, :].rearrange("p (a b) -> p a b", a=4), ACT.Copy)\
                            .then_inc(tr_ev, 1)
                for made, b, dst, evicted in ((rhs_mm, 1, RHS, rhs_ev), (u_mm, 2, U, u_ev)):
                    for h in range(2):
                        act.wait_ge(made, c * 2 + h + 1)
                        A(dst[:, 4 * h:4 * h + 4, :], ps[:, 4 * h + b, :].rearrange("p (a b) -> p a b", a=4), ACT.Copy)\
                            .then_inc(evicted, 1)
                for h in range(2):
                    act.wait_ge(ot_mm, c * 2 + h + 1)
                    for e in range(2):
                        rows = slice(e * CH, (e + 1) * CH)
                        A(w_a[rows, 4 * h:4 * h + 4, bass.ds(c * CH, CH)],
                          ps[rows, 4 * h + 1, :].rearrange("p (a b) -> p a b", a=4)[:, :, rows], ACT.Copy).then_inc(ot_ev, 1)

            for b in range(4):
                act.wait_ge(ht_mm, b + 1)
                t, half = b // 2, b % 2
                own.done(A(acc[:, t, half * 512:(half + 1) * 512], ps[:, b, :], ACT.Copy), ht_cp)
            for m in range(PAIRS):
                act.wait_ge(gn_x, m + 1)
                own.done(A(gn_sq[:, m, :], w_a[:, m, CH:TP], ACT.Square), gn_sqd)
            for m in range(PAIRS):
                act.wait_ge(gn_var, m + 1)
                own.done(A(gn_std[:, m, :], ps[:, m % 4, 0:SEQ], ACT.Sqrt, bias=eps_gn, scale=1.0 / HD), gn_sd)
            for t in range(2):
                act.wait_ge(acc_ok, 2 * t + 2)
                own.done(A(utok[:, t, :], acc[:, t, :], ACT.Square, accum_out=normcol[:, 2, t:t + 1]), n4_ss)
            own.settle()
            own.done(A(rcol[:, 6, :], normcol[:, 2, :], ACT.Sqrt, bias=epsD, scale=1.0 / D), n4_std)
            for b in range(4):
                act.wait_ge(utT_mm, b + 1)
                own.done(A(utT[:, 2 * b:2 * b + 2, :], ps[:, 4 + b, :].rearrange("p (a b) -> p a b", a=2), ACT.Copy), utT_cp)
            act.wait_ge(lg_sub, 1)
            own.done(A(route[:, 2, :, :], route[:, 1, :, :], ACT.Exp), lg_exp)

            act.sem_inc(e_silu, 2)
            act.sem_inc(ye_ev, 1)
            act.wait_ge(npass_ok, 1)
            n = act.value_load(npass_i[0:1, 0:1], min_val=1, max_val=2)
            with act.Fori(0, n) as pas:
                with act.Fori(0, EXPERTS // 2) as i:
                    it = pas * 4 + i

                    def made(n_):
                        act.wait_ge(w_used, it * NHALF + (2 * n_ + 2 + NRING))

                    def highs(a, b):
                        for m in range(a, min(b, NHALF)):
                            act.wait_ge(raw_in[m % NRAW], it * (16 * NHALF // NRAW) + 16 * (m // NRAW + 1))
                            act.wait_ge(w_used, it * NHALF + m + 1)
                            A(wsplit[:, m % NRING, 0, :], raw_w[:, m % NRAW, :], ACT.Copy).then_inc(w_hi, 1)

                    def tokens(j):
                        for half in range(2):
                            act.wait_ge(xg_mm, it * 4 + (2 * j + half + 1))
                            A(xsplit[:, j, 0, 4 * half:4 * half + 4, :], ps[:, 4 + half, :].rearrange("p (a b) -> p a b", a=4),
                              ACT.Copy).then_inc(xg_hi, 1)

                    def hidden(q):
                        act.wait_ge(et_mm, it * NB2 + q + 1)
                        A(hsplit[:, q % 2, 0, :, :], ps[:, 4, :].rearrange("p (a b) -> p a b", a=QB), ACT.Copy).then_inc(et_hi, 1)

                    highs(0, 2)
                    tokens(0)
                    highs(2, NRING)
                    for n_, (kind, q) in enumerate(TILES):
                        if kind == 0:
                            made(n_)
                            act.wait_ge(e_h, it * NB2 + q + 1)
                            A(silu[:, q % 2, :], ps[:, q % 2, :], ACT.Silu).then_inc(e_silu, 1)
                            if q % FB:
                                hidden(q - 1)
                        elif kind == 2 and q % FB == FB - 1:
                            if q < FB:
                                tokens(1)
                            hidden(q)
                            made(n_)
                            A(ye, ps[:, 6:8, :].rearrange("p a b -> p (a b)"), ACT.Copy).then_inc(ye_ev, 1)
                        highs(2 * n_ + NRING, 2 * n_ + 2 + NRING)

        @block.vector
        def _(dve):
            v = nc.vector
            own = Own(dve)
            own.done(v.memset(normcol[:, 0, 0:1], EPS), dve_own)
            own.done(v.memset(normcol[:, 0, 1:2], HD * EPS), dve_own)
            own.done(v.memset(normcol[:, 1, 0:1], GN_EPS), dve_own)
            dve.wait_ge(in_tr, 5)
            own.done(v.tensor_copy(hT[:, :, 0:META], ps[:, 4, 0:KC * META].rearrange("p (k t) -> p k t", k=KC)), in_rest)
            dve.wait_ge(in_tr, 6)
            own.done(v.tensor_copy(par[:, :, :], ps[:, 5, 0:KC * NROW].rearrange("p (k t) -> p k t", k=KC)), in_rest)
            dve.wait_ge(in_tr, 7)
            own.done(v.tensor_copy(sink[:, :], ps[:, 6, 0:HEADS]), in_rest)
            own.settle()
            own.done(v.tensor_scalar(one_minus_ka[:, :], par[:, :, R_KA], -1.0, 1.0, ALU.mult, ALU.add), dve_own)

            def norm(n):
                dve.wait_ge(norm_std, n)
                own.done(v.reciprocal(rstd, std), dve_own)
                own.settle()
                row = (R_MIXN, R_FFNN, R_MIXN + 1)[n - 1]
                for k in range(KC):
                    last = v.scalar_tensor_tensor(uT[:, k, 1:T + 1], hT[:, k, :], par[:, k, row:row + 1], rstd,
                                                  ALU.mult, ALU.mult)
                own.done(last, norm_u)

            norm(1)
            dve.wait_ge(kz_zero, 1)
            dve.wait_ge(ld_small, 16 * 6)
            for m in range(KC + KVH):
                dve.wait_ge(qk_std, m + 1)
                rs = rstd2[:, m % 2, :]
                own.done(v.reciprocal(rs, rs), dve_own)
                own.settle()
                if m < KC:
                    last = v.scalar_tensor_tensor(qT[:, m, :], raw[:, m % 2, :], qgain[:, 0:1], rs, ALU.mult, ALU.mult)
                else:
                    for h in range(2):
                        rows = slice(h * HD, (h + 1) * HD)
                        last = v.scalar_tensor_tensor(kz[rows, m - KC, h, :], raw[rows, m % 2, :], kgain[rows, 0:1],
                                                      rs[rows, :], ALU.mult, ALU.mult)
                own.done(last, qk_n)

            def masked(c):
                b = c % 2
                dve.wait_ge(sc_mm, c + 1)
                if c >= 2:
                    dve.wait_ge(pt_mm, c - 1)
                o1, o2, o0 = [scores[:, b, :, o:o + n] for o, n in SEG]
                m1, m2, m0 = [attmask[:, o:o + n].unsqueeze(1).to_broadcast([P, 2, n]) for o, n in SEG]
                v.tensor_tensor(o1, ps[:, 0, 0:288].rearrange("p (h k) -> p h k", h=2), m1, ALU.add)
                v.tensor_tensor(o0[0:META], ps[0:META, 0, 288:320].rearrange("p (h k) -> p h k", h=2), m0[0:META], ALU.add)
                own.done(v.tensor_tensor(o2, ps[:, 1:3, 0:T], m2, ALU.add), sc_rd)
                own.settle()
                st = stat[:, b, :, :].rearrange("p a (h s) -> p a h s", h=2)
                for s_, o in enumerate((o1, o2, o0)):
                    last = v.tensor_reduce(st[:, 0, :, s_], o, AX, ALU.max)
                own.done(last, dve_own)
                own.settle()
                sk = sink[:, 2 * c:2 * c + 2].unsqueeze(2).to_broadcast([P, 2, 3])
                own.done(v.tensor_tensor(st[:, 0], st[:, 0], sk, ALU.max), dve_own)
                own.settle()
                own.done(v.tensor_scalar(st[:, 1], st[:, 0], -1.0, None, ALU.mult), dve_own)
                own.settle()
                own.done(v.tensor_tensor(st[:, 3], st[:, 1], sk, ALU.add), sc_max)

            def normed(c):
                b = c % 2
                dve.wait_ge(sc_exp, c + 1)
                own.done(v.tensor_tensor(stat[:, b, 5, :], stat[:, b, 2, :], stat[:, b, 4, :], ALU.add), dve_own)
                own.settle()
                own.done(v.reciprocal(stat[:, b, 6, :], stat[:, b, 5, :]), dve_own)
                own.settle()
                st = stat[:, b, 6, :].rearrange("p (h s) -> p h s", h=2)
                for s_, (o, n) in enumerate(SEG):
                    w = scores[:, b, :, o:o + n]
                    last = v.tensor_tensor(w, w, st[:, :, s_:s_ + 1].to_broadcast([P, 2, n]), ALU.mult)
                own.done(last, p_ok)

            def copies(c):
                dve.wait_ge(pt_mm, c + 1)
                if c >= 2:
                    dve.wait_ge(pv_mm, c - 1)
                b = c % 2
                v.tensor_copy(pT[:, b, 512:768], ps[:, 4, 0:256])
                v.tensor_copy(pT[0:META, b, 1280:1312], ps[0:META, 4, 256:288])
                own.done(v.tensor_copy(pT[0:META, b, 768:1280], ps[0:META, 5, :]), pt_d)

            dve.wait_ge(consts_ok, 1)
            own.done(v.memset(scores[:, :, :, :], 0.0), dve_own)
            own.done(v.memset(stat[:, :, :, :], 0.0), dve_own)
            own.settle()
            masked(0)
            for c in range(PAIRS):
                if c >= 1:
                    copies(c - 1)
                if c + 1 < PAIRS:
                    masked(c + 1)
                normed(c)
            copies(PAIRS - 1)
            for m in range(KC):
                dve.wait_ge(wo_mm, m + 1)
                own.done(v.tensor_tensor(hT[:, m, :], hT[:, m, :], ps[:, m % 4, 0:T], ALU.add), wo_add)
            norm(2)

            dve.sem_inc(ffn_mul, QB)
            with dve.Fori(0, FB) as f:
                for q in range(QB):
                    dve.wait_ge(up_mm, f * QB + (q + 1))
                    dve.wait_ge(ffn_silu, f * QB + (q + 1 + QB))
                    v.tensor_tensor(hid[:, bass.ds(f * QB + q, 1), :], sgate[:, q:q + 1, :], ps[:, 4 + q:5 + q, 0:T],
                                    ALU.mult).then_inc(ffn_mul, 1)
            with dve.Fori(0, 2) as hf:
                dve.wait_ge(down_mm, (hf + 1) * 4)
                for q in range(QB):
                    hv = hT[:, bass.ds(hf * QB + q, 1), :]
                    v.tensor_tensor(hv, hv, ps[:, q:q + 1, 0:T], ALU.add).then_inc(down_add, 1)
            dve.wait_ge(down_add, KC)
            norm(3)

            own.settle()
            own.done(v.tensor_tensor(xx, uT[:, :, 0:T], uT[:, :, 1:T + 1], ALU.subtract), dve_own)
            own.settle()
            for j, i in enumerate((1, 4, 5, 2, 0, 3)):
                if j >= 2:
                    dve.wait_ge(*((mix_used, j - 1) if j < 5 else (pr_mm, 8)))
                for k in range(KC):
                    last = v.scalar_tensor_tensor(xm[j % 2][:, k, :], xx[:, k, :], par[:, k, R_MIX + i:R_MIX + i + 1],
                                                  uT[:, k, 1:T + 1], ALU.mult, ALU.add)
                own.done(last, mix_ok)
            own.settle()
            for m in range(PAIRS):
                dve.wait_ge(pr_ev, m + 1)
                own.done(v.tensor_scalar(kk_a[:, m, PAD:TP], k_a[:, m, PAD:TP], par[:, m, R_KK:R_KK + 1], None, ALU.mult), kk_ok)
            for m in range(PAIRS):
                dve.wait_ge(kk_ss, m + 1)
                own.done(v.tensor_scalar(tmp1[:, m, :], ps[:, 4 + m % 4, 0:T], 1e-24, None, ALU.max), kk_ev)
            for m in range(PAIRS):
                last = v.tensor_scalar(tmp2[:, m, :], b_a[:, m, PAD:TP], par[:, m, R_KA:R_KA + 1],
                                       one_minus_ka[:, m:m + 1], ALU.mult, ALU.add)
            own.done(last, dve_own)
            own.settle()
            own.done(v.tensor_tensor(k_a[:, :, PAD:TP], k_a[:, :, PAD:TP], tmp2, ALU.mult), dve_own)
            dve.wait_ge(kk_nrm, 1)
            own.done(v.reciprocal(tmp1, tmp1), dve_own)
            own.settle()
            own.done(v.tensor_tensor(kk_a[:, :, PAD:TP], kk_a[:, :, PAD:TP], tmp1, ALU.mult), dve_own)
            own.settle()
            own.done(v.tensor_tensor(b_a[:, :, PAD:TP], b_a[:, :, PAD:TP], kk_a[:, :, PAD:TP], ALU.mult), dve_own)
            for m in range(PAIRS):
                dve.wait_ge(pr_ev, 9 + m)
                own.done(v.scalar_tensor_tensor(tmp2[:, m, :], r_a[:, m, PAD:TP], par[:, m, R_RK:R_RK + 1],
                                                k_a[:, m, PAD:TP], ALU.mult, ALU.mult), rk_ok)
            dve.wait_ge(pads_zero, 3)
            dve.wait_ge(l2_ev, KC)
            dve.wait_ge(rk_ok, PAIRS)
            for m in range(PAIRS):
                own.done(v.tensor_tensor_scan(cum[:, m % 2, :], reset[:, :], w_a[:, m, :], 0.0, ALU.mult, ALU.add), dve_own)
                own.settle()
                own.done(v.tensor_tensor(w_a[:, m, :], cum[:, m % 2, :], w_a[:, m, :], ALU.subtract), cum_ok)
                dve.wait_ge(dec_exp, m + 1)
                v.tensor_tensor(r_a[:, m, :], r_a[:, m, :], expo[:, 0, :], ALU.mult)
                v.tensor_copy(chunkdecay[:, m, :], expo[:, 0, :].rearrange("p (c i) -> p c i", c=NCH)[:, :, CH - 1])
                v.tensor_tensor(b_a[:, m, :], b_a[:, m, :], expo[:, 1, :], ALU.mult)
                v.tensor_tensor(k_a[:, m, :], k_a[:, m, :], expo[:, 1, :], ALU.mult)
                own.done(v.scalar_tensor_tensor(kk_a[:, m, :], kk_a[:, m, :], -1.0, expo[:, 2, :], ALU.mult, ALU.mult), dec_done)
            for m in range(PAIRS):
                dve.wait_ge(rk_mm, m + 1)
                dve.wait_ge(pr_ev, 17 + m)
                own.done(v.tensor_tensor(bonus[:, m, :], ps[:, 4 + m % 4, META:T], v_a[:, m, CH:TP], ALU.mult), rk_ev)

            dve.wait_ge(work_zero, 4)
            v.memset(S[:, 0:4, :], 0.0).then_inc(s_ok, 1)
            v.memset(S[:, 4:8, :], 0.0).then_inc(s_ok, 1)
            own.settle()
            bc = lambda m_: m_.unsqueeze(1).to_broadcast([P, 4, P])
            with dve.Fori(0, NCH) as c:
                for src, j in ((kk_a, 0), (r_a, 1)):
                    for h in range(2):
                        rows = slice(h * CH, (h + 1) * CH)
                        last = v.tensor_copy(ARt[rows, :, j, rows], src[rows, :, bass.ds(c * CH, CH)])
                last.then_inc(bd_ar, 1)
                halves = [slice(4 * h, 4 * h + 4) for h in range(2)]

                def products(n):
                    dst, h = (NA, KA)[n // 2], n % 2
                    dve.wait_ge(ap_mm, c * 4 + n + 1)
                    for q in range(2):
                        last = v.tensor_tensor(
                            dst[:, 4 * h + 2 * q:4 * h + 2 * q + 2, :, :].rearrange("p a b c -> p a (b c)"),
                            ps[:, 4 * h + 2 * (n // 2) + q, :].rearrange("p (a b) -> p a b", a=2),
                            causal[:, :, :].rearrange("p b c -> p (b c)").unsqueeze(1).to_broadcast([P, 2, 2 * P]), ALU.mult)
                    last.then_inc(ap_ev, 1)

                for n in range(4):
                    products(n)
                dve.wait_ge(ap_ev, c * 4 + 4)
                for hs in halves:
                    last = v.tensor_tensor(XT[:, hs, :], NA[:, hs, 0, :], bc(level1T[:, :]), ALU.mult)
                last.then_inc(rec_own, 1)
                dve.wait_ge(rec_own, c * 12 + 1)
                for hs in halves:
                    last = v.tensor_tensor(XT[:, hs, :], XT[:, hs, :], bc(ident[:, :]), ALU.add)
                last.then_inc(rec_own, 1)
                dve.wait_ge(rec_own, c * 12 + 2)
                for hs in halves:
                    v.transpose(X[:, hs, :].rearrange("p a b -> p (a b)"), XT[:, hs, :].rearrange("p a b -> p (a b)"))\
                        .then_inc(x_ok, 1)
                for l in range(NLV):
                    for h, hs in enumerate(halves):
                        dve.wait_ge(y_mm, c * 10 + 2 * l + h + 1)
                        v.tensor_tensor(Y[:, hs, :], ps[:, 4 * h + 3, :].rearrange("p (a b) -> p a b", a=4),
                                        bc(levelmask[:, l, :]), ALU.mult).then_inc(y_ev, 1)
                    for h, hs in enumerate(halves):
                        dve.wait_ge(x_mm, c * 10 + 2 * l + h + 1)
                        b = ps[:, 4 * h, :].rearrange("p (a b) -> p a b", a=4)
                        if l < NLV - 1:
                            v.tensor_tensor(X[:, hs, :], X[:, hs, :], b, ALU.add).then_inc(rec_own, 1)
                            dve.wait_ge(rec_own, c * 12 + 3 + 2 * l + h)
                            v.transpose(XT[:, hs, :].rearrange("p a b -> p (a b)"), X[:, hs, :].rearrange("p a b -> p (a b)"))\
                                .then_inc(x_ok, 1)
                        else:
                            v.tensor_tensor(XT[:, hs, :], XT[:, hs, :], b, ALU.add).then_inc(x_ok, 1)
                for h, hs in enumerate(halves):
                    dve.wait_ge(s_mm, c * 2 + h + 1)
                    v.tensor_tensor(S[:, hs, :], S[:, hs, :], ps[:, 4 * h + 3, :].rearrange("p (a b) -> p a b", a=4), ALU.add)\
                        .then_inc(rec_own, 1)
                    dve.wait_ge(rec_own, c * 12 + 11 + h)
                    v.tensor_tensor(S[:, hs, :], S[:, hs, :],
                                    chunkdecay[:, hs, bass.ds(c, 1)].to_broadcast([P, 4, P]), ALU.mult).then_inc(s_ok, 1)

            dve.sem_inc(w_lo, NRAW)
            for m in range(PAIRS):
                dve.wait_ge(gn_mm, m + 1)
                o = w_a[:, m, CH:TP]
                own.done(v.scalar_tensor_tensor(o, ps[:, 4 + m % 4, 0:SEQ], -1.0 / HD, o, ALU.mult, ALU.add), gn_x)
            for m in range(PAIRS):
                dve.wait_ge(gn_sd, m + 1)
                own.done(v.reciprocal(gn_std[:, m, :], gn_std[:, m, :]), dve_own)
                own.settle()
                o = w_a[:, m, CH:TP]
                own.done(v.scalar_tensor_tensor(o, o, par[:, m, R_GNW:R_GNW + 1], gn_std[:, m, :], ALU.mult, ALU.mult), dve_own)
                own.settle()
                own.done(v.scalar_tensor_tensor(o, o, par[:, m, R_GNB:R_GNB + 1], bonus[:, m, :], ALU.add, ALU.add), dve_own)
                own.settle()
                own.done(v.tensor_tensor(o, o, g_a[:, m, :], ALU.mult), y_ok)
            for n in range(4):
                t, h = n // 2, n % 2
                dve.wait_ge(wo2_mm, n + 1)
                a_ = acc[:, t, h * 512:(h + 1) * 512]
                dve.wait_ge(ht_cp, 4)
                own.done(v.tensor_tensor(a_, a_, ps[:, n, :], ALU.add), acc_ok)
            dve.wait_ge(n4_std, 1)
            dve.wait_ge(ld_gain, 16)
            own.done(v.reciprocal(rcol[:, 7, :], rcol[:, 6, :]), dve_own)
            own.settle()
            for t in range(2):
                own.done(v.scalar_tensor_tensor(utok[:, t, :], acc[:, t, :], rcol[:, 7, t:t + 1], gainrow,
                                                ALU.mult, ALU.mult), utok_ok)

            col = lambda n: rcol[:, n, :]
            wide = lambda n: rcol[:, n, :].unsqueeze(2).to_broadcast([P, 2, EXPERTS])
            rt = lambda n: route[:, n, :, :]

            def step(ins, s_=dve_own):
                own.done(ins, s_)
                own.settle()

            dve.wait_ge(lg_mm, 1)
            step(v.tensor_copy(rt(3), ps[:, 0, 0:16].rearrange("p (t e) -> p t e", t=2)))
            step(v.tensor_reduce(col(0), rt(3), AX, ALU.max))
            step(v.tensor_tensor(rt(1), rt(3), wide(0), ALU.subtract), lg_sub)
            dve.wait_ge(lg_exp, 1)
            step(v.tensor_reduce(col(1), rt(2), AX, ALU.add))
            step(v.reciprocal(col(2), col(1)))
            step(v.tensor_tensor(rt(3), rt(2), wide(2), ALU.mult))
            for n, src, best in ((0, 3, 3), (1, 7, 4)):
                step(v.tensor_reduce(col(best), rt(src), AX, ALU.max))
                step(v.tensor_tensor(rt(4), rt(src), wide(best), ALU.is_equal))
                step(v.scalar_tensor_tensor(rt(5), rt(4), -8.0, expno8[:, :, :], ALU.mult, ALU.add))
                step(v.tensor_reduce(col(5), rt(5), AX, ALU.min))
                step(v.tensor_tensor(rt(8 + n), expno[:, :, :], wide(5), ALU.is_equal))
                if n == 0:
                    step(v.scalar_tensor_tensor(rt(7), rt(8), -2.0, rt(3), ALU.mult, ALU.add))
            step(v.tensor_tensor(rt(0), rt(8), rt(9), ALU.add), mask_ok)
            step(v.tensor_tensor(rt(6), rt(3), rt(0), ALU.mult))
            step(v.tensor_reduce(col(1), rt(6), AX, ALU.add))
            step(v.reciprocal(col(2), col(1)))
            step(v.tensor_tensor(rt(10), rt(6), wide(2), ALU.mult))
            dve.wait_ge(rank_mm, 1)
            step(v.tensor_copy(ranks[:, :, :], ps[:, 1, 0:24].rearrange("p (t e) -> p t e", t=3)))
            step(v.tensor_reduce(rcol[:, 0, 0:1], ranks[:, 2, :], AX, ALU.max))
            step(v.tensor_scalar(npass_i[:, :], rcol[:, 0, 0:1], float(P), 1.0, ALU.is_gt, ALU.add), npass_ok)

            dve.sem_inc(e_h, 2)
            dve.sem_inc(et_ev, 1)
            dve.sem_inc(es_add, 1)
            n = dve.value_load(npass_i[0:1, 0:1], min_val=1, max_val=2)
            chosen, gate = route[:, 0, :, :], route[:, 10, :, :]
            with dve.Fori(0, n) as pas:
                with dve.Fori(0, EXPERTS // 2) as i:
                    it = pas * 4 + i
                    for j in range(2):
                        e = bass.ds(2 * i + j, 1)
                        for t in range(2):
                            v.tensor_scalar(sel[:, j, t, :], slotno[:, :], ranks[:, t, e], chosen[:, t, e], ALU.is_equal, ALU.mult)
                            last = v.tensor_scalar(selg[:, j, t, :], slotno[:, :], ranks[:, t, e], gate[:, t, e],
                                                   ALU.is_equal, ALU.mult)
                        last.then_inc(sel_ok, 1)

                    def lows(a, b):
                        for m in range(a, min(b, NHALF)):
                            dve.wait_ge(w_hi, it * NHALF + m + 1)
                            v.tensor_tensor(wsplit[:, m % NRING, 1, :], raw_w[:, m % NRAW, :],
                                            wsplit[:, m % NRING, 0, :].bitcast(F32), ALU.subtract).then_inc(w_lo, 1)

                    def tokens(j):
                        for half in range(2):
                            dve.wait_ge(xg_hi, it * 4 + (2 * j + half + 1))
                            ks = slice(4 * half, 4 * half + 4)
                            v.tensor_tensor(xsplit[:, j, 1, ks, :], ps[:, 4 + half, :].rearrange("p (a b) -> p a b", a=4),
                                            xsplit[:, j, 0, ks, :].bitcast(F32), ALU.subtract).then_inc(xg_ev, 1)

                    def gate_rows(j):
                        dve.wait_ge(st_mm, it * 2 + j + 1)
                        v.tensor_copy(selT[:, j, :, :], ps[:, 5, 0:256].rearrange("p (a b) -> p a b", a=2)).then_inc(st_ev, 1)

                    def hidden_lo(q):
                        dve.wait_ge(et_hi, it * NB2 + q + 1)
                        v.tensor_tensor(hsplit[:, q % 2, 1, :, :], ps[:, 4, :].rearrange("p (a b) -> p a b", a=QB),
                                        hsplit[:, q % 2, 0, :, :].bitcast(F32), ALU.subtract).then_inc(et_ev, 1)

                    def collect(j):
                        for o in range(4):
                            t, h = o // 2, o % 2
                            dve.wait_ge(es_mm, it * 8 + (4 * j + o + 1))
                            a_ = acc[:, t, h * BLK:(h + 1) * BLK]
                            v.tensor_tensor(a_, a_, ps[:, 5 - o % 2, :], ALU.add).then_inc(es_add, 1)

                    lows(0, 2)
                    tokens(0)
                    gate_rows(0)
                    lows(2, NRING)
                    for n_, (kind, q) in enumerate(TILES):
                        if kind == 0 and q % FB:
                            hidden_lo(q - 1)
                        elif kind == 1:
                            if q == FB:
                                collect(0)
                            dve.wait_ge(w_used, it * NHALF + (2 * n_ + 2 + NRING))
                            dve.wait_ge(e_silu, it * NB2 + q + 3)
                            v.tensor_tensor(hbuf[:, q % 2, :], silu[:, q % 2, :], ps[:, 2 + q % 2, :], ALU.mult).then_inc(e_h, 1)
                        elif kind == 2 and q % FB == FB - 1:
                            if q < FB:
                                tokens(1)
                            hidden_lo(q)
                            if q < FB:
                                gate_rows(1)
                        lows(2 * n_ + NRING, 2 * n_ + 2 + NRING)
                    collect(1)
                    dve.wait_ge(es_add, it * 8 + 9)
                v.tensor_scalar(ranks[:, 0:2, :], ranks[:, 0:2, :], -float(P), None, ALU.add).then_inc(rec_own, 1)
                dve.wait_ge(rec_own, pas + (12 * NCH + 1))
            dve.sem_inc(acc_done, 1)


_INS = ['x', 'meta_tokens', 'mixer_norm', 'ffn_norm', 'attn_w_qkv', 'attn_q_norm', 'attn_k_norm', 'attn_sinks',
        'attn_w_o', 'rwkv_mix', 'rwkv_w0', 'rwkv_w1', 'rwkv_w2', 'rwkv_a0', 'rwkv_a1', 'rwkv_a2', 'rwkv_g1', 'rwkv_g2',
        'rwkv_k_k', 'rwkv_k_a', 'rwkv_r_k', 'rwkv_w_r', 'rwkv_w_k', 'rwkv_w_v', 'rwkv_w_o', 'rwkv_gn_w', 'rwkv_gn_b',
        'ffn_w_gate', 'ffn_w_up', 'ffn_w_down', 'moe_router', 'moe_w_gate', 'moe_w_up', 'moe_w_down']


def kernel(**inputs):
    import numpy as _np
    import concourse.bacc as _bacc
    from concourse import mybir as _mybir
    from concourse.bass_utils import run_bass_kernel_spmd as _run

    nc = _bacc.Bacc("TRN2", target_bir_lowering=False, num_devices=1)
    arrays, args = {}, []
    for name in _INS:
        a = _np.ascontiguousarray(inputs[name])
        arrays[f"in_{name}"] = a
        args.append(nc.dram_tensor(f"in_{name}", a.shape, _mybir.dt.from_np(a.dtype), kind="ExternalInput").ap())
    args.append(nc.dram_tensor("out_0", (1, SEQ, D), _mybir.dt.float32, kind="ExternalOutput").ap())
    build(nc, *args)
    r = _run(nc, [arrays], core_ids=[0])
    return r.results[0]["out_0"]
```

```python
import math
from contextlib import ExitStack

import concourse.bass as bass
from concourse import mybir

F32 = mybir.dt.float32
F32R = mybir.dt.float32r
I32 = mybir.dt.int32
ALU = mybir.AluOpType
ACT = mybir.ActivationFunctionType
AX = mybir.AxisListType.X

P = 128
D = 1024
KC = D // P
META = 16
SEQ = 256
T = META + SEQ
HEADS, KVH, HD = 16, 4, 64
PAIRS = HEADS // 2
FF = 3584
BLK = 512
FB = FF // BLK
QB = BLK // P
EXPERTS = 8
EPS, GN_EPS = 1e-5, 64e-5
CH = 64
PAD = CH - META
NCH = (PAD + T) // CH
TP = NCH * CH
LORA, GLORA = 64, 160
DECAY = math.exp(-0.5)
NEG = -1e30
R_MIXN, R_FFNN, R_MIX, R_W0, R_A0, R_KK, R_KA, R_RK, R_GNW, R_GNB, NROW = 0, 2, 4, 10, 11, 12, 13, 14, 15, 16, 17


class Own:

    def __init__(self, eng):
        self.eng, self.count, self.base, self.last = eng, {}, {}, None

    def done(self, ins, sem):
        ins.then_inc(sem, 1)
        k = id(sem)
        self.count[k] = self.count.get(k, 0) + 1
        self.last = (sem, k)
        return ins

    def settle(self):
        sem, k = self.last
        self.eng.wait_ge(sem, self.base.get(k, 0) + self.count[k])

    def at(self, **_):
        return None

    def body(self, bases):
        self.saved = dict(self.count)
        for sem, b in bases.items():
            self.base[id(sem)] = b
            self.count[id(sem)] = 0

    def end(self, totals):
        for sem, v in totals.items():
            self.base[id(sem)] = v
            self.count[id(sem)] = 0


def build(nc, x, meta_tokens, mixer_norm, ffn_norm, attn_w_qkv, attn_q_norm, attn_k_norm, attn_sinks, attn_w_o,
          rwkv_mix, rwkv_w0, rwkv_w1, rwkv_w2, rwkv_a0, rwkv_a1, rwkv_a2, rwkv_g1, rwkv_g2, rwkv_k_k, rwkv_k_a,
          rwkv_r_k, rwkv_w_r, rwkv_w_k, rwkv_w_v, rwkv_w_o, rwkv_gn_w, rwkv_gn_b, ffn_w_gate, ffn_w_up, ffn_w_down,
          moe_router, moe_w_gate, moe_w_up, moe_w_down, out):
    ctx = ExitStack()
    with ctx:
        def sb(name, shape, dt=F32):
            return ctx.enter_context(nc.sbuf_tensor(name, shape, dt))

        def sem(name):
            return ctx.enter_context(nc.semaphore(name))

        ident = sb("ident", [P, P])
        ones = sb("ones", [P, P])
        headones = sb("headones", [P, P])
        levelmask = sb("levelmask", [P, 5, P])
        level1T = sb("level1T", [P, P])
        causal = sb("causal", [P, 2, P])
        reset = sb("reset", [P, TP])
        slotno = sb("slotno", [P, P])
        before = sb("before", [P, P])
        expno = sb("expno", [P, 2, EXPERTS])
        expno8 = sb("expno8", [P, 2, EXPERTS])
        SEG = [(0, META + P), (META + P, T), (META + P + T, META)]
        NSC = 2 * META + P + T
        attmask = sb("attmask", [P, NSC])
        par = sb("par", [P, KC, NROW])
        one_minus_ka = sb("one_minus_ka", [P, KC])
        qgain = sb("qgain", [P, 1])
        kgain = sb("kgain", [P, 1])
        sinkrow = sb("sinkrow", [1, HEADS])
        sink = sb("sink", [P, HEADS])
        router = sb("router", [P, KC, EXPERTS])
        stat = sb("stat", [P, 2, 8, 6])
        chunkdecay = sb("chunkdecay", [P, PAIRS, NCH])
        NEXT = EXPERTS + 1
        route = sb("route", [P, 16, 2, NEXT])
        rcol = sb("rcol", [P, 8, 2])
        ranks = sb("ranks", [P, 3, NEXT])
        npass_i = sb("npass_i", [P, 1], I32)
        normcol = sb("normcol", [P, 3, 2])

        ARENA = 50016
        RAW = KC * T + 2 * KC * BLK
        SPLIT = 26752
        HALF = KC * BLK // 2
        NRAW, NRING = 7, 4
        with nc.sbuf_tensor("under_raw", [P, RAW], F32), nc.sbuf_tensor("raw_w", [P, NRAW, HALF], F32) as raw_w, \
                nc.sbuf_tensor("under_split", [P, SPLIT - RAW - NRAW * HALF], F32), \
                nc.sbuf_tensor("wsplit", [P, NRING, 2, HALF], F32R) as wsplit, \
                nc.sbuf_tensor("xsplit", [P, 2, 2, KC, P], F32R) as xsplit, \
                nc.sbuf_tensor("hsplit", [P, 2, 2, QB, P], F32R) as hsplit:
            pass
        arena = sb("arena", [P, ARENA])

        def area(off, *dims):
            n = 1
            for d in dims:
                n *= d
            assert off + n <= ARENA, (off, dims)
            v = arena[:, off:off + n]
            if len(dims) == 2:
                v = v.rearrange("p (a b) -> p a b", a=dims[0])
            elif len(dims) == 3:
                v = v.rearrange("p (a b c) -> p a b c", a=dims[0], b=dims[1])
            elif len(dims) == 4:
                v = v.rearrange("p (a b c d) -> p a b c d", a=dims[0], b=dims[1], c=dims[2])
            return v

        hT = area(0, KC, T)
        SLOT0 = KC * T
        SLOT = KC * BLK
        NSLOT = 6
        slot = [area(SLOT0 + s * SLOT, SLOT) for s in range(NSLOT)]
        slot_k = [area(SLOT0 + s * SLOT, KC, BLK) for s in range(NSLOT)]
        slot_d = [area(SLOT0 + s * SLOT, QB, D) for s in range(NSLOT)]
        UT = SLOT0 + NSLOT * SLOT
        uT = area(UT, KC, T + 1)
        A0 = UT + KC * (T + 1)
        qT = area(A0, KC, T)
        kz = area(A0 + 2176, KVH, 2, T)
        vdup = area(A0 + 4352, 3, KVH, P)
        oT = area(A0 + 5888, KC, T)
        scores = area(A0 + 8064, 2, 2, NSC)
        PTW = 512 + 256 + 512 + 32
        pT = area(A0 + 9792, 2, PTW)
        raw = area(A0 + 12416, 2, T)
        rsq = area(A0 + 12960, 2, T)
        rstd2 = area(A0 + 13504, 2, T)
        sq = area(A0 + 14048, KC, T)
        std = area(A0 + 16224, T)
        rstd = area(A0 + 16496, T)
        wkdup = area(A0 + 16768, KC, KVH, 2, HD)
        xtok = area(A0, 2, D)
        mtok = area(A0 + 2048, D)
        prow = area(A0 + 3072, D)
        hid = area(A0, FF // P, T)
        sgate = area(A0 + 7616, QB, T)
        ARR = ARENA - (6 * PAIRS * TP + 2 * PAIRS * SEQ)
        r_a, kk_a, k_a, b_a, v_a, w_a = [area(ARR + n * PAIRS * TP, PAIRS, TP) for n in range(6)]
        g_a = area(ARR + 6 * PAIRS * TP, PAIRS, SEQ)
        bonus = area(ARR + 6 * PAIRS * TP + PAIRS * SEQ, PAIRS, SEQ)
        X4 = SLOT0 + 4 * SLOT
        xx = area(X4, KC, T)
        xm = [area(X4 + 2176 * (1 + n), KC, T) for n in range(2)]
        th_w, th_a, sg_a, sg_b = [area(X4 + 6528 + n * T, T) for n in range(4)]
        assert X4 + 6528 + 4 * T <= UT
        cum = area(A0, 2, TP)
        expo = area(A0 + 2 * TP, 3, TP)
        assert A0 + 5 * TP <= ARR
        wk = SLOT0 + 2 * SLOT
        ARt = area(X4 + 2176, PAIRS, 2, P)
        Bt = area(UT - 1024, PAIRS, P)
        Kt, Vt = area(UT, PAIRS, P), area(UT + 1024, PAIRS, P)
        S = area(A0, PAIRS, P)
        Bs, Ks, Vs, X, XT, Y = [area(wk + n * 1024, PAIRS, P) for n in range(6)]
        NA = area(wk + 6144, PAIRS, 2, P)
        KA = area(wk + 8192, PAIRS, 2, P)
        RHS, U = [area(X4 + 4224 + n * 1024, PAIRS, P) for n in range(2)]
        assert wk + 10240 <= X4 + 2176 and X4 + 4224 + 2048 <= UT - 1024 and X4 + 6528 <= UT - 1024
        gn_std = area(UT, PAIRS, SEQ)
        gn_sq = area(ARR + 4096, PAIRS, SEQ)
        gainrow = area(ARR + 6144, D)
        assert UT + 2048 <= ARR
        utok = area(0, 2, D)
        hbuf = area(SLOT0, 2, BLK)
        silu = area(SLOT0 + 1024, 2, BLK)
        ye = area(SLOT0 + 2048, D)
        sel = area(SLOT0 + 3072, 2, 2, P)
        selg = area(SLOT0 + 3584, 2, 2, P)
        selT = area(SLOT0 + 4096, 2, 2, P)
        utT = area(SLOT0 + 4608, KC, SEQ)
        acc = area(RAW + NRAW * HALF, 2, D)
        assert RAW + NRAW * HALF + 2 * D <= SPLIT and SPLIT + 2 * (NRING * HALF + KC * 2 * P + QB * 2 * P) <= ARENA

        ps = ctx.enter_context(nc.psum_tensor("ps", [P, 8, 512], F32))

        ld_x = [sem("ld_x0"), sem("ld_x1")]
        ld_meta, ld_par, ld_small, ld_gain, ld_router = [sem(n) for n in (
            "ld_meta", "ld_par", "ld_small", "ld_gain", "ld_router")]
        slot_in = [sem(f"slot_in{s}") for s in range(NSLOT)]
        pool_own, ident_ok, consts_ok, kw_ok, kz_zero, pads_zero, work_zero = [sem(n) for n in (
            "pool_own", "ident_ok", "consts_ok", "kw_ok", "kz_zero", "pads_zero", "work_zero")]
        act_own, dve_own = sem("act_own"), sem("dve_own")
        in_tr, in_x, in_rest = sem("in_tr"), sem("in_x"), sem("in_rest")
        norm_sq, norm_ss, norm_std, norm_u = [sem(n) for n in ("norm_sq", "norm_ss", "norm_std", "norm_u")]
        qk_mm, qk_sq, qk_ss, qk_std, qk_n, v_mm, v_cp = [sem(n) for n in (
            "qk_mm", "qk_sq", "qk_ss", "qk_std", "qk_n", "v_mm", "v_cp")]
        sc_mm, sc_rd, sc_max, sc_exp, p_ok, pt_mm, pt_a, pt_d, pv_mm, o_cp = [sem(n) for n in (
            "sc_mm", "sc_rd", "sc_max", "sc_exp", "p_ok", "pt_mm", "pt_a", "pt_d", "pv_mm", "o_cp")]
        wo_mm, wo_add = sem("wo_mm"), sem("wo_add")
        gate_mm, up_mm, ffn_silu, ffn_mul, down_mm, down_q, down_add = [sem(n) for n in (
            "gate_mm", "up_mm", "ffn_silu", "ffn_mul", "down_mm", "down_q", "down_add")]
        xx_ok, mixk_ok = sem("xx_ok"), sem("mixk_ok")
        mix_ok, mix_used, lora_h, l2_mm, l2_ev, pr_mm, pr_ev = [sem(n) for n in (
            "mix_ok", "mix_used", "lora_h", "l2_mm", "l2_ev", "pr_mm", "pr_ev")]
        kk_ok, kk_sq, kk_ss, kk_ev, kk_nrm, kk_done, rk_ok, rk_mm, rk_ev = [sem(n) for n in (
            "kk_ok", "kk_sq", "kk_ss", "kk_ev", "kk_nrm", "kk_done", "rk_ok", "rk_mm", "rk_ev")]
        cum_ok, dec_exp, dec_done = [sem(n) for n in ("cum_ok", "dec_exp", "dec_done")]
        bd_ar, bd_b, bd_kv, ap_mm, ap_ev, tr_mm, tr_ev = [sem(n) for n in (
            "bd_ar", "bd_b", "bd_kv", "ap_mm", "ap_ev", "tr_mm", "tr_ev")]
        y_mm, y_ev, x_mm, x_ok, rhs_mm, rhs_ev, u_mm, u_ev, ot_mm, ot_ev, s_mm, s_ok, rec_own = [sem(n) for n in (
            "y_mm", "y_ev", "x_mm", "x_ok", "rhs_mm", "rhs_ev", "u_mm", "u_ev", "ot_mm", "ot_ev", "s_mm", "s_ok", "rec_own")]
        ht_mm, ht_cp, gn_mm, gn_x, gn_sqd, gn_var, gn_sd, y_ok, wo2_mm, acc_ok = [sem(n) for n in (
            "ht_mm", "ht_cp", "gn_mm", "gn_x", "gn_sqd", "gn_var", "gn_sd", "y_ok", "wo2_mm", "acc_ok")]
        n4_ss, n4_std, utok_ok, utT_mm, utT_cp, lg_mm, lg_sub, lg_exp, mask_ok, rank_mm, npass_ok = [sem(n) for n in (
            "n4_ss", "n4_std", "utok_ok", "utT_mm", "utT_cp", "lg_mm", "lg_sub", "lg_exp", "mask_ok", "rank_mm", "npass_ok")]
        sel_ok, xg_mm, xg_hi, xg_ev, st_mm, st_ev = [sem(n) for n in ("sel_ok", "xg_mm", "xg_hi", "xg_ev", "st_mm", "st_ev")]
        raw_in = [sem(f"raw_in{n}") for n in range(NRAW)]
        w_hi, w_lo, w_used, et_hi = sem("w_hi"), sem("w_lo"), sem("w_used"), sem("et_hi")
        et_mm, e_silu, e_h, et_ev, ye_ev, es_mm, es_add = [sem(n) for n in (
            "et_mm", "e_silu", "e_h", "et_ev", "ye_ev", "es_mm", "es_add")]
        acc_done, out_sem = sem("acc_done"), sem("out_sem")

        block = ctx.enter_context(nc.Block())

        NB2 = 2 * FB
        TILES = [(0, 0), (1, 0)]
        for q in range(1, NB2):
            TILES += [(0, q), (1, q), (2, q - 1)]
        TILES.append((2, NB2 - 1))
        NHALF = 2 * len(TILES)
        TURNS = EXPERTS // 2
        LATE = {0: (1, 0, 0), 1: (1, 2, 2), FB + 1: (0, 0, 4), FB + 2: (0, 2, 6)}
        AHEAD = 2
        SPLITS = [(2 * n + NRING, 2 * n + 2 + NRING) for n in range(len(TILES) - 2)] + [(0, 0), (NHALF, NHALF + AHEAD)]
        XQ = 5
        assert NHALF % NRAW == 0 and NHALF % NRING == 0
        NLV = 5

        @block.sync
        def _(sp):
            def cols(w, n):
                return w.rearrange("(k p) n -> p k n", p=P)[:, :, n * BLK:(n + 1) * BLK]

            def load(s, dst, src):
                sp.dma_start(dst, src).then_inc(slot_in[s], 16)

            wqkv, wo = attn_w_qkv[0], attn_w_o[0]
            wg, wu, wd = ffn_w_gate[0], ffn_w_up[0], ffn_w_down[0]
            for t in range(2):
                sp.dma_start(xtok[:, t, :], x[0, t * P:(t + 1) * P, :]).then_inc(ld_x[t], 16)
            sp.wait_ge(ld_par, 160)
            load(0, slot_k[0], cols(wqkv, 0))
            load(1, slot_k[1], cols(wqkv, 1))
            load(2, slot_k[2], cols(wqkv, 2))
            load(3, slot_k[3], cols(wo, 0))
            load(4, slot_k[4], cols(wo, 1))
            load(5, slot_k[5], cols(wg, 0))
            sp.dma_start(router[:, :, :], moe_router[0].rearrange("(k p) e -> p k e", p=P)).then_inc(ld_router, 16)
            sp.wait_ge(qk_mm, 4)
            load(0, slot_k[0], cols(wu, 0))
            wd_v = wd.rearrange("(r k p) n -> r p k n", p=P, k=FB)
            dk = [slot_k[1 + r][:, 0:FB, :] for r in range(4)]
            for r, (s_, n) in enumerate(((qk_mm, 8), (v_mm, 3), (wo_mm, 4), (wo_mm, 8))):
                sp.wait_ge(s_, n)
                load(1 + r, dk[r], wd_v[r, :, :, 0:BLK])
            with sp.Fori(1, FB) as f:
                sp.wait_ge(gate_mm, f * QB)
                load(5, slot_k[5], wg.rearrange("(k p) n -> p k n", p=P)[:, :, bass.ds(f * BLK, BLK)])
                sp.wait_ge(up_mm, f * QB)
                load(0, slot_k[0], wu.rearrange("(k p) n -> p k n", p=P)[:, :, bass.ds(f * BLK, BLK)])
            sp.wait_ge(up_mm, FB * QB)
            load(0, slot_k[0], cols(rwkv_w_k[0], 0))
            for r in range(4):
                sp.wait_ge(down_mm, r + 1)
                load(1 + r, dk[r], wd_v[r, :, :, BLK:D])
            sp.wait_ge(down_mm, 5)
            load(1, slot_k[1], cols(rwkv_w_k[0], 1))
            sp.wait_ge(down_mm, 6)
            for off, w in ((0, rwkv_w1), (KC * LORA, rwkv_a1), (2 * KC * LORA, rwkv_g1)):
                n = w.shape[2]
                sp.dma_start(slot[2][:, off:off + KC * n].rearrange("p (k n) -> p k n", k=KC),
                             w[0].rearrange("(k p) n -> p k n", p=P)).then_inc(slot_in[2], 16)
            sp.wait_ge(down_mm, 7)
            for rows, off, src in ((slice(0, 64), 0, rwkv_w2[0]), (slice(64, 128), 0, rwkv_a2[0]),
                                   (slice(0, 128), D, rwkv_g2[0, 0:P]), (slice(0, GLORA - P), 2 * D, rwkv_g2[0, P:GLORA])):
                sp.dma_start(slot[3][rows, off:off + D], src).then_inc(slot_in[3], 16)
            for s, w, n, s_, used in ((0, rwkv_w_r, 0, pr_mm, 4), (1, rwkv_w_r, 1, pr_mm, 8), (2, rwkv_w_v, 0, mix_used, 3),
                                      (3, rwkv_w_v, 1, l2_mm, 24), (0, rwkv_w_o, 0, pr_mm, 12), (1, rwkv_w_o, 1, pr_mm, 16)):
                sp.wait_ge(s_, used)
                load(s, slot_k[s], cols(w[0], n))
            we_g = moe_w_gate[0].rearrange("e (k p) n -> e p k n", p=P)
            we_u = moe_w_up[0].rearrange("e (k p) n -> e p k n", p=P)
            we_d = moe_w_down[0].rearrange("e (f k p) n -> e f p k n", p=P, k=QB)

            def expert_tiles(i, it, a, b):
                for m in range(a, b):
                    (kind, q), h = TILES[m // 2], m % 2
                    e, f = 2 * i + q // FB, q % FB
                    sp.wait_ge(w_lo, it * NHALF + (m + 1))
                    if kind < 2:
                        dst = raw_w[:, m % NRAW, :].rearrange("p (k n) -> p k n", k=KC // 2)
                        src = (we_g, we_u)[kind][e, :, h * (KC // 2):(h + 1) * (KC // 2), f * BLK:(f + 1) * BLK]
                    else:
                        dst = raw_w[:, m % NRAW, :].rearrange("p (k n) -> p k n", k=QB // 2)
                        src = we_d[e, f, :, h * (QB // 2):(h + 1) * (QB // 2), :]
                    sp.dma_start(dst, src).then_inc(raw_in[m % NRAW], 16)

            sp.wait_ge(ot_ev, 4 * NCH)
            sp.wait_ge(s_ok, 2 * NCH + 2)
            sp.dma_start(gainrow, ffn_norm[1:2, :].to_broadcast([P, D])).then_inc(ld_gain, 16)
            with sp.Fori(0, TURNS) as i:
                expert_tiles(i, i, 0, NHALF)
            expert_tiles(0, TURNS, 0, AHEAD)
            sp.wait_ge(npass_ok, 1)
            n = sp.value_load(npass_i[0:1, 0:1], min_val=1, max_val=2)
            with sp.If(n > 1):
                expert_tiles(0, TURNS, AHEAD, NHALF)
                with sp.Fori(1, TURNS) as i:
                    expert_tiles(i, i + TURNS, 0, NHALF)
                expert_tiles(0, 2 * TURNS, 0, AHEAD)
            sp.wait_ge(acc_done, 1)
            sp.dma_start(out[0].rearrange("(t p) d -> p t d", p=P), acc).then_inc(out_sem, 16)
            sp.wait_ge(out_sem, 16)

        @block.gpsimd
        def _(pool):
            g = nc.gpsimd
            own = Own(pool)

            def one(ins, s_=pool_own):
                own.done(ins, s_)
                own.settle()

            def keep(v, pattern, base, mult, op=ALU.is_ge, fill=0.0):
                one(g.affine_select(out=v, in_=v, pattern=pattern, compare_op=op, fill=fill, base=base,
                                    channel_multiplier=mult))

            def fill(v, value):
                one(g.memset(v, value))

            fill(ident[:, :], 0.0)
            one(g.affine_select(out=ident[:, :], in_=ident[:, :], pattern=[[-1, P]], compare_op=ALU.not_equal, fill=1.0,
                                base=0, channel_multiplier=1), ident_ok)
            fill(ones[:, :], 1.0)
            fill(uT[:, :, 0:1], 0.0)
            fill(attmask[:, :], 0.0)
            keep(attmask[:, META:META + P], [[-1, P]], 0, 1, fill=NEG)
            a = SEG[1][0] + META
            keep(attmask[:, a:a + P], [[1, P]], -1, -1, fill=NEG)
            keep(attmask[:, a + P:a + 2 * P], [[-1, P]], 0, 1, fill=NEG)
            keep(attmask[:, SEG[2][0]:NSC], [[-1, META]], 0, 1, fill=NEG)
            fill(headones[:, :], 1.0)
            hv = headones[:, :].rearrange("p (h i) -> p h i", h=2)
            keep(hv, [[-CH, 2], [0, CH]], 0, 1)
            keep(hv, [[CH, 2], [0, CH]], CH - 1, -1)
            for j in range(2):
                v = causal[:, j, :].rearrange("p (h i) -> p h i", h=2)
                fill(v, 1.0)
                keep(v, [[-CH, 2], [0, CH]], 0, 1)
                keep(v, [[CH, 2], [1, CH]], j - 1, -1)
            fill(levelmask[:, :, :], 0.0)
            for l in range(2, 7):
                b = 1 << (l - 1)
                v = levelmask[:, l - 2, :].rearrange("p (j x i) -> p j x i", x=2, i=b)[:, :, 0, :]
                fill(v, 1.0)
                keep(v, [[-2 * b, P // (2 * b)], [0, b]], -b, 1)
                keep(v, [[2 * b, P // (2 * b)], [0, b]], 2 * b - 1, -1)
            fill(level1T[:, :], 0.0)
            v = level1T[:, :].rearrange("p (j x) -> p j x", x=2)[:, :, 1]
            fill(v, 1.0)
            keep(v, [[-2, P // 2]], 0, 1, op=ALU.is_equal)
            fill(reset[:, :], 1.0)
            fill(reset[:, :].rearrange("p (c i) -> p c i", c=NCH)[:, :, 0], 0.0)
            fill(before[:, :], 1.0)
            keep(before[:, :], [[1, P]], -1, -1)
            for v, pattern, base in ((slotno[:, :], [[1, P]], 0), (expno[:, :, :], [[0, 2], [1, EXPERTS]], 0)):
                one(g.iota(v, pattern=pattern, base=base, channel_multiplier=0, allow_small_or_imprecise_dtypes=True))
            one(g.iota(expno8[:, :, :], pattern=[[0, 2], [1, EXPERTS]], base=EXPERTS, channel_multiplier=0,
                       allow_small_or_imprecise_dtypes=True), consts_ok)
            pool.wait_ge(in_x, 4)
            pool.wait_ge(in_rest, 2)
            one(g.memset(kz[:, :, :, :], 0.0), kz_zero)
            pool.wait_ge(slot_in[2], 16)
            for h in range(2):
                one(g.tensor_copy(wkdup[:, :, :, h, :], slot_k[2][:, :, 0:256].rearrange("p k (g d) -> p k g d", g=KVH)), kw_ok)
            pool.wait_ge(norm_u, 3 * KC)
            for arr in (r_a, kk_a, k_a, b_a, v_a, w_a):
                fill(arr[:, :, 0:PAD], 0.0)
            fill(th_w[HD:P, :], 0.0)
            fill(th_a[0:HD, :], 0.0)
            for lo in (32, 64, 96):
                fill(sg_b[lo:lo + 32, :], 0.0)
            pool.wait_ge(down_mm, 7)
            for lo in (32, 64, 96):
                one(g.memset(slot[3][lo:lo + 32, 2 * D:3 * D], 0.0), pads_zero)
            pool.wait_ge(l2_mm, 24)
            one(g.memset(Bt[:, :, :], 0.0), work_zero)
            pool.wait_ge(mix_ok, 5)
            for v in (Kt[:, :, :], Vt[:, :, :]):
                one(g.memset(v, 0.0), work_zero)
            pool.wait_ge(pr_mm, 16)
            one(g.memset(ARt[:, :, :, :], 0.0), work_zero)
            pool.wait_ge(dec_done, PAIRS)
            pool.wait_ge(pr_ev, 24)
            with pool.Fori(0, NCH) as c:
                for n, (dst, src) in enumerate(((Kt, k_a), (Vt, v_a))):
                    for h in range(2):
                        rows = slice(h * CH, (h + 1) * CH)
                        g.tensor_copy(dst[rows, :, rows], src[rows, :, bass.ds(c * CH, CH)]).then_inc(bd_kv, 1)
                        pool.wait_ge(bd_kv, c * 4 + (2 * n + h + 1))
                pool.wait_ge(tr_mm, 6 * (c + 1))

        @block.tensor
        def _(pe):
            mm, tr = nc.tensor.matmul, nc.tensor.transpose

            pe.wait_ge(ident_ok, 1)
            for t in range(2):
                pe.wait_ge(ld_x[t], 16)
                for half in range(2):
                    for c in range(4):
                        k = half * 4 + c
                        last = tr(ps[:, 2 * t + half, c * P:(c + 1) * P], xtok[:, t, k * P:(k + 1) * P], ident[:, :])
                    last.then_inc(in_tr, 1)
            pe.wait_ge(ld_meta, 16)
            for k in range(KC):
                last = tr(ps[:, 4, k * META:(k + 1) * META], mtok[0:META, k * P:(k + 1) * P], ident[0:META, 0:META])
            last.then_inc(in_tr, 1)
            pe.wait_ge(ld_par, 160)
            for k in range(KC):
                last = tr(ps[:, 5, k * NROW:(k + 1) * NROW], prow[0:NROW, k * P:(k + 1) * P], ident[0:NROW, 0:NROW])
            last.then_inc(in_tr, 1)
            def sum_sq(n, k):
                pe.wait_ge(norm_sq, (n - 1) * KC + k + 1)
                last = mm(ps[:, 7 if n < 3 else 0, 0:T], ones[:, :], sq[:, k, :], start=(k == 0), stop=(k == KC - 1))
                if k == KC - 1:
                    last.then_inc(norm_ss, 1)

            pe.wait_ge(pool_own, 2)
            for k in range(KC):
                sum_sq(1, k)
            pe.wait_ge(ld_small, 16 * 5)
            mm(ps[:, 6, 0:HEADS], ones[0:1, :], sinkrow[:, :], start=True, stop=True).then_inc(in_tr, 1)

            pe.wait_ge(consts_ok, 1)

            def head_ss(m):
                pe.wait_ge(qk_sq, m + 1)
                if m >= 2:
                    pe.wait_ge(qk_std, m - 1)
                mm(ps[:, 3 + m % 2, 0:T], headones[:, :], rsq[:, m % 2, :], start=True, stop=True).then_inc(qk_ss, 1)

            for m in range(KC + KVH):
                if m in (0, 4, 8):
                    pe.wait_ge(slot_in[m // 4], 16)
                if m == KC:
                    pe.wait_ge(kw_ok, 2)
                if m >= 3:
                    pe.wait_ge(qk_sq, m - 2)
                for k in range(KC):
                    if m == 0:
                        pe.wait_ge(norm_u, k + 1)
                    if m < KC:
                        w = slot_k[m // 4][:, k, (m % 4) * P:(m % 4 + 1) * P]
                    else:
                        w = wkdup[:, k, m - KC, :, :].rearrange("p a b -> p (a b)")
                    last = mm(ps[:, m % 3, 0:T], w, uT[:, k, 1:T + 1], start=(k == 0), stop=(k == KC - 1))
                last.then_inc(qk_mm, 1)
                if m >= 1:
                    head_ss(m - 1)
            for t in range(3):
                n = P if t < 2 else META
                for k in range(KC):
                    last = mm(ps[0:n, 5 + t, 0:256], uT[:, k, 1 + t * P:1 + t * P + n], slot_k[2][:, k, 256:512],
                              start=(k == 0), stop=(k == KC - 1))
                last.then_inc(v_mm, 1)
            head_ss(KC + KVH - 1)

            def score(c):
                g = c // 2
                if c >= 1:
                    pe.wait_ge(sc_rd, c)
                mm(ps[:, 0, 0:2 * (META + P)], qT[:, c, META:META + P], kz[:, g, :, 0:META + P], start=True, stop=True)
                mm(ps[0:META, 0, 288:288 + 2 * META], qT[:, c, 0:META], kz[:, g, :, 0:META], start=True, stop=True)
                for h in range(2):
                    last = mm(ps[:, 1 + h, 0:T], qT[:, c, META + P:T], kz[:, g, h, :], start=True, stop=True)
                last.then_inc(sc_mm, 1)

            pe.wait_ge(qk_n, KC + KVH)
            pe.wait_ge(v_cp, 3)
            score(0)
            score(1)
            for c in range(PAIRS):
                g, b = c // 2, c % 2
                pe.wait_ge(p_ok, c + 1)
                if c >= 1:
                    pe.wait_ge(pt_a, c)
                    pe.wait_ge(pt_d, c)
                for h in range(2):
                    p1, p2, p0 = [scores[:, b, h, o:o + n] for o, n in SEG]
                    hs = slice(h * P, (h + 1) * P)
                    tr(ps[:, 3, h * P:h * P + P], p1[:, 0:P], ident[:, :])
                    tr(ps[:, 3, 256 + h * P:256 + h * P + P], p2[:, 0:P], ident[:, :])
                    tr(ps[:, 4, h * P:h * P + P], p2[:, P:2 * P], ident[:, :])
                    tr(ps[0:META, 5, h * P:h * P + P], p1[:, P:P + META], ident[:, :])
                    tr(ps[0:META, 5, 256 + h * P:256 + h * P + P], p2[:, 2 * P:T], ident[:, :])
                    last = tr(ps[0:META, 4, 256 + h * META:256 + (h + 1) * META], p0[0:META, :], ident[0:META, 0:META])
                last.then_inc(pt_mm, 1)
                if c + 2 < PAIRS:
                    score(c + 2)
                pe.wait_ge(pt_a, c + 1)
                pe.wait_ge(pt_d, c + 1)
                if c >= 1:
                    pe.wait_ge(o_cp, c)
                pt = pT[:, b, :]
                mm(ps[:, 6, 0:256], vdup[:, 0, g, :], pt[:, 0:256], start=True, stop=False)
                mm(ps[:, 6, 0:256], vdup[0:META, 1, g, :], pt[0:META, 768:1024], start=False, stop=True)
                mm(ps[:, 6, 256:512], vdup[:, 0, g, :], pt[:, 256:512], start=True, stop=False)
                mm(ps[:, 6, 256:512], vdup[:, 1, g, :], pt[:, 512:768], start=False, stop=False)
                mm(ps[:, 6, 256:512], vdup[0:META, 2, g, :], pt[0:META, 1024:1280], start=False, stop=True)
                mm(ps[:, 7, 0:2 * META], vdup[0:META, 0, g, :], pt[0:META, 1280:1312], start=True, stop=True)\
                    .then_inc(pv_mm, 1)

            pe.wait_ge(o_cp, PAIRS)
            for m in range(KC):
                if m in (0, 4):
                    pe.wait_ge(slot_in[3 + m // 4], 16)
                if m >= 4:
                    pe.wait_ge(wo_add, m - 3)
                for k in range(KC):
                    last = mm(ps[:, m % 4, 0:T], slot_k[3 + m // 4][:, k, (m % 4) * P:(m % 4 + 1) * P], oT[:, k, :],
                              start=(k == 0), stop=(k == KC - 1))
                last.then_inc(wo_mm, 1)
                if m >= 1:
                    sum_sq(2, m - 1)
            sum_sq(2, KC - 1)

            with pe.Fori(0, FB) as f:
                for s, b0, made, free, loads in ((5, 0, gate_mm, ffn_silu, 1), (0, 4, up_mm, ffn_mul, 2)):
                    pe.wait_ge(slot_in[s], f * 16 + 16 * loads)
                    for q in range(QB):
                        pe.wait_ge(free, f * QB + (q + 1))
                        for k in range(KC):
                            if s == 5 and q == 0:
                                pe.wait_ge(norm_u, KC + k + 1)
                            last = mm(ps[:, b0 + q, 0:T], slot_k[s][:, k, q * P:(q + 1) * P], uT[:, k, 1:T + 1],
                                      start=(k == 0), stop=(k == KC - 1))
                        last.then_inc(made, 1)
            pe.wait_ge(ffn_mul, QB + FB * QB)
            for hf in range(2):
                for r in range(4):
                    pe.wait_ge(slot_in[1 + r], hf * 16 + 32)
                    kq = [(k, q) for k in range(FB) for q in range(QB)]
                    if r == 3:
                        kq = [(k, q) for q in range(QB) for k in range(FB)]
                    for k, q in kq:
                        last = mm(ps[:, 4 * hf + q, 0:T], slot_k[1 + r][:, k, q * P:(q + 1) * P], hid[:, r * FB + k, :],
                                  start=(r + k == 0), stop=(r == 3 and k == FB - 1))
                        if r == 3 and k == FB - 1:
                            last.then_inc(down_q, 1)
                            if q == QB - 1:
                                pe.wait_ge(down_q, hf * QB + QB)
                                pe.sem_inc(down_mm, 1)
                    if r < 3:
                        last.then_inc(down_mm, 1)
            for k in range(KC):
                sum_sq(3, k)

            def project(j):
                which, m = j // KC, j % KC
                s = (0, 0, 2)[which] + m // 4
                if m == 0 and which:
                    pe.wait_ge(mix_ok, 3 + which)
                if m % 4 == 0:
                    pe.wait_ge(slot_in[s], 16 * {0: 9, 1: 4, 2: 7, 3: 8}[s] + (16 if which == 1 else 0))
                if j >= 4:
                    pe.wait_ge(pr_ev, j - 3)
                for k in range(KC):
                    if j == 0:
                        pe.wait_ge(mixk_ok, k + 1)
                    last = mm(ps[:, j % 4, 0:T], slot_k[s][:, k, (m % 4) * P:(m % 4 + 1) * P], xm[which // 2][:, k, :],
                              start=(k == 0), stop=(k == KC - 1))
                last.then_inc(pr_mm, 1)

            def per_head(m, src, ready, made, read):
                pe.wait_ge(ready, m + 1)
                if m >= 4:
                    pe.wait_ge(read, m - 3)
                mm(ps[:, 4 + m % 4, 0:T], headones[:, :], src[:, m, PAD:TP], start=True, stop=True).then_inc(made, 1)

            for j in range(KC):
                project(j)
            l1 = [slot[2][:, o:o + KC * n].rearrange("p (k n) -> p k n", k=KC)
                  for o, n in ((0, LORA), (KC * LORA, LORA), (2 * KC * LORA, GLORA))]
            pe.wait_ge(slot_in[2], 16 * 6)
            pe.wait_ge(mix_ok, 1)
            pe.wait_ge(pr_ev, 5)
            for k in range(KC):
                last = mm(ps[0:LORA, 0, 0:T], l1[0][:, k, :], xm[1][:, k, :], start=(k == 0), stop=(k == KC - 1))
            last.then_inc(mix_used, 1)
            for m in range(4):
                per_head(m, v_a, kk_sq, kk_ss, kk_ev)
            pe.wait_ge(mix_ok, 2)
            pe.wait_ge(pr_ev, 8)
            for k in range(KC):
                last = mm(ps[HD:P, 1, 0:T], l1[1][:, k, :], xm[0][:, k, :], start=(k == 0), stop=(k == KC - 1))
            last.then_inc(mix_used, 1)
            for m in range(4, PAIRS):
                per_head(m, v_a, kk_sq, kk_ss, kk_ev)
            pe.wait_ge(mix_ok, 3)
            for k in range(KC):
                mm(ps[:, 2, 0:T], l1[2][:, k, 0:P], xm[1][:, k, :], start=(k == 0), stop=(k == KC - 1))
            for k in range(KC):
                last = mm(ps[0:GLORA - P, 3, 0:T], l1[2][:, k, P:GLORA], xm[1][:, k, :], start=(k == 0), stop=(k == KC - 1))
            last.then_inc(mix_used, 1)
            pe.wait_ge(slot_in[3], 16 * 7)
            pe.wait_ge(pads_zero, 3)
            pe.wait_ge(kk_ev, KC)
            for j in range(3 * KC):
                which, m = j // KC, j % KC
                if m == 0:
                    pe.wait_ge(lora_h, (1, 2, 4)[which])
                if j >= 4:
                    pe.wait_ge(l2_ev, j - 3)
                bank = ps[:, 4 + j % 4, 0:T]
                cs = slice(m * P, (m + 1) * P)
                if which < 2:
                    last = mm(bank, slot[3][:, cs], (th_w, th_a)[which], start=True, stop=True)
                else:
                    mm(bank, slot[3][:, D + m * P:D + (m + 1) * P], sg_a, start=True, stop=False)
                    last = mm(bank, slot[3][:, 2 * D + m * P:2 * D + (m + 1) * P], sg_b, start=False, stop=True)
                last.then_inc(l2_mm, 1)
            pe.wait_ge(lora_h, 4)
            for j in range(KC, 3 * KC):
                project(j)
                if 12 <= j < 20:
                    if j == 12:
                        pe.wait_ge(l2_ev, 24)
                    per_head(j - 12, v_a, rk_ok, rk_mm, rk_ev)

            pe.wait_ge(work_zero, 4)
            pe.wait_ge(pr_ev, 24)
            pe.wait_ge(rk_ev, PAIRS)
            with pe.Fori(0, NCH) as c:
                pe.wait_ge(bd_ar, c + 1)
                pe.wait_ge(bd_b, c + 1)
                for h in range(2):
                    for p in range(4):
                        last = mm(ps[:, 4 * h + p // 2, (p % 2) * 256:(p % 2 + 1) * 256], Bt[:, 4 * h + p, :],
                                  ARt[:, 4 * h + p, :, :], start=True, stop=True)
                    last.then_inc(ap_mm, 1)
                pe.wait_ge(bd_kv, c * 4 + 4)
                for h in range(2):
                    for p in range(4):
                        last = mm(ps[:, 4 * h + 2 + p // 2, (p % 2) * 256:(p % 2 + 1) * 256], Kt[:, 4 * h + p, :],
                                  ARt[:, 4 * h + p, :, :], start=True, stop=True)
                    last.then_inc(ap_mm, 1)
                for n, src in enumerate((Bt, Kt, Vt)):
                    for h in range(2):
                        pe.wait_ge(ap_ev, c * 4 + (1 + h if n < 2 else 3 + h))
                        for p in range(4):
                            last = tr(ps[:, 4 * h + n, p * P:(p + 1) * P], src[:, 4 * h + p, :], ident[:, :])
                        last.then_inc(tr_mm, 1)
                for h in range(2):
                    pe.wait_ge(tr_ev, c * 6 + 5 + h)
                    pe.wait_ge(s_ok, c * 2 + h + 1)
                    for p in range(4 * h, 4 * h + 4):
                        o = ps[:, 4 * h + 1, (p % 4) * P:(p % 4 + 1) * P]
                        mm(o, ARt[:, p, 0, :], S[:, p, :], start=True, stop=False)
                        last = mm(o, KA[:, p, 0, :], Vs[:, p, :], start=False, stop=True)
                    last.then_inc(rhs_mm, 1)
                for l in range(NLV):
                    for h in range(2):
                        pe.wait_ge(x_ok, c * 12 + 2 * l + h + 1)
                        for p in range(4 * h, 4 * h + 4):
                            last = mm(ps[:, 4 * h + 3, (p % 4) * P:(p % 4 + 1) * P], NA[:, p, 0, :], X[:, p, :],
                                      start=True, stop=True)
                        last.then_inc(y_mm, 1)
                    for h in range(2):
                        pe.wait_ge(y_ev, c * 10 + 2 * l + h + 1)
                        for p in range(4 * h, 4 * h + 4):
                            o = ps[:, 4 * h, (p % 4) * P:(p % 4 + 1) * P]
                            if l < NLV - 1:
                                last = mm(o, XT[:, p, :], Y[:, p, :], start=True, stop=True)
                            else:
                                last = mm(o, Y[:, p, :], XT[:, p, :], start=True, stop=True)
                        last.then_inc(x_mm, 1)
                for h in range(2):
                    pe.wait_ge(x_ok, c * 12 + 11 + h)
                    pe.wait_ge(rhs_ev, c * 2 + h + 1)
                    for p in range(4 * h, 4 * h + 4):
                        last = mm(ps[:, 4 * h + 2, (p % 4) * P:(p % 4 + 1) * P], XT[:, p, :], RHS[:, p, :], start=True, stop=True)
                    last.then_inc(u_mm, 1)
                for h in range(2):
                    pe.wait_ge(u_ev, c * 2 + h + 1)
                    for p in range(4 * h, 4 * h + 4):
                        o = ps[:, 4 * h + 1, (p % 4) * P:(p % 4 + 1) * P]
                        mm(o, S[:, p, :], ARt[:, p, 1, :], start=True, stop=False)
                        mm(o, U[:, p, :], NA[:, p, 1, :], start=False, stop=False)
                        last = mm(o, Vs[:, p, :], KA[:, p, 1, :], start=False, stop=True)
                    last.then_inc(ot_mm, 1)
                for h in range(2):
                    for p in range(4 * h, 4 * h + 4):
                        o = ps[:, 4 * h + 3, (p % 4) * P:(p % 4 + 1) * P]
                        mm(o, Bs[:, p, :], U[:, p, :], start=True, stop=False)
                        last = mm(o, Ks[:, p, :], Vs[:, p, :], start=False, stop=True)
                    last.then_inc(s_mm, 1)

            pe.wait_ge(s_ok, 2 * NCH + 2)
            pe.wait_ge(ot_ev, 4 * NCH)
            for t in range(2):
                for half in range(2):
                    for q in range(4):
                        k = 4 * half + q
                        last = tr(ps[:, 2 * t + half, q * P:(q + 1) * P], hT[:, k, META + t * P:META + (t + 1) * P], ident[:, :])
                    last.then_inc(ht_mm, 1)
            for m in range(PAIRS):
                if m >= 4:
                    pe.wait_ge(gn_x, m - 3)
                mm(ps[:, 4 + m % 4, 0:SEQ], headones[:, :], w_a[:, m, CH:TP], start=True, stop=True).then_inc(gn_mm, 1)
            pe.wait_ge(ht_cp, 4)
            for m in range(PAIRS):
                pe.wait_ge(gn_sqd, m + 1)
                if m >= 4:
                    pe.wait_ge(gn_sd, m - 3)
                mm(ps[:, m % 4, 0:SEQ], headones[:, :], gn_sq[:, m, :], start=True, stop=True).then_inc(gn_var, 1)

            pe.wait_ge(y_ok, PAIRS)
            pe.wait_ge(gn_sd, PAIRS)
            pe.wait_ge(slot_in[0], 16 * 11)
            pe.wait_ge(slot_in[1], 16 * 6)
            for t in range(2):
                for n in range(2):
                    for k in range(KC):
                        last = mm(ps[:, 2 * t + n, :], w_a[:, k, CH + t * P:CH + (t + 1) * P], slot_k[n][:, k, :],
                                  start=(k == 0), stop=(k == KC - 1))
                    last.then_inc(wo2_mm, 1)

            for m in range(KC):
                if m == 0:
                    pe.wait_ge(utok_ok, 2)
                    pe.wait_ge(gn_x, PAIRS)
                for t in range(2):
                    last = tr(ps[:, 4 + m // 2, (m % 2) * SEQ + t * P:(m % 2) * SEQ + (t + 1) * P],
                              utok[:, t, m * P:(m + 1) * P], ident[:, :])
                if m % 2:
                    last.then_inc(utT_mm, 1)
            pe.wait_ge(acc_ok, 4)
            pe.wait_ge(utT_cp, 4)
            pe.wait_ge(ld_router, 16)
            for t in range(2):
                for k in range(KC):
                    last = mm(ps[:, 0, t * EXPERTS:(t + 1) * EXPERTS], utT[:, k, t * P:(t + 1) * P], router[:, k, :],
                              start=(k == 0), stop=(k == KC - 1))
            last.then_inc(lg_mm, 1)
            chosen = route[:, 0, :, 0:EXPERTS]
            pe.wait_ge(mask_ok, 1)
            mm(ps[:, 1, 0:8], before[:, :], chosen[:, 0, :], start=True, stop=True)
            mm(ps[:, 1, 8:16], ones[:, :], chosen[:, 0, :], start=True, stop=False)
            mm(ps[:, 1, 8:16], before[:, :], chosen[:, 1, :], start=False, stop=True)
            mm(ps[:, 1, 16:24], ones[:, :], chosen[:, 0, :], start=True, stop=False)
            mm(ps[:, 1, 16:24], ones[:, :], chosen[:, 1, :], start=False, stop=True).then_inc(rank_mm, 1)

            pe.sem_inc(w_used, NRING)
            pe.wait_ge(npass_ok, 1)
            n = pe.value_load(npass_i[0:1, 0:1], min_val=1, max_val=2)

            def gather(j, sels, b5, b4):
                pe.wait_ge(sel_ok, sels)
                for half in range(2):
                    pe.wait_ge((es_add, et_ev)[half], (b5, b4)[half])
                    for q in range(4):
                        k = 4 * half + q
                        for t in range(2):
                            last = mm(ps[:, 5 - half, q * P:(q + 1) * P], utok[:, t, k * P:(k + 1) * P],
                                      sel[:, j, t, :], start=(t == 0), stop=(t == 1))
                    last.then_inc(xg_mm, 1)

            def sel_tr(j, read):
                pe.wait_ge(xg_ev, read)
                for t in range(2):
                    last = tr(ps[:, 5, t * P:(t + 1) * P], selg[:, j, t, :], ident[:, :])
                last.then_inc(st_mm, 1)

            def scatter(j, o, added):
                pe.wait_ge(es_add, added)
                t, n_ = o // 2, o % 2
                mm(ps[:, 5, :], selT[:, j, t, :], ye[:, n_ * BLK:(n_ + 1) * BLK], start=True, stop=True).then_inc(es_mm, 1)

            with pe.Fori(0, n) as pas:
                first = pas * TURNS
                gather(0, first * 2 + pas + 1, pas * (8 * TURNS + 4) + 1, first * NB2 + 1)
                sel_tr(0, first * 4 + pas * 2 + 2)
                with pe.Fori(0, TURNS) as i:
                    it = pas * TURNS + i
                    tables = it * 2 + pas
                    adds = it * 8 + pas * 4

                    def half_tile(m, k):
                        pe.wait_ge(w_lo, it * NHALF + (m + NRAW + 1))
                        return [wsplit[:, m % NRING, part, :].rearrange("p (k n) -> p k n", k=k) for part in range(2)]

                    def split_mm(o, x_, w_, first_, last_):
                        mm(o, x_[0], w_[0], start=first_, stop=False)
                        mm(o, x_[0], w_[1], start=False, stop=False)
                        return mm(o, x_[1], w_[0], start=False, stop=last_)

                    def gate_up(q, kind):
                        j, m = q // FB, 2 * TILES.index((kind, q))
                        if q % FB == 0 and kind == 0:
                            pe.wait_ge(xg_ev, tables * 2 + (2 * j + 2))
                        pe.wait_ge((e_silu, e_h)[kind], it * NB2 + (q + 1))
                        for h in range(2):
                            whi, wlo = half_tile(m + h, KC // 2)
                            for kk in range(KC // 2):
                                k = h * (KC // 2) + kk
                                last = split_mm(ps[:, 2 * kind + q % 2, :], (xsplit[:, j, 0, k, :], xsplit[:, j, 1, k, :]),
                                                (whi[:, kk, :], wlo[:, kk, :]), k == 0, k == KC - 1)
                            last.then_inc(w_used, 1)

                    def hidden_tr(q):
                        pe.wait_ge(e_h, it * NB2 + (q + 3))
                        pe.wait_ge(et_ev, it * NB2 + (q + 1))
                        if q in (0, XQ):
                            pe.wait_ge(xg_ev, tables * 2 + (2 if q == 0 else 4))
                        for k in range(QB):
                            last = tr(ps[:, 4, k * P:(k + 1) * P], hbuf[:, q % 2, k * P:(k + 1) * P], ident[:, :])
                        last.then_inc(et_mm, 1)

                    def down(q):
                        f, m = q % FB, 2 * TILES.index((2, q))
                        pe.wait_ge(et_ev, it * NB2 + (q + 2))
                        if f == 0:
                            pe.wait_ge(ye_ev, it * 2 + (q // FB + 1))
                        for h in range(2):
                            whi, wlo = half_tile(m + h, QB // 2)
                            for kk in range(QB // 2):
                                k = h * (QB // 2) + kk
                                for n_ in range(2):
                                    cs = slice(n_ * BLK, (n_ + 1) * BLK)
                                    last = split_mm(ps[:, 6 + n_, :], (hsplit[:, q % 2, 0, k, :], hsplit[:, q % 2, 1, k, :]),
                                                    (whi[:, kk, cs], wlo[:, kk, cs]), f + k == 0, f == FB - 1 and k == QB - 1)
                            last.then_inc(w_used, 1)

                    for q in range(NB2):
                        gate_up(q, 0)
                        if q == XQ + 1:
                            sel_tr(1, tables * 2 + 3)
                        if q in LATE:
                            j, o, n_ = LATE[q]
                            if o == 0:
                                pe.wait_ge(ye_ev, it * 2 + (2 - j))
                                pe.wait_ge(st_ev, tables + (2 - j))
                            scatter(j, o, adds + (n_ + 1))
                        if q:
                            hidden_tr(q - 1)
                        gate_up(q, 1)
                        if q in LATE:
                            scatter(j, o + 1, adds + (n_ + 2))
                        if q:
                            down(q - 1)
                        if q == XQ:
                            gather(1, tables + 2, adds + 5, it * NB2 + (q + 1))
                    hidden_tr(NB2 - 1)
                    gather(0, tables + 3, adds + 9, it * NB2 + (NB2 + 1))
                    down(NB2 - 1)
                    sel_tr(0, tables * 2 + 5)
                turns = pas * TURNS + TURNS
                pe.wait_ge(ye_ev, turns * 2 + 1)
                pe.wait_ge(st_ev, turns * 2 + pas + 1)
                for o in range(4):
                    scatter(1, o, turns * 8 + pas * 4 + (o + 1))

        @block.scalar
        def _(act):
            A = nc.scalar.activation
            own = Own(act)
            act.dma_start(mtok[0:META, :], meta_tokens[:, :]).then_inc(ld_meta, 16)
            for row, src in ((R_MIXN, mixer_norm), (R_FFNN, ffn_norm), (R_MIX, rwkv_mix[0]), (R_W0, rwkv_w0),
                             (R_A0, rwkv_a0), (R_KK, rwkv_k_k), (R_KA, rwkv_k_a),
                             (R_RK, rwkv_r_k.rearrange("o h n -> o (h n)")), (R_GNW, rwkv_gn_w), (R_GNB, rwkv_gn_b)):
                act.dma_start(prow[row:row + src.shape[0], :], src).then_inc(ld_par, 16)
            for half in range(2):
                rows = slice(half * HD, (half + 1) * HD)
                act.dma_start(qgain[rows, :], attn_q_norm.rearrange("o (n u) -> (o n) u", u=1)).then_inc(ld_small, 16)
                act.dma_start(kgain[rows, :], attn_k_norm.rearrange("o (n u) -> (o n) u", u=1)).then_inc(ld_small, 16)
            act.dma_start(sinkrow[:, :], attn_sinks[:, :]).then_inc(ld_small, 16)
            for t in range(2):
                for half in range(2):
                    b = 2 * t + half
                    act.wait_ge(in_tr, b + 1)
                    own.done(A(hT[:, 4 * half:4 * half + 4, META + t * P:META + (t + 1) * P],
                               ps[:, b, :].rearrange("p (a b) -> p a b", a=4), ACT.Copy), in_x)

            def norm(n):
                if n == 1:
                    act.wait_ge(in_rest, 1)
                    own.settle()
                for k in range(KC):
                    if n > 1:
                        act.wait_ge((wo_add, down_add)[n - 2], k + 1)
                    own.done(A(sq[:, k, :], hT[:, k, :], ACT.Square), norm_sq)
                act.wait_ge(norm_ss, n)
                own.done(A(std, ps[:, 7 if n < 3 else 0, 0:T], ACT.Sqrt, bias=epsD, scale=1.0 / D), norm_std)

            epsD, eps_q, eps_k, eps_gn = [normcol[:, 0, 0:1], normcol[:, 0, 1:2], normcol[:, 0, 0:1], normcol[:, 1, 0:1]]
            act.wait_ge(dve_own, 5)
            norm(1)

            def head_std(m):
                act.wait_ge(qk_ss, m + 1)
                if m >= 2:
                    act.wait_ge(qk_n, m - 1)
                b = ps[:, 3 + m % 2, 0:T]
                if m < KC:
                    own.done(A(rstd2[:, m % 2, :], b, ACT.Sqrt, bias=eps_q), qk_std)
                else:
                    own.done(A(rstd2[:, m % 2, :], b, ACT.Sqrt, bias=eps_k, scale=1.0 / HD), qk_std)

            for m in range(KC + KVH):
                act.wait_ge(qk_mm, m + 1)
                if m >= 2:
                    act.wait_ge(qk_ss, m - 1)
                    act.wait_ge(qk_n, m - 1)
                A(raw[:, m % 2, :], ps[:, m % 3, 0:T], ACT.Copy)
                own.done(A(rsq[:, m % 2, :], ps[:, m % 3, 0:T], ACT.Square), qk_sq)
                if m >= 1:
                    head_std(m - 1)
            for t in range(3):
                n = P if t < 2 else META
                act.wait_ge(v_mm, t + 1)
                for half in range(2):
                    last = A(vdup[0:n, t, :, half * HD:(half + 1) * HD],
                             ps[0:n, 5 + t, 0:256].rearrange("p (g d) -> p g d", g=KVH), ACT.Copy)
                own.done(last, v_cp)
            head_std(KC + KVH - 1)

            def exps(c):
                b = c % 2
                act.wait_ge(sc_max, c + 1)
                for h in range(2):
                    for s_, (o, n) in enumerate(SEG):
                        v = scores[:, b, h, o:o + n]
                        A(v, v, ACT.Exp, bias=stat[:, b, 1, 3 * h + s_:3 * h + s_ + 1],
                          accum_out=stat[:, b, 2, 3 * h + s_:3 * h + s_ + 1])
                own.done(A(stat[:, b, 4, :], stat[:, b, 3, :], ACT.Exp), sc_exp)

            def probs_copy(c):
                act.wait_ge(pt_mm, c + 1)
                if c >= 2:
                    act.wait_ge(pv_mm, c - 1)
                own.done(A(pT[:, c % 2, 0:512], ps[:, 3, :], ACT.Copy), pt_a)

            def out_copy(c):
                act.wait_ge(pv_mm, c + 1)
                for h in range(2):
                    rows = slice(h * HD, (h + 1) * HD)
                    A(oT[rows, c, 0:META], ps[rows, 7, h * META:(h + 1) * META], ACT.Copy)
                    last = A(oT[rows, c, META:T].rearrange("p (b q) -> p b q", b=2),
                             ps[rows, 6, :].rearrange("p (b h q) -> p b h q", b=2, h=2)[:, :, h, :], ACT.Copy)
                own.done(last, o_cp)

            exps(0)
            exps(1)
            for c in range(PAIRS):
                probs_copy(c)
                if c + 2 < PAIRS:
                    exps(c + 2)
                out_copy(c)
            norm(2)

            act.sem_inc(ffn_silu, QB)
            with act.Fori(0, FB) as f:
                for q in range(QB):
                    act.wait_ge(gate_mm, f * QB + (q + 1))
                    act.wait_ge(ffn_mul, f * QB + (q + 1))
                    A(sgate[:, q, :], ps[:, q, 0:T], ACT.Silu).then_inc(ffn_silu, 1)
            norm(3)

            def take(j):
                which, m = j // KC, j % KC
                act.wait_ge(pr_mm, j + 1)
                if which == 2:
                    act.wait_ge(rk_mm, m + 1)
                own.done(A((k_a, r_a, v_a)[which][:, m, PAD:TP], ps[:, j % 4, 0:T], ACT.Copy), pr_ev)

            def square(m):
                act.wait_ge(kk_ok, m + 1)
                own.done(A(v_a[:, m, PAD:TP], kk_a[:, m, PAD:TP], ACT.Square), kk_sq)

            for j in range(KC):
                take(j)
                if j >= 1:
                    square(j - 1)
            square(KC - 1)
            act.wait_ge(pads_zero, 3)
            act.wait_ge(mix_used, 1)
            own.done(A(th_w[0:HD, :], ps[0:HD, 0, 0:T], ACT.Tanh), lora_h)
            act.wait_ge(mix_used, 2)
            own.done(A(th_a[HD:P, :], ps[HD:P, 1, 0:T], ACT.Copy), lora_h)
            act.wait_ge(kk_ev, PAIRS)
            own.done(A(r_a[:, :, PAD:TP], r_a[:, :, PAD:TP], ACT.Sqrt), kk_nrm)
            act.wait_ge(mix_used, 3)
            own.done(A(sg_a, ps[:, 2, 0:T], ACT.Sigmoid), lora_h)
            own.done(A(sg_b[0:GLORA - P, :], ps[0:GLORA - P, 3, 0:T], ACT.Sigmoid), lora_h)
            for j in range(3 * KC):
                which, m = j // KC, j % KC
                act.wait_ge(l2_mm, j + 1)
                bank = ps[:, 4 + j % 4, 0:T]
                if which == 0:
                    own.done(A(w_a[:, m, PAD:TP], bank, ACT.Sigmoid, bias=par[:, m, R_W0:R_W0 + 1]), l2_ev)
                elif which == 1:
                    own.done(A(b_a[:, m, PAD:TP], bank, ACT.Sigmoid, bias=par[:, m, R_A0:R_A0 + 1]), l2_ev)
                else:
                    own.done(A(g_a[:, m, :], bank[:, META:T], ACT.Copy), l2_ev)

            def decays(m):
                act.wait_ge(cum_ok, m + 1)
                if m >= 1:
                    act.wait_ge(dec_done, m)
                A(expo[:, 0, :], cum[:, m % 2, :], ACT.Exp, scale=-DECAY)
                A(expo[:, 1, :], cum[:, m % 2, :], ACT.Exp, scale=DECAY)
                own.done(A(expo[:, 2, :], w_a[:, m, :], ACT.Exp, scale=-DECAY), dec_exp)

            act.wait_ge(kk_done, 1)
            for j in range(KC, 3 * KC):
                take(j)
                if 10 <= j < 18:
                    decays(j - 10)
                if 13 <= j < 21:
                    act.wait_ge(rk_mm, j - 12)
                    own.done(A(bonus[:, j - 13, :], ps[:, 4 + (j - 13) % 4, META:T], ACT.Copy), rk_ev)

            act.wait_ge(work_zero, 4)
            act.wait_ge(dec_done, PAIRS)
            with act.Fori(0, NCH) as c:
                for h in range(2):
                    rows = slice(h * CH, (h + 1) * CH)
                    last = A(Bt[rows, :, rows], b_a[rows, :, bass.ds(c * CH, CH)], ACT.Copy)
                last.then_inc(bd_b, 1)
                for n, dst in enumerate((Bs, Ks, Vs)):
                    for h in range(2):
                        act.wait_ge(tr_mm, c * 6 + 2 * n + h + 1)
                        A(dst[:, 4 * h:4 * h + 4, :], ps[:, 4 * h + n, :].rearrange("p (a b) -> p a b", a=4), ACT.Copy)\
                            .then_inc(tr_ev, 1)
                for made, b, dst, evicted in ((rhs_mm, 1, RHS, rhs_ev), (u_mm, 2, U, u_ev)):
                    for h in range(2):
                        act.wait_ge(made, c * 2 + h + 1)
                        A(dst[:, 4 * h:4 * h + 4, :], ps[:, 4 * h + b, :].rearrange("p (a b) -> p a b", a=4), ACT.Copy)\
                            .then_inc(evicted, 1)
                for h in range(2):
                    act.wait_ge(ot_mm, c * 2 + h + 1)
                    for e in range(2):
                        rows = slice(e * CH, (e + 1) * CH)
                        A(w_a[rows, 4 * h:4 * h + 4, bass.ds(c * CH, CH)],
                          ps[rows, 4 * h + 1, :].rearrange("p (a b) -> p a b", a=4)[:, :, rows], ACT.Copy).then_inc(ot_ev, 1)

            for b in range(4):
                act.wait_ge(ht_mm, b + 1)
                t, half = b // 2, b % 2
                own.done(A(acc[:, t, half * 512:(half + 1) * 512], ps[:, b, :], ACT.Copy), ht_cp)
            for m in range(PAIRS):
                act.wait_ge(gn_x, m + 1)
                own.done(A(gn_sq[:, m, :], w_a[:, m, CH:TP], ACT.Square), gn_sqd)
            for m in range(PAIRS):
                act.wait_ge(gn_var, m + 1)
                own.done(A(gn_std[:, m, :], ps[:, m % 4, 0:SEQ], ACT.Sqrt, bias=eps_gn, scale=1.0 / HD), gn_sd)
            for t in range(2):
                act.wait_ge(acc_ok, 2 * t + 2)
                own.done(A(utok[:, t, :], acc[:, t, :], ACT.Square, accum_out=normcol[:, 2, t:t + 1]), n4_ss)
            own.settle()
            own.done(A(rcol[:, 6, :], normcol[:, 2, :], ACT.Sqrt, bias=epsD, scale=1.0 / D), n4_std)
            for b in range(4):
                act.wait_ge(utT_mm, b + 1)
                own.done(A(utT[:, 2 * b:2 * b + 2, :], ps[:, 4 + b, :].rearrange("p (a b) -> p a b", a=2), ACT.Copy), utT_cp)
            act.wait_ge(lg_sub, 1)
            own.done(A(route[:, 2, :, 0:EXPERTS], route[:, 1, :, 0:EXPERTS], ACT.Exp), lg_exp)

            act.sem_inc(e_silu, 2)
            act.sem_inc(ye_ev, 1)
            act.wait_ge(npass_ok, 1)
            n = act.value_load(npass_i[0:1, 0:1], min_val=1, max_val=2)

            def highs(it, a, b):
                for m in range(a, b):
                    act.wait_ge(raw_in[m % NRAW], it * (16 * NHALF // NRAW) + 16 * (m // NRAW + 1))
                    act.wait_ge(w_used, it * NHALF + (m + 1))
                    A(wsplit[:, m % NRING, 0, :], raw_w[:, m % NRAW, :], ACT.Copy).then_inc(w_hi, 1)

            def tokens(j, made):
                for half in range(2):
                    act.wait_ge(xg_mm, made + (half + 1))
                    A(xsplit[:, j, 0, 4 * half:4 * half + 4, :], ps[:, 5 - half, :].rearrange("p (a b) -> p a b", a=4),
                      ACT.Copy).then_inc(xg_hi, 1)

            for m in range(AHEAD):
                act.wait_ge(raw_in[m], 16)
                act.wait_ge(w_used, m + 1)
                A(wsplit[:, m, 0, :], raw_w[:, m, :], ACT.Copy).then_inc(w_hi, 1)
            with act.Fori(0, n) as pas:
                tokens(0, pas * (TURNS * 4 + 2))
                with act.Fori(0, TURNS) as i:
                    it = pas * TURNS + i
                    tables = it * 2 + pas

                    def made(n_):
                        act.wait_ge(w_used, it * NHALF + (2 * n_ + 2 + NRING))

                    def hidden(q):
                        act.wait_ge(et_mm, it * NB2 + (q + 1))
                        A(hsplit[:, q % 2, 0, :, :], ps[:, 4, :].rearrange("p (a b) -> p a b", a=QB), ACT.Copy).then_inc(et_hi, 1)

                    highs(it, AHEAD, NRING)
                    for n_, (kind, q) in enumerate(TILES):
                        if kind == 0:
                            made(n_)
                            act.wait_ge(e_h, it * NB2 + (q + 1))
                            A(silu[:, q % 2, :], ps[:, q % 2, :], ACT.Silu).then_inc(e_silu, 1)
                            if q:
                                hidden(q - 1)
                        if (kind, q) == (2, NB2 - 1):
                            hidden(q)
                            tokens(0, tables * 2 + 4)
                        highs(it, *SPLITS[n_])
                        if (kind, q) == (2, XQ - 1):
                            tokens(1, tables * 2 + 2)
                        if kind == 2 and q % FB == FB - 1:
                            made(n_)
                            A(ye, ps[:, 6:8, :].rearrange("p a b -> p (a b)"), ACT.Copy).then_inc(ye_ev, 1)

        @block.vector
        def _(dve):
            v = nc.vector
            own = Own(dve)
            own.done(v.memset(route[:, :, :, :], 0.0), dve_own)
            own.done(v.memset(ranks[:, :, :], -1.0), dve_own)
            own.done(v.memset(normcol[:, 0, 0:1], EPS), dve_own)
            own.done(v.memset(normcol[:, 0, 1:2], HD * EPS), dve_own)
            own.done(v.memset(normcol[:, 1, 0:1], GN_EPS), dve_own)
            dve.wait_ge(in_tr, 5)
            own.done(v.tensor_copy(hT[:, :, 0:META], ps[:, 4, 0:KC * META].rearrange("p (k t) -> p k t", k=KC)), in_rest)
            dve.wait_ge(in_tr, 6)
            own.done(v.tensor_copy(par[:, :, :], ps[:, 5, 0:KC * NROW].rearrange("p (k t) -> p k t", k=KC)), in_rest)
            own.settle()
            own.done(v.tensor_scalar(one_minus_ka[:, :], par[:, :, R_KA], -1.0, 1.0, ALU.mult, ALU.add), dve_own)

            def rms(n):
                dve.wait_ge(norm_std, n)
                own.done(v.reciprocal(rstd, std), dve_own)
                own.settle()

            def normed_chunk(n, k):
                row = (R_MIXN, R_FFNN, R_MIXN + 1)[n - 1]
                own.done(v.scalar_tensor_tensor(uT[:, k, 1:T + 1], hT[:, k, :], par[:, k, row:row + 1], rstd,
                                                ALU.mult, ALU.mult), norm_u)

            def norm(n):
                rms(n)
                for k in range(KC):
                    normed_chunk(n, k)

            norm(1)
            dve.wait_ge(in_tr, 7)
            own.done(v.tensor_copy(sink[:, :], ps[:, 6, 0:HEADS]), in_rest)
            dve.wait_ge(kz_zero, 1)
            dve.wait_ge(ld_small, 16 * 5)
            for m in range(KC + KVH):
                dve.wait_ge(qk_std, m + 1)
                rs = rstd2[:, m % 2, :]
                own.done(v.reciprocal(rs, rs), dve_own)
                own.settle()
                if m < KC:
                    last = v.scalar_tensor_tensor(qT[:, m, :], raw[:, m % 2, :], qgain[:, 0:1], rs, ALU.mult, ALU.mult)
                else:
                    for h in range(2):
                        rows = slice(h * HD, (h + 1) * HD)
                        last = v.scalar_tensor_tensor(kz[rows, m - KC, h, :], raw[rows, m % 2, :], kgain[rows, 0:1],
                                                      rs[rows, :], ALU.mult, ALU.mult)
                own.done(last, qk_n)

            def masked(c):
                b = c % 2
                dve.wait_ge(sc_mm, c + 1)
                if c >= 2:
                    dve.wait_ge(pt_mm, c - 1)
                o1, o2, o0 = [scores[:, b, :, o:o + n] for o, n in SEG]
                m1, m2, m0 = [attmask[:, o:o + n].unsqueeze(1).to_broadcast([P, 2, n]) for o, n in SEG]
                v.tensor_tensor(o1, ps[:, 0, 0:288].rearrange("p (h k) -> p h k", h=2), m1, ALU.add)
                v.tensor_tensor(o0[0:META], ps[0:META, 0, 288:320].rearrange("p (h k) -> p h k", h=2), m0[0:META], ALU.add)
                own.done(v.tensor_tensor(o2, ps[:, 1:3, 0:T], m2, ALU.add), sc_rd)
                own.settle()
                st = stat[:, b, :, :].rearrange("p a (h s) -> p a h s", h=2)
                for s_, o in enumerate((o1, o2, o0)):
                    last = v.tensor_reduce(st[:, 0, :, s_], o, AX, ALU.max)
                own.done(last, dve_own)
                own.settle()
                sk = sink[:, 2 * c:2 * c + 2].unsqueeze(2).to_broadcast([P, 2, 3])
                own.done(v.tensor_tensor(st[:, 0], st[:, 0], sk, ALU.max), dve_own)
                own.settle()
                own.done(v.tensor_scalar(st[:, 1], st[:, 0], -1.0, None, ALU.mult), dve_own)
                own.settle()
                own.done(v.tensor_tensor(st[:, 3], st[:, 1], sk, ALU.add), sc_max)

            def normed(c):
                b = c % 2
                dve.wait_ge(sc_exp, c + 1)
                own.done(v.tensor_tensor(stat[:, b, 5, :], stat[:, b, 2, :], stat[:, b, 4, :], ALU.add), dve_own)
                own.settle()
                own.done(v.reciprocal(stat[:, b, 6, :], stat[:, b, 5, :]), dve_own)
                own.settle()
                st = stat[:, b, 6, :].rearrange("p (h s) -> p h s", h=2)
                for s_, (o, n) in enumerate(SEG):
                    w = scores[:, b, :, o:o + n]
                    last = v.tensor_tensor(w, w, st[:, :, s_:s_ + 1].to_broadcast([P, 2, n]), ALU.mult)
                own.done(last, p_ok)

            def copies(c):
                dve.wait_ge(pt_mm, c + 1)
                if c >= 2:
                    dve.wait_ge(pv_mm, c - 1)
                b = c % 2
                v.tensor_copy(pT[:, b, 512:768], ps[:, 4, 0:256])
                v.tensor_copy(pT[0:META, b, 1280:1312], ps[0:META, 4, 256:288])
                own.done(v.tensor_copy(pT[0:META, b, 768:1280], ps[0:META, 5, :]), pt_d)

            dve.wait_ge(consts_ok, 1)
            own.done(v.memset(scores[:, :, :, :], 0.0), dve_own)
            own.done(v.memset(stat[:, :, :, :], 0.0), dve_own)
            own.settle()
            masked(0)
            masked(1)
            normed(0)
            for c in range(PAIRS):
                copies(c)
                if c + 1 < PAIRS:
                    normed(c + 1)
                if c + 2 < PAIRS:
                    masked(c + 2)
            for m in range(KC):
                dve.wait_ge(wo_mm, m + 1)
                own.done(v.tensor_tensor(hT[:, m, :], hT[:, m, :], ps[:, m % 4, 0:T], ALU.add), wo_add)
            norm(2)

            dve.sem_inc(ffn_mul, QB)
            with dve.Fori(0, FB) as f:
                for q in range(QB):
                    dve.wait_ge(up_mm, f * QB + (q + 1))
                    dve.wait_ge(ffn_silu, f * QB + (q + 1 + QB))
                    v.tensor_tensor(hid[:, bass.ds(f * QB + q, 1), :], sgate[:, q:q + 1, :], ps[:, 4 + q:5 + q, 0:T],
                                    ALU.mult).then_inc(ffn_mul, 1)
            for k in range(KC):
                dve.wait_ge(down_q, k + 1)
                own.done(v.tensor_tensor(hT[:, k, :], hT[:, k, :], ps[:, k, 0:T], ALU.add), down_add)
            own.settle()

            def mix(k, buf, i):
                return v.scalar_tensor_tensor(xm[buf][:, k, :], xx[:, k, :], par[:, k, R_MIX + i:R_MIX + i + 1],
                                              uT[:, k, 1:T + 1], ALU.mult, ALU.add)

            rms(3)
            for k in range(KC + 2):
                if k < KC:
                    normed_chunk(3, k)
                if 1 <= k <= KC:
                    dve.wait_ge(norm_u, 2 * KC + k)
                    own.done(v.tensor_tensor(xx[:, k - 1, :], uT[:, k - 1, 0:T], uT[:, k - 1, 1:T + 1], ALU.subtract), xx_ok)
                if k >= 2:
                    dve.wait_ge(xx_ok, k - 1)
                    own.done(mix(k - 2, 0, 2), mixk_ok)

            def mixes(buf, i, free=None, n=0):
                if free is not None:
                    dve.wait_ge(free, n)
                for k in range(KC):
                    last = mix(k, buf, i)
                own.done(last, mix_ok)

            def kk_floor(m):
                dve.wait_ge(kk_ss, m + 1)
                own.done(v.tensor_scalar(r_a[:, m, PAD:TP], ps[:, 4 + m % 4, 0:T], 1e-24, None, ALU.max), kk_ev)

            mixes(1, 1)
            for m in range(PAIRS):
                dve.wait_ge(pr_ev, m + 1)
                own.done(v.tensor_scalar(kk_a[:, m, PAD:TP], k_a[:, m, PAD:TP], par[:, m, R_KK:R_KK + 1], None, ALU.mult), kk_ok)
            mixes(0, 4, pr_mm, KC)
            for m in range(4):
                kk_floor(m)
            mixes(1, 5, mix_used, 1)
            for m in range(4, PAIRS):
                kk_floor(m)
            mixes(0, 0, mix_used, 2)
            mixes(1, 3, mix_used, 3)
            dve.wait_ge(l2_ev, 2 * KC)
            for m in range(PAIRS):
                last = v.tensor_scalar(v_a[:, m, PAD:TP], b_a[:, m, PAD:TP], par[:, m, R_KA:R_KA + 1],
                                       one_minus_ka[:, m:m + 1], ALU.mult, ALU.add)
            own.done(last, dve_own)
            own.settle()
            own.done(v.tensor_tensor(k_a[:, :, PAD:TP], k_a[:, :, PAD:TP], v_a[:, :, PAD:TP], ALU.mult), dve_own)
            dve.wait_ge(kk_nrm, 1)
            own.done(v.reciprocal(r_a[:, :, PAD:TP], r_a[:, :, PAD:TP]), dve_own)
            own.settle()
            own.done(v.tensor_tensor(kk_a[:, :, PAD:TP], kk_a[:, :, PAD:TP], r_a[:, :, PAD:TP], ALU.mult), kk_done)
            own.settle()
            own.done(v.tensor_tensor(b_a[:, :, PAD:TP], b_a[:, :, PAD:TP], kk_a[:, :, PAD:TP], ALU.mult), dve_own)
            own.settle()
            dve.wait_ge(pads_zero, 3)
            for m in range(PAIRS):
                dve.wait_ge(pr_ev, KC + 1 + m)
                own.done(v.scalar_tensor_tensor(v_a[:, m, PAD:TP], r_a[:, m, PAD:TP], par[:, m, R_RK:R_RK + 1],
                                                k_a[:, m, PAD:TP], ALU.mult, ALU.mult), rk_ok)
                own.done(v.tensor_tensor_scan(cum[:, m % 2, :], reset[:, :], w_a[:, m, :], 0.0, ALU.mult, ALU.add), dve_own)
                own.settle()
                dve.wait_ge(rk_ok, m + 1)
                own.done(v.tensor_tensor(w_a[:, m, :], cum[:, m % 2, :], w_a[:, m, :], ALU.subtract), cum_ok)
                dve.wait_ge(dec_exp, m + 1)
                v.tensor_tensor(r_a[:, m, :], r_a[:, m, :], expo[:, 0, :], ALU.mult)
                v.tensor_copy(chunkdecay[:, m, :], expo[:, 0, :].rearrange("p (c i) -> p c i", c=NCH)[:, :, CH - 1])
                v.tensor_tensor(b_a[:, m, :], b_a[:, m, :], expo[:, 1, :], ALU.mult)
                v.tensor_tensor(k_a[:, m, :], k_a[:, m, :], expo[:, 1, :], ALU.mult)
                own.done(v.scalar_tensor_tensor(kk_a[:, m, :], kk_a[:, m, :], -1.0, expo[:, 2, :], ALU.mult, ALU.mult), dec_done)
            for m in range(PAIRS):
                dve.wait_ge(rk_ev, m + 1)
                dve.wait_ge(pr_ev, 2 * KC + 1 + m)
                own.done(v.tensor_tensor(bonus[:, m, :], bonus[:, m, :], v_a[:, m, CH:TP], ALU.mult), dve_own)
            own.settle()

            dve.wait_ge(work_zero, 4)
            v.memset(S[:, 0:4, :], 0.0).then_inc(s_ok, 1)
            v.memset(S[:, 4:8, :], 0.0).then_inc(s_ok, 1)
            own.settle()
            bc = lambda m_: m_.unsqueeze(1).to_broadcast([P, 4, P])
            with dve.Fori(0, NCH) as c:
                for src, j in ((kk_a, 0), (r_a, 1)):
                    for h in range(2):
                        rows = slice(h * CH, (h + 1) * CH)
                        last = v.tensor_copy(ARt[rows, :, j, rows], src[rows, :, bass.ds(c * CH, CH)])
                last.then_inc(bd_ar, 1)
                halves = [slice(4 * h, 4 * h + 4) for h in range(2)]

                def products(n):
                    dst, h = (NA, KA)[n // 2], n % 2
                    dve.wait_ge(ap_mm, c * 4 + n + 1)
                    for q in range(2):
                        last = v.tensor_tensor(
                            dst[:, 4 * h + 2 * q:4 * h + 2 * q + 2, :, :].rearrange("p a b c -> p a (b c)"),
                            ps[:, 4 * h + 2 * (n // 2) + q, :].rearrange("p (a b) -> p a b", a=2),
                            causal[:, :, :].rearrange("p b c -> p (b c)").unsqueeze(1).to_broadcast([P, 2, 2 * P]), ALU.mult)
                    last.then_inc(ap_ev, 1)

                for n in range(4):
                    products(n)
                dve.wait_ge(ap_ev, c * 4 + 4)
                for hs in halves:
                    last = v.tensor_tensor(XT[:, hs, :], NA[:, hs, 0, :], bc(level1T[:, :]), ALU.mult)
                last.then_inc(rec_own, 1)
                dve.wait_ge(rec_own, c * 12 + 1)
                for hs in halves:
                    last = v.tensor_tensor(XT[:, hs, :], XT[:, hs, :], bc(ident[:, :]), ALU.add)
                last.then_inc(rec_own, 1)
                dve.wait_ge(rec_own, c * 12 + 2)
                for hs in halves:
                    v.transpose(X[:, hs, :].rearrange("p a b -> p (a b)"), XT[:, hs, :].rearrange("p a b -> p (a b)"))\
                        .then_inc(x_ok, 1)
                for l in range(NLV):
                    for h, hs in enumerate(halves):
                        dve.wait_ge(y_mm, c * 10 + 2 * l + h + 1)
                        v.tensor_tensor(Y[:, hs, :], ps[:, 4 * h + 3, :].rearrange("p (a b) -> p a b", a=4),
                                        bc(levelmask[:, l, :]), ALU.mult).then_inc(y_ev, 1)
                    for h, hs in enumerate(halves):
                        dve.wait_ge(x_mm, c * 10 + 2 * l + h + 1)
                        b = ps[:, 4 * h, :].rearrange("p (a b) -> p a b", a=4)
                        if l < NLV - 1:
                            v.tensor_tensor(X[:, hs, :], X[:, hs, :], b, ALU.add).then_inc(rec_own, 1)
                            dve.wait_ge(rec_own, c * 12 + 3 + 2 * l + h)
                            v.transpose(XT[:, hs, :].rearrange("p a b -> p (a b)"), X[:, hs, :].rearrange("p a b -> p (a b)"))\
                                .then_inc(x_ok, 1)
                        else:
                            v.tensor_tensor(XT[:, hs, :], XT[:, hs, :], b, ALU.add).then_inc(x_ok, 1)
                for h, hs in enumerate(halves):
                    dve.wait_ge(s_mm, c * 2 + h + 1)
                    v.tensor_tensor(S[:, hs, :], S[:, hs, :], ps[:, 4 * h + 3, :].rearrange("p (a b) -> p a b", a=4), ALU.add)\
                        .then_inc(rec_own, 1)
                    dve.wait_ge(rec_own, c * 12 + 11 + h)
                    v.tensor_tensor(S[:, hs, :], S[:, hs, :],
                                    chunkdecay[:, hs, bass.ds(c, 1)].to_broadcast([P, 4, P]), ALU.mult).then_inc(s_ok, 1)

            dve.sem_inc(w_lo, NRAW)
            for m in range(PAIRS):
                dve.wait_ge(gn_mm, m + 1)
                o = w_a[:, m, CH:TP]
                own.done(v.scalar_tensor_tensor(o, ps[:, 4 + m % 4, 0:SEQ], -1.0 / HD, o, ALU.mult, ALU.add), gn_x)
            for m in range(PAIRS):
                dve.wait_ge(gn_sd, m + 1)
                own.done(v.reciprocal(gn_std[:, m, :], gn_std[:, m, :]), dve_own)
                own.settle()
                o = w_a[:, m, CH:TP]
                own.done(v.scalar_tensor_tensor(o, o, par[:, m, R_GNW:R_GNW + 1], gn_std[:, m, :], ALU.mult, ALU.mult), dve_own)
                own.settle()
                own.done(v.scalar_tensor_tensor(o, o, par[:, m, R_GNB:R_GNB + 1], bonus[:, m, :], ALU.add, ALU.add), dve_own)
                own.settle()
                own.done(v.tensor_tensor(o, o, g_a[:, m, :], ALU.mult), y_ok)
            for n in range(4):
                t, h = n // 2, n % 2
                dve.wait_ge(wo2_mm, n + 1)
                a_ = acc[:, t, h * 512:(h + 1) * 512]
                dve.wait_ge(ht_cp, 4)
                own.done(v.tensor_tensor(a_, a_, ps[:, n, :], ALU.add), acc_ok)
            dve.wait_ge(n4_std, 1)
            dve.wait_ge(ld_gain, 16)
            own.done(v.reciprocal(rcol[:, 7, :], rcol[:, 6, :]), dve_own)
            own.settle()
            for t in range(2):
                own.done(v.scalar_tensor_tensor(utok[:, t, :], acc[:, t, :], rcol[:, 7, t:t + 1], gainrow,
                                                ALU.mult, ALU.mult), utok_ok)

            col = lambda n: rcol[:, n, :]
            wide = lambda n: rcol[:, n, :].unsqueeze(2).to_broadcast([P, 2, EXPERTS])
            rt = lambda n: route[:, n, :, 0:EXPERTS]

            def step(ins, s_=dve_own):
                own.done(ins, s_)
                own.settle()

            dve.wait_ge(lg_mm, 1)
            step(v.tensor_copy(rt(3), ps[:, 0, 0:16].rearrange("p (t e) -> p t e", t=2)))
            step(v.tensor_reduce(col(0), rt(3), AX, ALU.max))
            step(v.tensor_tensor(rt(1), rt(3), wide(0), ALU.subtract), lg_sub)
            dve.wait_ge(lg_exp, 1)
            step(v.tensor_reduce(col(1), rt(2), AX, ALU.add))
            step(v.reciprocal(col(2), col(1)))
            step(v.tensor_tensor(rt(3), rt(2), wide(2), ALU.mult))
            for n, src, best in ((0, 3, 3), (1, 7, 4)):
                step(v.tensor_reduce(col(best), rt(src), AX, ALU.max))
                step(v.tensor_tensor(rt(4), rt(src), wide(best), ALU.is_equal))
                step(v.scalar_tensor_tensor(rt(5), rt(4), -8.0, expno8[:, :, :], ALU.mult, ALU.add))
                step(v.tensor_reduce(col(5), rt(5), AX, ALU.min))
                step(v.tensor_tensor(rt(8 + n), expno[:, :, :], wide(5), ALU.is_equal))
                if n == 0:
                    step(v.scalar_tensor_tensor(rt(7), rt(8), -2.0, rt(3), ALU.mult, ALU.add))
            step(v.tensor_tensor(rt(0), rt(8), rt(9), ALU.add), mask_ok)
            step(v.tensor_tensor(rt(6), rt(3), rt(0), ALU.mult))
            step(v.tensor_reduce(col(1), rt(6), AX, ALU.add))
            step(v.reciprocal(col(2), col(1)))
            step(v.tensor_tensor(rt(10), rt(6), wide(2), ALU.mult))
            dve.wait_ge(rank_mm, 1)
            step(v.tensor_copy(ranks[:, :, 0:EXPERTS], ps[:, 1, 0:24].rearrange("p (t e) -> p t e", t=3)))
            step(v.tensor_reduce(rcol[:, 0, 0:1], ranks[:, 2, 0:EXPERTS], AX, ALU.max))
            step(v.tensor_scalar(npass_i[:, :], rcol[:, 0, 0:1], float(P), 1.0, ALU.is_gt, ALU.add), npass_ok)

            dve.sem_inc(e_h, 2)
            dve.sem_inc(et_ev, 1)
            dve.sem_inc(es_add, 1)
            n = dve.value_load(npass_i[0:1, 0:1], min_val=1, max_val=2)
            chosen, gate = route[:, 0, :, :], route[:, 10, :, :]

            def choose(j, expert):
                e = bass.ds(expert, 1)
                for t in range(2):
                    v.tensor_scalar(sel[:, j, t, :], slotno[:, :], ranks[:, t, e], chosen[:, t, e], ALU.is_equal, ALU.mult)
                    last = v.tensor_scalar(selg[:, j, t, :], slotno[:, :], ranks[:, t, e], gate[:, t, e],
                                           ALU.is_equal, ALU.mult)
                last.then_inc(sel_ok, 1)

            def lows(it, a, b):
                for m in range(a, b):
                    dve.wait_ge(w_hi, it * NHALF + (m + 1))
                    v.tensor_tensor(wsplit[:, m % NRING, 1, :], raw_w[:, m % NRAW, :],
                                    wsplit[:, m % NRING, 0, :].bitcast(F32), ALU.subtract).then_inc(w_lo, 1)

            def tokens(j, made):
                for half in range(2):
                    dve.wait_ge(xg_hi, made + (half + 1))
                    ks = slice(4 * half, 4 * half + 4)
                    v.tensor_tensor(xsplit[:, j, 1, ks, :], ps[:, 5 - half, :].rearrange("p (a b) -> p a b", a=4),
                                    xsplit[:, j, 0, ks, :].bitcast(F32), ALU.subtract).then_inc(xg_ev, 1)

            def gate_rows(j, made):
                dve.wait_ge(st_mm, made)
                v.tensor_copy(selT[:, j, :, :], ps[:, 5, 0:256].rearrange("p (a b) -> p a b", a=2)).then_inc(st_ev, 1)

            def collect(o, made):
                dve.wait_ge(es_mm, made)
                t, h = o // 2, o % 2
                a_ = acc[:, t, h * BLK:(h + 1) * BLK]
                v.tensor_tensor(a_, a_, ps[:, 5, :], ALU.add).then_inc(es_add, 1)

            v.memset(ye, 0.0)
            for m in range(AHEAD):
                dve.wait_ge(w_hi, m + 1)
                v.tensor_tensor(wsplit[:, m, 1, :], raw_w[:, m, :], wsplit[:, m, 0, :].bitcast(F32), ALU.subtract)\
                    .then_inc(w_lo, 1)
            with dve.Fori(0, n) as pas:
                choose(0, 0)
                v.memset(selT[:, 1, :, :], 0.0)
                tokens(0, pas * (TURNS * 4 + 2))
                gate_rows(0, pas * (TURNS * 2 + 1) + 1)
                with dve.Fori(0, TURNS) as i:
                    it = pas * TURNS + i
                    tables = it * 2 + pas
                    adds = it * 8 + pas * 4

                    def hidden_lo(q):
                        dve.wait_ge(et_hi, it * NB2 + (q + 1))
                        v.tensor_tensor(hsplit[:, q % 2, 1, :, :], ps[:, 4, :].rearrange("p (a b) -> p a b", a=QB),
                                        hsplit[:, q % 2, 0, :, :].bitcast(F32), ALU.subtract).then_inc(et_ev, 1)

                    lows(it, AHEAD, NRING)
                    for n_, (kind, q) in enumerate(TILES):
                        if kind == 0:
                            if q == XQ + 1:
                                gate_rows(1, tables + 2)
                            if q in LATE:
                                _, o, n0 = LATE[q]
                                collect(o, adds + (n0 + 1))
                            if q:
                                hidden_lo(q - 1)
                        elif kind == 1:
                            dve.wait_ge(w_used, it * NHALF + (2 * n_ + 2 + NRING))
                            dve.wait_ge(e_silu, it * NB2 + (q + 3))
                            v.tensor_tensor(hbuf[:, q % 2, :], silu[:, q % 2, :], ps[:, 2 + q % 2, :], ALU.mult).then_inc(e_h, 1)
                            if q in LATE:
                                collect(o + 1, adds + (n0 + 2))
                            if q == 3:
                                choose(1, 2 * i + 1)
                            if q == FB + 3:
                                choose(0, 2 * i + 2)
                        if (kind, q) == (2, NB2 - 1):
                            hidden_lo(q)
                            tokens(0, tables * 2 + 4)
                            gate_rows(0, tables + 3)
                        lows(it, *SPLITS[n_])
                        if (kind, q) == (2, XQ - 1):
                            tokens(1, tables * 2 + 2)
                turns = pas * TURNS + TURNS
                for o in range(4):
                    collect(o, turns * 8 + pas * 4 + (o + 1))
                v.tensor_scalar(ranks[:, 0:2, :], ranks[:, 0:2, :], -float(P), None, ALU.add).then_inc(rec_own, 1)
                dve.wait_ge(rec_own, pas + (12 * NCH + 1))
                dve.wait_ge(es_add, turns * 8 + pas * 4 + 5)
            dve.sem_inc(acc_done, 1)


_INS = ['x', 'meta_tokens', 'mixer_norm', 'ffn_norm', 'attn_w_qkv', 'attn_q_norm', 'attn_k_norm', 'attn_sinks',
        'attn_w_o', 'rwkv_mix', 'rwkv_w0', 'rwkv_w1', 'rwkv_w2', 'rwkv_a0', 'rwkv_a1', 'rwkv_a2', 'rwkv_g1', 'rwkv_g2',
        'rwkv_k_k', 'rwkv_k_a', 'rwkv_r_k', 'rwkv_w_r', 'rwkv_w_k', 'rwkv_w_v', 'rwkv_w_o', 'rwkv_gn_w', 'rwkv_gn_b',
        'ffn_w_gate', 'ffn_w_up', 'ffn_w_down', 'moe_router', 'moe_w_gate', 'moe_w_up', 'moe_w_down']


def kernel(**inputs):
    import numpy as _np
    import concourse.bacc as _bacc
    from concourse import mybir as _mybir
    from concourse.bass_utils import run_bass_kernel_spmd as _run

    nc = _bacc.Bacc("TRN2", target_bir_lowering=False, num_devices=1)
    arrays, args = {}, []
    for name in _INS:
        a = _np.ascontiguousarray(inputs[name])
        arrays[f"in_{name}"] = a
        args.append(nc.dram_tensor(f"in_{name}", a.shape, _mybir.dt.from_np(a.dtype), kind="ExternalInput").ap())
    args.append(nc.dram_tensor("out_0", (1, SEQ, D), _mybir.dt.float32, kind="ExternalOutput").ap())
    build(nc, *args)
    r = _run(nc, [arrays], core_ids=[0])
    return r.results[0]["out_0"]
```

```python
import math
from contextlib import ExitStack

import concourse.bass as bass
from concourse import mybir

F32 = mybir.dt.float32
F32R = mybir.dt.float32r
I32 = mybir.dt.int32
ALU = mybir.AluOpType
ACT = mybir.ActivationFunctionType
AX = mybir.AxisListType.X

P = 128
D = 1024
KC = D // P
META = 16
SEQ = 256
T = META + SEQ
HEADS, KVH, HD = 16, 4, 64
PAIRS = HEADS // 2
FF = 3584
BLK = 512
FB = FF // BLK
QB = BLK // P
EXPERTS = 8
EPS, GN_EPS = 1e-5, 64e-5
CH = 64
PAD = CH - META
NCH = (PAD + T) // CH
TP = NCH * CH
LORA, GLORA = 64, 160
DECAY = math.exp(-0.5)
NEG = -1e30
R_MIXN, R_FFNN, R_MIX, R_W0, R_A0, R_KK, R_KA, R_RK, R_GNW, R_GNB, NROW = 0, 2, 4, 10, 11, 12, 13, 14, 15, 16, 17


class Own:

    def __init__(self, eng):
        self.eng, self.count, self.last = eng, {}, None

    def done(self, ins, sem):
        ins.then_inc(sem, 1)
        k = id(sem)
        self.count[k] = self.count.get(k, 0) + 1
        self.last = (sem, k)
        return ins

    def settle(self):
        sem, k = self.last
        self.eng.wait_ge(sem, self.count[k])


def build(nc, x, meta_tokens, mixer_norm, ffn_norm, attn_w_qkv, attn_q_norm, attn_k_norm, attn_sinks, attn_w_o,
          rwkv_mix, rwkv_w0, rwkv_w1, rwkv_w2, rwkv_a0, rwkv_a1, rwkv_a2, rwkv_g1, rwkv_g2, rwkv_k_k, rwkv_k_a,
          rwkv_r_k, rwkv_w_r, rwkv_w_k, rwkv_w_v, rwkv_w_o, rwkv_gn_w, rwkv_gn_b, ffn_w_gate, ffn_w_up, ffn_w_down,
          moe_router, moe_w_gate, moe_w_up, moe_w_down, out):
    ctx = ExitStack()
    with ctx:
        def sb(name, shape, dt=F32):
            return ctx.enter_context(nc.sbuf_tensor(name, shape, dt))

        def sem(name):
            return ctx.enter_context(nc.semaphore(name))

        ident = sb("ident", [P, P])
        ones = sb("ones", [P, P])
        headones = sb("headones", [P, P])
        levelmask = sb("levelmask", [P, 5, P])
        level1T = sb("level1T", [P, P])
        causal = sb("causal", [P, 2, P])
        reset = sb("reset", [P, TP])
        slotno = sb("slotno", [P, P])
        before = sb("before", [P, P])
        expno = sb("expno", [P, 2, EXPERTS])
        expno8 = sb("expno8", [P, 2, EXPERTS])
        SEG = [(0, META + P), (META + P, T), (META + P + T, META)]
        NSC = 2 * META + P + T
        attmask = sb("attmask", [P, NSC])
        par = sb("par", [P, KC, NROW])
        one_minus_ka = sb("one_minus_ka", [P, KC])
        qgain = sb("qgain", [P, 1])
        kgain = sb("kgain", [P, 1])
        sinkrow = sb("sinkrow", [1, HEADS])
        sink = sb("sink", [P, HEADS])
        router = sb("router", [P, KC, EXPERTS])
        stat = sb("stat", [P, 2, 8, 6])
        chunkdecay = sb("chunkdecay", [P, PAIRS, NCH])
        NEXT = EXPERTS + 1
        route = sb("route", [P, 16, 2, NEXT])
        rcol = sb("rcol", [P, 8, 2])
        ranks = sb("ranks", [P, 3, NEXT])
        npass_i = sb("npass_i", [P, 1], I32)
        normcol = sb("normcol", [P, 3, 2])

        ARENA = 50016
        RAW = KC * T + 2 * KC * BLK
        SPLIT = 26752
        HALF = KC * BLK // 2
        NRAW, NRING = 7, 4
        with nc.sbuf_tensor("under_raw", [P, RAW], F32), nc.sbuf_tensor("raw_w", [P, NRAW, HALF], F32) as raw_w, \
                nc.sbuf_tensor("under_split", [P, SPLIT - RAW - NRAW * HALF], F32), \
                nc.sbuf_tensor("wsplit", [P, NRING, 2, HALF], F32R) as wsplit, \
                nc.sbuf_tensor("xsplit", [P, 2, 2, KC, P], F32R) as xsplit, \
                nc.sbuf_tensor("hsplit", [P, 2, 2, QB, P], F32R) as hsplit:
            pass
        arena = sb("arena", [P, ARENA])

        def area(off, *dims):
            n = 1
            for d in dims:
                n *= d
            assert off + n <= ARENA, (off, dims)
            v = arena[:, off:off + n]
            if len(dims) == 2:
                v = v.rearrange("p (a b) -> p a b", a=dims[0])
            elif len(dims) == 3:
                v = v.rearrange("p (a b c) -> p a b c", a=dims[0], b=dims[1])
            elif len(dims) == 4:
                v = v.rearrange("p (a b c d) -> p a b c d", a=dims[0], b=dims[1], c=dims[2])
            return v

        hT = area(0, KC, T)
        SLOT0 = KC * T
        SLOT = KC * BLK
        NSLOT = 6
        slot = [area(SLOT0 + s * SLOT, SLOT) for s in range(NSLOT)]
        slot_k = [area(SLOT0 + s * SLOT, KC, BLK) for s in range(NSLOT)]
        slot_d = [area(SLOT0 + s * SLOT, QB, D) for s in range(NSLOT)]
        UT = SLOT0 + NSLOT * SLOT
        uT = area(UT, KC, T + 1)
        A0 = UT + KC * (T + 1)
        qT = area(A0, KC, T)
        kz = area(A0 + 2176, KVH, 2, T)
        vdup = area(A0 + 4352, 3, KVH, P)
        oT = area(A0 + 5888, KC, T)
        scores = area(A0 + 8064, 2, 2, NSC)
        PTW = 512 + 256 + 512 + 32
        pT = area(A0 + 9792, 2, PTW)
        raw = area(A0 + 12416, 2, T)
        rsq = area(A0 + 12960, 2, T)
        rstd2 = area(A0 + 13504, 2, T)
        sq = area(A0 + 14048, KC, T)
        std = area(A0 + 16224, T)
        rstd = area(A0 + 16496, T)
        wkdup = area(A0 + 16768, KC, KVH, 2, HD)
        xtok = area(A0, 2, D)
        mtok = area(A0 + 2048, D)
        prow = area(A0 + 3072, D)
        hid = area(A0, FF // P, T)
        sgate = area(A0 + 7616, QB, T)
        ARR = ARENA - (6 * PAIRS * TP + 2 * PAIRS * SEQ)
        r_a, kk_a, k_a, b_a, v_a, w_a = [area(ARR + n * PAIRS * TP, PAIRS, TP) for n in range(6)]
        g_a = area(ARR + 6 * PAIRS * TP, PAIRS, SEQ)
        bonus = area(ARR + 6 * PAIRS * TP + PAIRS * SEQ, PAIRS, SEQ)
        X4 = SLOT0 + 4 * SLOT
        xx = area(X4, KC, T)
        xm = [area(X4 + 2176 * (1 + n), KC, T) for n in range(2)]
        th_w, th_a, sg_a, sg_b = [area(X4 + 6528 + n * T, T) for n in range(4)]
        assert X4 + 6528 + 4 * T <= UT
        cum = area(A0, 2, TP)
        expo = area(A0 + 2 * TP, 3, TP)
        assert A0 + 5 * TP <= ARR
        wk = SLOT0 + 2 * SLOT
        ARt = area(X4 + 2176, PAIRS, 2, P)
        Bt = area(UT - 1024, PAIRS, P)
        Kt, Vt = area(UT, PAIRS, P), area(UT + 1024, PAIRS, P)
        S = area(A0, PAIRS, P)
        Bs, Ks, Vs, X, XT, Y = [area(wk + n * 1024, PAIRS, P) for n in range(6)]
        NA = area(wk + 6144, PAIRS, 2, P)
        KA = area(wk + 8192, PAIRS, 2, P)
        RHS, U = [area(X4 + 4224 + n * 1024, PAIRS, P) for n in range(2)]
        assert wk + 10240 <= X4 + 2176 and X4 + 4224 + 2048 <= UT - 1024 and X4 + 6528 <= UT - 1024
        gn_std = area(UT, PAIRS, SEQ)
        gn_sq = area(ARR + 4096, PAIRS, SEQ)
        gainrow = area(ARR + 6144, D)
        assert UT + 2048 <= ARR
        utok = area(0, 2, D)
        hbuf = area(SLOT0, 2, BLK)
        silu = area(SLOT0 + 1024, 2, BLK)
        ye = area(SLOT0 + 2048, D)
        sel = area(SLOT0 + 3072, 2, 2, P)
        selg = area(SLOT0 + 3584, 2, 2, P)
        selT = area(SLOT0 + 4096, 2, 2, P)
        utT = area(SLOT0 + 4608, KC, SEQ)
        acc = area(RAW + NRAW * HALF, 2, D)
        assert RAW + NRAW * HALF + 2 * D <= SPLIT and SPLIT + 2 * (NRING * HALF + KC * 2 * P + QB * 2 * P) <= ARENA

        ps = ctx.enter_context(nc.psum_tensor("ps", [P, 8, 512], F32))

        QK = [0, 1, 2, 3, 8, 9, 10, 11, 4, 5, 6, 7]

        ld_x = [sem("ld_x0"), sem("ld_x1")]
        ld_meta, ld_par, ld_small, ld_gain, ld_router = [sem(n) for n in (
            "ld_meta", "ld_par", "ld_small", "ld_gain", "ld_router")]
        slot_in = [sem(f"slot_in{s}") for s in range(NSLOT)]
        pool_own, ident_ok, consts_ok, kw_ok, kz_zero, pads_zero, work_zero = [sem(n) for n in (
            "pool_own", "ident_ok", "consts_ok", "kw_ok", "kz_zero", "pads_zero", "work_zero")]
        act_own, dve_own = sem("act_own"), sem("dve_own")
        in_tr, in_x, in_rest = sem("in_tr"), sem("in_x"), sem("in_rest")
        norm_sq, norm_ss, norm_std, norm_u = [sem(n) for n in ("norm_sq", "norm_ss", "norm_std", "norm_u")]
        qk_mm, qk_sq, qk_ss, qk_std, qk_n, v_mm, v_cp = [sem(n) for n in (
            "qk_mm", "qk_sq", "qk_ss", "qk_std", "qk_n", "v_mm", "v_cp")]
        sc_mm, sc_rd, sc_max, sc_exp, p_ok, pt_mm, pt_a, pt_d, pv_mm, o_cp = [sem(n) for n in (
            "sc_mm", "sc_rd", "sc_max", "sc_exp", "p_ok", "pt_mm", "pt_a", "pt_d", "pv_mm", "o_cp")]
        wo_mm, wo_add = sem("wo_mm"), sem("wo_add")
        gate_mm, up_mm, ffn_silu, ffn_mul, down_mm, down_q, down_add = [sem(n) for n in (
            "gate_mm", "up_mm", "ffn_silu", "ffn_mul", "down_mm", "down_q", "down_add")]
        xx_ok, mixk_ok = sem("xx_ok"), sem("mixk_ok")
        mix_ok, mix_used, lora_h, l2_mm, l2_ev, pr_mm, pr_ev = [sem(n) for n in (
            "mix_ok", "mix_used", "lora_h", "l2_mm", "l2_ev", "pr_mm", "pr_ev")]
        kk_ok, kk_sq, kk_ss, kk_ev, kk_nrm, kk_done, rk_ok, rk_mm, rk_ev = [sem(n) for n in (
            "kk_ok", "kk_sq", "kk_ss", "kk_ev", "kk_nrm", "kk_done", "rk_ok", "rk_mm", "rk_ev")]
        cum_ok, dec_exp, dec_done = [sem(n) for n in ("cum_ok", "dec_exp", "dec_done")]
        bd_ar, bd_b, bd_kv, ap_mm, ap_ev, tr_mm, tr_ev = [sem(n) for n in (
            "bd_ar", "bd_b", "bd_kv", "ap_mm", "ap_ev", "tr_mm", "tr_ev")]
        y_mm, y_ev, x_mm, x_ok, rhs_mm, rhs_ev, u_mm, u_ev, ot_mm, ot_ev, s_mm, s_ok, rec_own = [sem(n) for n in (
            "y_mm", "y_ev", "x_mm", "x_ok", "rhs_mm", "rhs_ev", "u_mm", "u_ev", "ot_mm", "ot_ev", "s_mm", "s_ok", "rec_own")]
        ht_mm, ht_cp, gn_mm, gn_x, gn_sqd, gn_var, gn_sd, y_ok, wo2_mm, acc_ok = [sem(n) for n in (
            "ht_mm", "ht_cp", "gn_mm", "gn_x", "gn_sqd", "gn_var", "gn_sd", "y_ok", "wo2_mm", "acc_ok")]
        n4_ss, n4_std, utok_ok, utT_mm, utT_cp, lg_mm, lg_sub, lg_exp, mask_ok, rank_mm, npass_ok = [sem(n) for n in (
            "n4_ss", "n4_std", "utok_ok", "utT_mm", "utT_cp", "lg_mm", "lg_sub", "lg_exp", "mask_ok", "rank_mm", "npass_ok")]
        sel_ok, xg_mm, xg_hi, xg_ev, st_mm, st_ev = [sem(n) for n in ("sel_ok", "xg_mm", "xg_hi", "xg_ev", "st_mm", "st_ev")]
        raw_in = [sem(f"raw_in{n}") for n in range(NRAW)]
        w_hi, w_lo, w_used, et_hi = sem("w_hi"), sem("w_lo"), sem("w_used"), sem("et_hi")
        et_mm, e_silu, e_h, et_ev, ye_ev, es_mm, es_add = [sem(n) for n in (
            "et_mm", "e_silu", "e_h", "et_ev", "ye_ev", "es_mm", "es_add")]
        acc_done, out_sem = sem("acc_done"), sem("out_sem")

        block = ctx.enter_context(nc.Block())

        NB2 = 2 * FB
        TILES = [(0, 0), (1, 0)]
        for q in range(1, NB2):
            TILES += [(0, q), (1, q), (2, q - 1)]
        TILES.append((2, NB2 - 1))
        NHALF = 2 * len(TILES)
        TURNS = EXPERTS // 2
        LATE = {0: (1, 0, 0), 1: (1, 2, 2), FB + 1: (0, 0, 4), FB + 2: (0, 2, 6)}
        AHEAD = 2
        SPLITS = [(2 * n + NRING, 2 * n + 2 + NRING) for n in range(len(TILES) - 2)] + [(0, 0), (NHALF, NHALF + AHEAD)]
        XQ = 5
        assert NHALF % NRAW == 0 and NHALF % NRING == 0
        NLV = 5
        NLV0 = 3
        LESS = {"y": 4, "x": 4, "rec": 6}

        @block.sync
        def _(sp):
            def cols(w, n):
                return w.rearrange("(k p) n -> p k n", p=P)[:, :, n * BLK:(n + 1) * BLK]

            def load(s, dst, src):
                sp.dma_start(dst, src).then_inc(slot_in[s], 16)

            wqkv, wo = attn_w_qkv[0], attn_w_o[0]
            wg, wu, wd = ffn_w_gate[0], ffn_w_up[0], ffn_w_down[0]
            for t in range(2):
                sp.dma_start(xtok[:, t, :], x[0, t * P:(t + 1) * P, :]).then_inc(ld_x[t], 16)
            sp.wait_ge(ld_par, 160)
            load(0, slot_k[0], cols(wqkv, 0))
            load(2, slot_k[2], cols(wqkv, 2))
            load(1, slot_k[1], cols(wqkv, 1))
            load(3, slot_k[3], cols(wo, 0))
            load(4, slot_k[4], cols(wo, 1))
            load(5, slot_k[5], cols(wg, 0))
            sp.dma_start(router[:, :, :], moe_router[0].rearrange("(k p) e -> p k e", p=P)).then_inc(ld_router, 16)
            sp.wait_ge(qk_mm, 4)
            load(0, slot_k[0], cols(wu, 0))
            wd_v = wd.rearrange("(r k p) n -> r p k n", p=P, k=FB)
            dk = [slot_k[1 + r][:, 0:FB, :] for r in range(4)]
            for r, (s_, n) in enumerate(((qk_mm, 12), (v_mm, 3), (wo_mm, 4), (wo_mm, 8))):
                sp.wait_ge(s_, n)
                load(1 + r, dk[r], wd_v[r, :, :, 0:BLK])
            with sp.Fori(1, FB) as f:
                sp.wait_ge(gate_mm, f * QB)
                load(5, slot_k[5], wg.rearrange("(k p) n -> p k n", p=P)[:, :, bass.ds(f * BLK, BLK)])
                sp.wait_ge(up_mm, f * QB)
                load(0, slot_k[0], wu.rearrange("(k p) n -> p k n", p=P)[:, :, bass.ds(f * BLK, BLK)])
            sp.wait_ge(up_mm, FB * QB)
            load(0, slot_k[0], cols(rwkv_w_k[0], 0))
            for r in range(4):
                sp.wait_ge(down_mm, r + 1)
                load(1 + r, dk[r], wd_v[r, :, :, BLK:D])
            sp.wait_ge(down_mm, 5)
            load(1, slot_k[1], cols(rwkv_w_k[0], 1))
            sp.wait_ge(down_mm, 6)
            for off, w in ((0, rwkv_w1), (KC * LORA, rwkv_a1), (2 * KC * LORA, rwkv_g1)):
                n = w.shape[2]
                sp.dma_start(slot[2][:, off:off + KC * n].rearrange("p (k n) -> p k n", k=KC),
                             w[0].rearrange("(k p) n -> p k n", p=P)).then_inc(slot_in[2], 16)
            sp.wait_ge(down_mm, 7)
            for rows, off, src in ((slice(0, 64), 0, rwkv_w2[0]), (slice(64, 128), 0, rwkv_a2[0]),
                                   (slice(0, 128), D, rwkv_g2[0, 0:P]), (slice(0, GLORA - P), 2 * D, rwkv_g2[0, P:GLORA])):
                sp.dma_start(slot[3][rows, off:off + D], src).then_inc(slot_in[3], 16)
            for s, w, n, s_, used in ((0, rwkv_w_r, 0, pr_mm, 4), (1, rwkv_w_r, 1, pr_mm, 8), (2, rwkv_w_v, 0, mix_used, 3),
                                      (3, rwkv_w_v, 1, l2_mm, 24), (0, rwkv_w_o, 0, pr_mm, 12), (1, rwkv_w_o, 1, pr_mm, 16)):
                sp.wait_ge(s_, used)
                load(s, slot_k[s], cols(w[0], n))
            we_g = moe_w_gate[0].rearrange("e (k p) n -> e p k n", p=P)
            we_u = moe_w_up[0].rearrange("e (k p) n -> e p k n", p=P)
            we_d = moe_w_down[0].rearrange("e (f k p) n -> e f p k n", p=P, k=QB)

            def expert_tiles(i, it, a, b):
                for m in range(a, b):
                    (kind, q), h = TILES[m // 2], m % 2
                    e, f = 2 * i + q // FB, q % FB
                    sp.wait_ge(w_lo, it * NHALF + (m + 1))
                    if kind < 2:
                        dst = raw_w[:, m % NRAW, :].rearrange("p (k n) -> p k n", k=KC // 2)
                        src = (we_g, we_u)[kind][e, :, h * (KC // 2):(h + 1) * (KC // 2), f * BLK:(f + 1) * BLK]
                    else:
                        dst = raw_w[:, m % NRAW, :].rearrange("p (k n) -> p k n", k=QB // 2)
                        src = we_d[e, f, :, h * (QB // 2):(h + 1) * (QB // 2), :]
                    sp.dma_start(dst, src).then_inc(raw_in[m % NRAW], 16)

            sp.wait_ge(ot_ev, 4 * (NCH - 1) + 1)
            sp.dma_start(gainrow, ffn_norm[1:2, :].to_broadcast([P, D])).then_inc(ld_gain, 16)
            with sp.Fori(0, TURNS) as i:
                expert_tiles(i, i, 0, NHALF)
            expert_tiles(0, TURNS, 0, AHEAD)
            sp.wait_ge(npass_ok, 1)
            n = sp.value_load(npass_i[0:1, 0:1], min_val=1, max_val=2)
            with sp.If(n > 1):
                expert_tiles(0, TURNS, AHEAD, NHALF)
                with sp.Fori(1, TURNS) as i:
                    expert_tiles(i, i + TURNS, 0, NHALF)
                expert_tiles(0, 2 * TURNS, 0, AHEAD)
            sp.wait_ge(acc_done, 1)
            sp.dma_start(out[0].rearrange("(t p) d -> p t d", p=P), acc).then_inc(out_sem, 16)
            sp.wait_ge(out_sem, 16)

        @block.gpsimd
        def _(pool):
            g = nc.gpsimd
            own = Own(pool)

            def one(ins, s_=pool_own):
                own.done(ins, s_)
                own.settle()

            def keep(v, pattern, base, mult, op=ALU.is_ge, fill=0.0):
                one(g.affine_select(out=v, in_=v, pattern=pattern, compare_op=op, fill=fill, base=base,
                                    channel_multiplier=mult))

            def fill(v, value):
                one(g.memset(v, value))

            fill(ident[:, :], 0.0)
            one(g.affine_select(out=ident[:, :], in_=ident[:, :], pattern=[[-1, P]], compare_op=ALU.not_equal, fill=1.0,
                                base=0, channel_multiplier=1), ident_ok)
            fill(ones[:, :], 1.0)
            fill(uT[:, :, 0:1], 0.0)
            fill(attmask[:, :], 0.0)
            keep(attmask[:, META:META + P], [[-1, P]], 0, 1, fill=NEG)
            a = SEG[1][0] + META
            keep(attmask[:, a:a + P], [[1, P]], -1, -1, fill=NEG)
            keep(attmask[:, a + P:a + 2 * P], [[-1, P]], 0, 1, fill=NEG)
            keep(attmask[:, SEG[2][0]:NSC], [[-1, META]], 0, 1, fill=NEG)
            fill(headones[:, :], 1.0)
            hv = headones[:, :].rearrange("p (h i) -> p h i", h=2)
            keep(hv, [[-CH, 2], [0, CH]], 0, 1)
            keep(hv, [[CH, 2], [0, CH]], CH - 1, -1)
            for j in range(2):
                v = causal[:, j, :].rearrange("p (h i) -> p h i", h=2)
                fill(v, 1.0)
                keep(v, [[-CH, 2], [0, CH]], 0, 1)
                keep(v, [[CH, 2], [1, CH]], j - 1, -1)
            fill(levelmask[:, :, :], 0.0)
            for l in range(2, 7):
                b = 1 << (l - 1)
                v = levelmask[:, l - 2, :].rearrange("p (j x i) -> p j x i", x=2, i=b)[:, :, 0, :]
                fill(v, 1.0)
                keep(v, [[-2 * b, P // (2 * b)], [0, b]], -b, 1)
                keep(v, [[2 * b, P // (2 * b)], [0, b]], 2 * b - 1, -1)
            fill(level1T[:, :], 0.0)
            v = level1T[:, :].rearrange("p (j x) -> p j x", x=2)[:, :, 1]
            fill(v, 1.0)
            keep(v, [[-2, P // 2]], 0, 1, op=ALU.is_equal)
            fill(reset[:, :], 1.0)
            fill(reset[:, :].rearrange("p (c i) -> p c i", c=NCH)[:, :, 0], 0.0)
            fill(before[:, :], 1.0)
            keep(before[:, :], [[1, P]], -1, -1)
            for v, pattern, base in ((slotno[:, :], [[1, P]], 0), (expno[:, :, :], [[0, 2], [1, EXPERTS]], 0)):
                one(g.iota(v, pattern=pattern, base=base, channel_multiplier=0, allow_small_or_imprecise_dtypes=True))
            one(g.iota(expno8[:, :, :], pattern=[[0, 2], [1, EXPERTS]], base=EXPERTS, channel_multiplier=0,
                       allow_small_or_imprecise_dtypes=True), consts_ok)
            pool.wait_ge(in_x, 4)
            pool.wait_ge(in_rest, 2)
            one(g.memset(kz[:, :, :, :], 0.0), kz_zero)
            pool.wait_ge(slot_in[2], 16)
            for h in range(2):
                one(g.tensor_copy(wkdup[:, :, :, h, :], slot_k[2][:, :, 0:256].rearrange("p k (g d) -> p k g d", g=KVH)), kw_ok)
            pool.wait_ge(norm_u, 3 * KC)
            for arr in (r_a, kk_a, k_a, b_a, v_a, w_a):
                fill(arr[:, :, 0:PAD], 0.0)
            fill(th_w[HD:P, :], 0.0)
            fill(th_a[0:HD, :], 0.0)
            for lo in (32, 64, 96):
                fill(sg_b[lo:lo + 32, :], 0.0)
            pool.wait_ge(down_mm, 7)
            for lo in (32, 64, 96):
                one(g.memset(slot[3][lo:lo + 32, 2 * D:3 * D], 0.0), pads_zero)
            pool.wait_ge(l2_mm, 24)
            one(g.memset(Bt[:, :, :], 0.0), work_zero)
            pool.wait_ge(mix_ok, 5)
            for v in (Kt[:, :, :], Vt[:, :, :]):
                one(g.memset(v, 0.0), work_zero)
            pool.wait_ge(pr_mm, 16)
            one(g.memset(ARt[:, :, :, :], 0.0), work_zero)

            def blocks(c, n):
                dst, src = ((Kt, k_a), (Vt, v_a))[n]
                for h in range(2):
                    rows = slice(h * CH, (h + 1) * CH)
                    g.tensor_copy(dst[rows, :, rows], src[rows, :, bass.ds(c * CH, CH)]).then_inc(bd_kv, 1)
                    pool.wait_ge(bd_kv, c * 4 + (2 * n + h + 1))

            pool.wait_ge(dec_done, PAIRS)
            blocks(0, 0)
            pool.wait_ge(pr_ev, 24)
            blocks(0, 1)
            with pool.Fori(1, NCH) as c:
                pool.wait_ge(tr_mm, 6 * c)
                blocks(c, 0)
                blocks(c, 1)

        @block.tensor
        def _(pe):
            mm, tr = nc.tensor.matmul, nc.tensor.transpose

            pe.wait_ge(ident_ok, 1)
            for t in range(2):
                pe.wait_ge(ld_x[t], 16)
                for half in range(2):
                    for c in range(4):
                        k = half * 4 + c
                        last = tr(ps[:, 2 * t + half, c * P:(c + 1) * P], xtok[:, t, k * P:(k + 1) * P], ident[:, :])
                    last.then_inc(in_tr, 1)
            pe.wait_ge(ld_meta, 16)
            for k in range(KC):
                last = tr(ps[:, 4, k * META:(k + 1) * META], mtok[0:META, k * P:(k + 1) * P], ident[0:META, 0:META])
            last.then_inc(in_tr, 1)
            pe.wait_ge(ld_par, 160)
            for k in range(KC):
                last = tr(ps[:, 5, k * NROW:(k + 1) * NROW], prow[0:NROW, k * P:(k + 1) * P], ident[0:NROW, 0:NROW])
            last.then_inc(in_tr, 1)
            def sum_sq(n, k):
                pe.wait_ge(norm_sq, (n - 1) * KC + k + 1)
                last = mm(ps[:, 7 if n < 3 else 0, 0:T], ones[:, :], sq[:, k, :], start=(k == 0), stop=(k == KC - 1))
                if k == KC - 1:
                    last.then_inc(norm_ss, 1)

            pe.wait_ge(pool_own, 2)
            for k in range(KC):
                sum_sq(1, k)
            pe.wait_ge(ld_small, 16 * 5)
            mm(ps[:, 6, 0:HEADS], ones[0:1, :], sinkrow[:, :], start=True, stop=True).then_inc(in_tr, 1)

            pe.wait_ge(consts_ok, 1)

            def head_ss(i):
                pe.wait_ge(qk_sq, i + 1)
                if i >= 2:
                    pe.wait_ge(qk_std, i - 1)
                mm(ps[:, 3 + i % 2, 0:T], headones[:, :], rsq[:, i % 2, :], start=True, stop=True).then_inc(qk_ss, 1)

            for i, m in enumerate(QK):
                if m in (0, 4, 8):
                    pe.wait_ge(slot_in[m // 4], 16)
                if m == KC:
                    pe.wait_ge(kw_ok, 2)
                if i >= 3:
                    pe.wait_ge(qk_sq, i - 2)
                for k in range(KC):
                    if i == 0:
                        pe.wait_ge(norm_u, k + 1)
                    if m < KC:
                        w = slot_k[m // 4][:, k, (m % 4) * P:(m % 4 + 1) * P]
                    else:
                        w = wkdup[:, k, m - KC, :, :].rearrange("p a b -> p (a b)")
                    last = mm(ps[:, i % 3, 0:T], w, uT[:, k, 1:T + 1], start=(k == 0), stop=(k == KC - 1))
                last.then_inc(qk_mm, 1)
                if i >= 1:
                    head_ss(i - 1)

            def values(t):
                n = P if t < 2 else META
                for k in range(KC):
                    last = mm(ps[0:n, 5 + t, 0:256], uT[:, k, 1 + t * P:1 + t * P + n], slot_k[2][:, k, 256:512],
                              start=(k == 0), stop=(k == KC - 1))
                last.then_inc(v_mm, 1)

            def score(c):
                g = c // 2
                pe.wait_ge(qk_n, 8 if c < 4 else 12)
                if c >= 1:
                    pe.wait_ge(sc_rd, c)
                mm(ps[:, 0, 0:2 * (META + P)], qT[:, c, META:META + P], kz[:, g, :, 0:META + P], start=True, stop=True)
                mm(ps[0:META, 0, 288:288 + 2 * META], qT[:, c, 0:META], kz[:, g, :, 0:META], start=True, stop=True)
                for h in range(2):
                    last = mm(ps[:, 1 + h, 0:T], qT[:, c, META + P:T], kz[:, g, h, :], start=True, stop=True)
                last.then_inc(sc_mm, 1)

            values(0)
            pe.wait_ge(qk_sq, KC + KVH)
            score(0)
            head_ss(KC + KVH - 1)
            values(1)
            score(1)
            values(2)
            pe.wait_ge(v_cp, 3)
            pe.wait_ge(qk_std, 12)
            for c in range(PAIRS):
                g, b = c // 2, c % 2
                pe.wait_ge(p_ok, c + 1)
                if c >= 1:
                    pe.wait_ge(pt_a, c)
                    pe.wait_ge(pt_d, c)
                for h in range(2):
                    p1, p2, p0 = [scores[:, b, h, o:o + n] for o, n in SEG]
                    hs = slice(h * P, (h + 1) * P)
                    tr(ps[:, 3, h * P:h * P + P], p1[:, 0:P], ident[:, :])
                    tr(ps[:, 3, 256 + h * P:256 + h * P + P], p2[:, 0:P], ident[:, :])
                    tr(ps[:, 4, h * P:h * P + P], p2[:, P:2 * P], ident[:, :])
                    tr(ps[0:META, 5, h * P:h * P + P], p1[:, P:P + META], ident[:, :])
                    tr(ps[0:META, 5, 256 + h * P:256 + h * P + P], p2[:, 2 * P:T], ident[:, :])
                    last = tr(ps[0:META, 4, 256 + h * META:256 + (h + 1) * META], p0[0:META, :], ident[0:META, 0:META])
                last.then_inc(pt_mm, 1)
                if c + 2 < PAIRS:
                    score(c + 2)
                pe.wait_ge(pt_a, c + 1)
                pe.wait_ge(pt_d, c + 1)
                if c >= 1:
                    pe.wait_ge(o_cp, c)
                pt = pT[:, b, :]
                mm(ps[:, 6, 0:256], vdup[:, 0, g, :], pt[:, 0:256], start=True, stop=False)
                mm(ps[:, 6, 0:256], vdup[0:META, 1, g, :], pt[0:META, 768:1024], start=False, stop=True)
                mm(ps[:, 6, 256:512], vdup[:, 0, g, :], pt[:, 256:512], start=True, stop=False)
                mm(ps[:, 6, 256:512], vdup[:, 1, g, :], pt[:, 512:768], start=False, stop=False)
                mm(ps[:, 6, 256:512], vdup[0:META, 2, g, :], pt[0:META, 1024:1280], start=False, stop=True)
                mm(ps[:, 7, 0:2 * META], vdup[0:META, 0, g, :], pt[0:META, 1280:1312], start=True, stop=True)\
                    .then_inc(pv_mm, 1)

            pe.wait_ge(o_cp, PAIRS)
            for m in range(KC):
                if m in (0, 4):
                    pe.wait_ge(slot_in[3 + m // 4], 16)
                if m >= 4:
                    pe.wait_ge(wo_add, m - 3)
                for k in range(KC):
                    last = mm(ps[:, m % 4, 0:T], slot_k[3 + m // 4][:, k, (m % 4) * P:(m % 4 + 1) * P], oT[:, k, :],
                              start=(k == 0), stop=(k == KC - 1))
                last.then_inc(wo_mm, 1)
                if m >= 1:
                    sum_sq(2, m - 1)
            sum_sq(2, KC - 1)

            with pe.Fori(0, FB) as f:
                for s, b0, made, free, loads in ((5, 0, gate_mm, ffn_silu, 1), (0, 4, up_mm, ffn_mul, 2)):
                    pe.wait_ge(slot_in[s], f * 16 + 16 * loads)
                    for q in range(QB):
                        pe.wait_ge(free, f * QB + (q + 1))
                        for k in range(KC):
                            if s == 5 and q == 0:
                                pe.wait_ge(norm_u, KC + k + 1)
                            last = mm(ps[:, b0 + q, 0:T], slot_k[s][:, k, q * P:(q + 1) * P], uT[:, k, 1:T + 1],
                                      start=(k == 0), stop=(k == KC - 1))
                        last.then_inc(made, 1)
            pe.wait_ge(ffn_mul, QB + FB * QB)
            for hf in range(2):
                for r in range(4):
                    pe.wait_ge(slot_in[1 + r], hf * 16 + 32)
                    kq = [(k, q) for k in range(FB) for q in range(QB)]
                    if r == 3:
                        kq = [(k, q) for q in range(QB) for k in range(FB)]
                    for k, q in kq:
                        last = mm(ps[:, 4 * hf + q, 0:T], slot_k[1 + r][:, k, q * P:(q + 1) * P], hid[:, r * FB + k, :],
                                  start=(r + k == 0), stop=(r == 3 and k == FB - 1))
                        if r == 3 and k == FB - 1:
                            last.then_inc(down_q, 1)
                            if q == QB - 1:
                                pe.wait_ge(down_q, hf * QB + QB)
                                pe.sem_inc(down_mm, 1)
                    if r < 3:
                        last.then_inc(down_mm, 1)
            for k in range(KC):
                sum_sq(3, k)

            def project(j):
                which, m = j // KC, j % KC
                s = (0, 0, 2)[which] + m // 4
                if m == 0 and which:
                    pe.wait_ge(mix_ok, 3 + which)
                if m % 4 == 0:
                    pe.wait_ge(slot_in[s], 16 * {0: 9, 1: 4, 2: 7, 3: 8}[s] + (16 if which == 1 else 0))
                if j >= 4:
                    pe.wait_ge(pr_ev, j - 3)
                for k in range(KC):
                    if j == 0:
                        pe.wait_ge(mixk_ok, k + 1)
                    last = mm(ps[:, j % 4, 0:T], slot_k[s][:, k, (m % 4) * P:(m % 4 + 1) * P], xm[which // 2][:, k, :],
                              start=(k == 0), stop=(k == KC - 1))
                last.then_inc(pr_mm, 1)

            def per_head(m, src, ready, made, read):
                pe.wait_ge(ready, m + 1)
                if m >= 4:
                    pe.wait_ge(read, m - 3)
                mm(ps[:, 4 + m % 4, 0:T], headones[:, :], src[:, m, PAD:TP], start=True, stop=True).then_inc(made, 1)

            for j in range(KC):
                project(j)
            l1 = [slot[2][:, o:o + KC * n].rearrange("p (k n) -> p k n", k=KC)
                  for o, n in ((0, LORA), (KC * LORA, LORA), (2 * KC * LORA, GLORA))]
            pe.wait_ge(slot_in[2], 16 * 6)
            pe.wait_ge(mix_ok, 1)
            pe.wait_ge(pr_ev, 5)
            for k in range(KC):
                last = mm(ps[0:LORA, 0, 0:T], l1[0][:, k, :], xm[1][:, k, :], start=(k == 0), stop=(k == KC - 1))
            last.then_inc(mix_used, 1)
            for m in range(4):
                per_head(m, v_a, kk_sq, kk_ss, kk_ev)
            pe.wait_ge(mix_ok, 2)
            pe.wait_ge(pr_ev, 8)
            for k in range(KC):
                last = mm(ps[HD:P, 1, 0:T], l1[1][:, k, :], xm[0][:, k, :], start=(k == 0), stop=(k == KC - 1))
            last.then_inc(mix_used, 1)
            for m in range(4, PAIRS):
                per_head(m, v_a, kk_sq, kk_ss, kk_ev)
            pe.wait_ge(mix_ok, 3)
            for k in range(KC):
                mm(ps[:, 2, 0:T], l1[2][:, k, 0:P], xm[1][:, k, :], start=(k == 0), stop=(k == KC - 1))
            for k in range(KC):
                last = mm(ps[0:GLORA - P, 3, 0:T], l1[2][:, k, P:GLORA], xm[1][:, k, :], start=(k == 0), stop=(k == KC - 1))
            last.then_inc(mix_used, 1)
            pe.wait_ge(slot_in[3], 16 * 7)
            pe.wait_ge(pads_zero, 3)
            pe.wait_ge(kk_ev, KC)
            for j in range(3 * KC):
                which, m = j // KC, j % KC
                if m == 0:
                    pe.wait_ge(lora_h, (1, 2, 4)[which])
                if j >= 4:
                    pe.wait_ge(l2_ev, j - 3)
                bank = ps[:, 4 + j % 4, 0:T]
                cs = slice(m * P, (m + 1) * P)
                if which < 2:
                    last = mm(bank, slot[3][:, cs], (th_w, th_a)[which], start=True, stop=True)
                else:
                    mm(bank, slot[3][:, D + m * P:D + (m + 1) * P], sg_a, start=True, stop=False)
                    last = mm(bank, slot[3][:, 2 * D + m * P:2 * D + (m + 1) * P], sg_b, start=False, stop=True)
                last.then_inc(l2_mm, 1)
            pe.wait_ge(lora_h, 4)
            for j in range(KC, 3 * KC):
                project(j)
                if 12 <= j < 20:
                    if j == 12:
                        pe.wait_ge(l2_ev, 24)
                    per_head(j - 12, v_a, rk_ok, rk_mm, rk_ev)

            pe.wait_ge(work_zero, 4)
            pe.wait_ge(pr_ev, 24)
            pe.wait_ge(rk_ev, PAIRS)

            def chunk(c, first=False, last_=False):
                n = 128 if first else 256
                less = {k: 0 if first else v for k, v in LESS.items()}
                pe.wait_ge(bd_ar, c + 1)
                pe.wait_ge(bd_b, c + 1)
                if not first:
                    pe.wait_ge(ot_ev, c * 4 + (1 - 4))
                for h in range(2):
                    for p in range(4):
                        o = (p % 2) * 256
                        last = mm(ps[:, 4 * h + p // 2, o:o + n], Bt[:, 4 * h + p, :],
                                  ARt[:, 4 * h + p, :, :].rearrange("p a b -> p (a b)")[:, 0:n], start=True, stop=True)
                    last.then_inc(ap_mm, 1)
                pe.wait_ge(bd_kv, c * 4 + 2)
                if not first:
                    pe.wait_ge(s_ok, c * 2)
                for h in range(2):
                    for p in range(4):
                        o = (p % 2) * 256
                        last = mm(ps[:, 4 * h + 2 + p // 2, o:o + n], Kt[:, 4 * h + p, :],
                                  ARt[:, 4 * h + p, :, :].rearrange("p a b -> p (a b)")[:, 0:n], start=True, stop=True)
                    last.then_inc(ap_mm, 1)
                for j, src in enumerate((Bt, Kt, Vt)):
                    for h in range(2):
                        if last_ and j < 2:
                            continue
                        pe.wait_ge(ap_ev, c * 4 + (1 + h if j < 2 else 3 + h))
                        if j == 2:
                            pe.wait_ge(bd_kv, c * 4 + 4)
                        for p in range(4):
                            last = tr(ps[:, 4 * h + j, p * P:(p + 1) * P], src[:, 4 * h + p, :], ident[:, :])
                        last.then_inc(tr_mm, 1)
                for h in range(2):
                    pe.wait_ge(tr_ev, c * 6 + ((1 if last_ else 5) + h))
                    for p in range(4 * h, 4 * h + 4):
                        o = ps[:, 4 * h + 1, (p % 4) * P:(p % 4 + 1) * P]
                        if not first:
                            mm(o, ARt[:, p, 0, :], S[:, p, :], start=True, stop=False)
                        last = mm(o, KA[:, p, 0, :], Vs[:, p, :], start=first, stop=True)
                    last.then_inc(rhs_mm, 1)
                levels = NLV0 if first else NLV
                for l in range(levels):
                    for h in range(2):
                        pe.wait_ge(x_ok, c * 12 + (2 * l + h + 1 - less["x"]))
                        for p in range(4 * h, 4 * h + 4):
                            last = mm(ps[:, 4 * h + 3, (p % 4) * P:(p % 4 + 1) * P], NA[:, p, 0, :], X[:, p, :],
                                      start=True, stop=True)
                        last.then_inc(y_mm, 1)
                    for h in range(2):
                        pe.wait_ge(y_ev, c * 10 + (2 * l + h + 1 - less["y"]))
                        for p in range(4 * h, 4 * h + 4):
                            o = ps[:, 4 * h, (p % 4) * P:(p % 4 + 1) * P]
                            if l < levels - 1:
                                last = mm(o, XT[:, p, :], Y[:, p, :], start=True, stop=True)
                            else:
                                last = mm(o, Y[:, p, :], XT[:, p, :], start=True, stop=True)
                        last.then_inc(x_mm, 1)
                for h in range(2):
                    pe.wait_ge(x_ok, c * 12 + (2 * levels + h + 1 - less["x"]))
                    pe.wait_ge(rhs_ev, c * 2 + (h + 1))
                    for p in range(4 * h, 4 * h + 4):
                        last = mm(ps[:, 4 * h + 2, (p % 4) * P:(p % 4 + 1) * P], XT[:, p, :], RHS[:, p, :], start=True, stop=True)
                    last.then_inc(u_mm, 1)
                for h in range(2):
                    pe.wait_ge(u_ev, c * 2 + (h + 1))
                    if first:
                        continue
                    for p in range(4 * h, 4 * h + 4):
                        o = ps[:, 4 * h + 1, (p % 4) * P:(p % 4 + 1) * P]
                        mm(o, S[:, p, :], ARt[:, p, 1, :], start=True, stop=False)
                        mm(o, U[:, p, :], NA[:, p, 1, :], start=False, stop=False)
                        last = mm(o, Vs[:, p, :], KA[:, p, 1, :], start=False, stop=True)
                    last.then_inc(ot_mm, 1)
                if not last_:
                    for h in range(2):
                        for p in range(4 * h, 4 * h + 4):
                            o = ps[:, 4 * h + 3, (p % 4) * P:(p % 4 + 1) * P]
                            mm(o, Bs[:, p, :], U[:, p, :], start=True, stop=False)
                            last = mm(o, Ks[:, p, :], Vs[:, p, :], start=False, stop=True)
                        last.then_inc(s_mm, 1)

            chunk(0, first=True)
            with pe.Fori(1, NCH - 1) as c:
                chunk(c)
            chunk(NCH - 1, last_=True)

            pe.wait_ge(ot_ev, 4 * (NCH - 1) + 1)
            for t in range(2):
                for half in range(2):
                    for q in range(4):
                        k = 4 * half + q
                        last = tr(ps[:, 2 * t + half, q * P:(q + 1) * P], hT[:, k, META + t * P:META + (t + 1) * P], ident[:, :])
                    last.then_inc(ht_mm, 1)
            for m in range(PAIRS):
                if m >= 4:
                    pe.wait_ge(gn_x, m - 3)
                mm(ps[:, 4 + m % 4, 0:SEQ], headones[:, :], w_a[:, m, CH:TP], start=True, stop=True).then_inc(gn_mm, 1)
            pe.wait_ge(ht_cp, 4)
            for m in range(PAIRS):
                pe.wait_ge(gn_sqd, m + 1)
                if m >= 4:
                    pe.wait_ge(gn_sd, m - 3)
                mm(ps[:, m % 4, 0:SEQ], headones[:, :], gn_sq[:, m, :], start=True, stop=True).then_inc(gn_var, 1)

            pe.wait_ge(gn_sd, PAIRS)
            pe.wait_ge(slot_in[0], 16 * 11)
            pe.wait_ge(slot_in[1], 16 * 6)
            for k in range(KC):
                pe.wait_ge(y_ok, k + 1)
                for t in range(2):
                    for n in range(2):
                        last = mm(ps[:, 2 * t + n, :], w_a[:, k, CH + t * P:CH + (t + 1) * P], slot_k[n][:, k, :],
                                  start=(k == 0), stop=(k == KC - 1))
                        if k == KC - 1:
                            last.then_inc(wo2_mm, 1)

            pe.wait_ge(gn_x, PAIRS)
            for n in range(4):
                t, half = n // 2, n % 2
                pe.wait_ge(utok_ok, n + 1)
                for q in range(4):
                    k = 4 * half + q
                    last = tr(ps[:, 4 + n, q * P:(q + 1) * P], utok[:, t, k * P:(k + 1) * P], ident[:, :])
                last.then_inc(utT_mm, 1)
            pe.wait_ge(ld_router, 16)
            pe.wait_ge(acc_ok, 4)
            for t in range(2):
                for k in range(KC):
                    if k % 4 == 0:
                        pe.wait_ge(utT_cp, 2 * t + k // 4 + 1)
                    last = mm(ps[:, 0, t * EXPERTS:(t + 1) * EXPERTS], utT[:, k, t * P:(t + 1) * P], router[:, k, :],
                              start=(k == 0), stop=(k == KC - 1))
            last.then_inc(lg_mm, 1)
            chosen = route[:, 0, :, 0:EXPERTS]
            pe.wait_ge(mask_ok, 1)
            mm(ps[:, 1, 0:8], before[:, :], chosen[:, 0, :], start=True, stop=True)
            mm(ps[:, 1, 8:16], ones[:, :], chosen[:, 0, :], start=True, stop=False)
            mm(ps[:, 1, 8:16], before[:, :], chosen[:, 1, :], start=False, stop=True)
            mm(ps[:, 1, 16:24], ones[:, :], chosen[:, 0, :], start=True, stop=False)
            mm(ps[:, 1, 16:24], ones[:, :], chosen[:, 1, :], start=False, stop=True).then_inc(rank_mm, 1)

            pe.sem_inc(w_used, NRING)
            pe.wait_ge(npass_ok, 1)
            n = pe.value_load(npass_i[0:1, 0:1], min_val=1, max_val=2)

            def gather(j, sels, b5, b4):
                pe.wait_ge(sel_ok, sels)
                for half in range(2):
                    pe.wait_ge((es_add, et_ev)[half], (b5, b4)[half])
                    for q in range(4):
                        k = 4 * half + q
                        for t in range(2):
                            last = mm(ps[:, 5 - half, q * P:(q + 1) * P], utok[:, t, k * P:(k + 1) * P],
                                      sel[:, j, t, :], start=(t == 0), stop=(t == 1))
                    last.then_inc(xg_mm, 1)

            def sel_tr(j, read):
                pe.wait_ge(xg_ev, read)
                for t in range(2):
                    last = tr(ps[:, 5, t * P:(t + 1) * P], selg[:, j, t, :], ident[:, :])
                last.then_inc(st_mm, 1)

            def scatter(j, o, added):
                pe.wait_ge(es_add, added)
                t, n_ = o // 2, o % 2
                mm(ps[:, 5, :], selT[:, j, t, :], ye[:, n_ * BLK:(n_ + 1) * BLK], start=True, stop=True).then_inc(es_mm, 1)

            with pe.Fori(0, n) as pas:
                first = pas * TURNS
                gather(0, first * 2 + pas + 1, pas * (8 * TURNS + 4) + 1, first * NB2 + 1)
                sel_tr(0, first * 4 + pas * 2 + 2)
                with pe.Fori(0, TURNS) as i:
                    it = pas * TURNS + i
                    tables = it * 2 + pas
                    adds = it * 8 + pas * 4

                    def half_tile(m, k):
                        pe.wait_ge(w_lo, it * NHALF + (m + NRAW + 1))
                        return [wsplit[:, m % NRING, part, :].rearrange("p (k n) -> p k n", k=k) for part in range(2)]

                    def split_mm(o, x_, w_, first_, last_):
                        mm(o, x_[0], w_[0], start=first_, stop=False)
                        mm(o, x_[0], w_[1], start=False, stop=False)
                        return mm(o, x_[1], w_[0], start=False, stop=last_)

                    def gate_up(q, kind):
                        j, m = q // FB, 2 * TILES.index((kind, q))
                        if q % FB == 0 and kind == 0:
                            pe.wait_ge(xg_ev, tables * 2 + (2 * j + 2))
                        pe.wait_ge((e_silu, e_h)[kind], it * NB2 + (q + 1))
                        for h in range(2):
                            whi, wlo = half_tile(m + h, KC // 2)
                            for kk in range(KC // 2):
                                k = h * (KC // 2) + kk
                                last = split_mm(ps[:, 2 * kind + q % 2, :], (xsplit[:, j, 0, k, :], xsplit[:, j, 1, k, :]),
                                                (whi[:, kk, :], wlo[:, kk, :]), k == 0, k == KC - 1)
                            last.then_inc(w_used, 1)

                    def hidden_tr(q):
                        pe.wait_ge(e_h, it * NB2 + (q + 3))
                        pe.wait_ge(et_ev, it * NB2 + (q + 1))
                        if q in (0, XQ):
                            pe.wait_ge(xg_ev, tables * 2 + (2 if q == 0 else 4))
                        for k in range(QB):
                            last = tr(ps[:, 4, k * P:(k + 1) * P], hbuf[:, q % 2, k * P:(k + 1) * P], ident[:, :])
                        last.then_inc(et_mm, 1)

                    def down(q):
                        f, m = q % FB, 2 * TILES.index((2, q))
                        pe.wait_ge(et_ev, it * NB2 + (q + 2))
                        if f == 0:
                            pe.wait_ge(ye_ev, it * 2 + (q // FB + 1))
                        for h in range(2):
                            whi, wlo = half_tile(m + h, QB // 2)
                            for kk in range(QB // 2):
                                k = h * (QB // 2) + kk
                                for n_ in range(2):
                                    cs = slice(n_ * BLK, (n_ + 1) * BLK)
                                    last = split_mm(ps[:, 6 + n_, :], (hsplit[:, q % 2, 0, k, :], hsplit[:, q % 2, 1, k, :]),
                                                    (whi[:, kk, cs], wlo[:, kk, cs]), f + k == 0, f == FB - 1 and k == QB - 1)
                            last.then_inc(w_used, 1)

                    for q in range(NB2):
                        gate_up(q, 0)
                        if q == XQ + 1:
                            sel_tr(1, tables * 2 + 3)
                        if q in LATE:
                            j, o, n_ = LATE[q]
                            if o == 0:
                                pe.wait_ge(ye_ev, it * 2 + (2 - j))
                                pe.wait_ge(st_ev, tables + (2 - j))
                            scatter(j, o, adds + (n_ + 1))
                        if q:
                            hidden_tr(q - 1)
                        gate_up(q, 1)
                        if q in LATE:
                            scatter(j, o + 1, adds + (n_ + 2))
                        if q:
                            down(q - 1)
                        if q == XQ:
                            gather(1, tables + 2, adds + 5, it * NB2 + (q + 1))
                    hidden_tr(NB2 - 1)
                    gather(0, tables + 3, adds + 9, it * NB2 + (NB2 + 1))
                    down(NB2 - 1)
                    sel_tr(0, tables * 2 + 5)
                turns = pas * TURNS + TURNS
                pe.wait_ge(ye_ev, turns * 2 + 1)
                pe.wait_ge(st_ev, turns * 2 + pas + 1)
                for o in range(4):
                    scatter(1, o, turns * 8 + pas * 4 + (o + 1))

        @block.scalar
        def _(act):
            A = nc.scalar.activation
            own = Own(act)
            act.dma_start(mtok[0:META, :], meta_tokens[:, :]).then_inc(ld_meta, 16)
            for row, src in ((R_MIXN, mixer_norm), (R_FFNN, ffn_norm), (R_MIX, rwkv_mix[0]), (R_W0, rwkv_w0),
                             (R_A0, rwkv_a0), (R_KK, rwkv_k_k), (R_KA, rwkv_k_a),
                             (R_RK, rwkv_r_k.rearrange("o h n -> o (h n)")), (R_GNW, rwkv_gn_w), (R_GNB, rwkv_gn_b)):
                act.dma_start(prow[row:row + src.shape[0], :], src).then_inc(ld_par, 16)
            for half in range(2):
                rows = slice(half * HD, (half + 1) * HD)
                act.dma_start(qgain[rows, :], attn_q_norm.rearrange("o (n u) -> (o n) u", u=1)).then_inc(ld_small, 16)
                act.dma_start(kgain[rows, :], attn_k_norm.rearrange("o (n u) -> (o n) u", u=1)).then_inc(ld_small, 16)
            act.dma_start(sinkrow[:, :], attn_sinks[:, :]).then_inc(ld_small, 16)
            for t in range(2):
                for half in range(2):
                    b = 2 * t + half
                    act.wait_ge(in_tr, b + 1)
                    own.done(A(hT[:, 4 * half:4 * half + 4, META + t * P:META + (t + 1) * P],
                               ps[:, b, :].rearrange("p (a b) -> p a b", a=4), ACT.Copy), in_x)

            def norm(n):
                if n == 1:
                    act.wait_ge(in_rest, 1)
                    own.settle()
                for k in range(KC):
                    if n > 1:
                        act.wait_ge((wo_add, down_add)[n - 2], k + 1)
                    own.done(A(sq[:, k, :], hT[:, k, :], ACT.Square), norm_sq)
                act.wait_ge(norm_ss, n)
                own.done(A(std, ps[:, 7 if n < 3 else 0, 0:T], ACT.Sqrt, bias=epsD, scale=1.0 / D), norm_std)

            epsD, eps_q, eps_k, eps_gn = [normcol[:, 0, 0:1], normcol[:, 0, 1:2], normcol[:, 0, 0:1], normcol[:, 1, 0:1]]
            act.wait_ge(dve_own, 5)
            norm(1)

            def head_std(i):
                act.wait_ge(qk_ss, i + 1)
                if i >= 2:
                    act.wait_ge(qk_n, i - 1)
                b = ps[:, 3 + i % 2, 0:T]
                if QK[i] < KC:
                    own.done(A(rstd2[:, i % 2, :], b, ACT.Sqrt, bias=eps_q), qk_std)
                else:
                    own.done(A(rstd2[:, i % 2, :], b, ACT.Sqrt, bias=eps_k, scale=1.0 / HD), qk_std)

            for i in range(KC + KVH):
                act.wait_ge(qk_mm, i + 1)
                if i >= 2:
                    act.wait_ge(qk_ss, i - 1)
                    act.wait_ge(qk_n, i - 1)
                A(raw[:, i % 2, :], ps[:, i % 3, 0:T], ACT.Copy)
                own.done(A(rsq[:, i % 2, :], ps[:, i % 3, 0:T], ACT.Square), qk_sq)
                if i >= 1:
                    head_std(i - 1)

            def values(t):
                n = P if t < 2 else META
                act.wait_ge(v_mm, t + 1)
                for half in range(2):
                    last = A(vdup[0:n, t, :, half * HD:(half + 1) * HD],
                             ps[0:n, 5 + t, 0:256].rearrange("p (g d) -> p g d", g=KVH), ACT.Copy)
                own.done(last, v_cp)

            values(0)
            head_std(KC + KVH - 1)

            def exps(c):
                b = c % 2
                act.wait_ge(sc_max, c + 1)
                for h in range(2):
                    for s_, (o, n) in enumerate(SEG):
                        v = scores[:, b, h, o:o + n]
                        A(v, v, ACT.Exp, bias=stat[:, b, 1, 3 * h + s_:3 * h + s_ + 1],
                          accum_out=stat[:, b, 2, 3 * h + s_:3 * h + s_ + 1])
                own.done(A(stat[:, b, 4, :], stat[:, b, 3, :], ACT.Exp), sc_exp)

            def probs_copy(c):
                act.wait_ge(pt_mm, c + 1)
                if c >= 2:
                    act.wait_ge(pv_mm, c - 1)
                own.done(A(pT[:, c % 2, 0:512], ps[:, 3, :], ACT.Copy), pt_a)

            def out_copy(c):
                act.wait_ge(pv_mm, c + 1)
                for h in range(2):
                    rows = slice(h * HD, (h + 1) * HD)
                    A(oT[rows, c, 0:META], ps[rows, 7, h * META:(h + 1) * META], ACT.Copy)
                    last = A(oT[rows, c, META:T].rearrange("p (b q) -> p b q", b=2),
                             ps[rows, 6, :].rearrange("p (b h q) -> p b h q", b=2, h=2)[:, :, h, :], ACT.Copy)
                own.done(last, o_cp)

            exps(0)
            values(1)
            values(2)
            exps(1)
            for c in range(PAIRS):
                probs_copy(c)
                if c + 2 < PAIRS:
                    exps(c + 2)
                out_copy(c)
            norm(2)

            act.sem_inc(ffn_silu, QB)
            with act.Fori(0, FB) as f:
                for q in range(QB):
                    act.wait_ge(gate_mm, f * QB + (q + 1))
                    act.wait_ge(ffn_mul, f * QB + (q + 1))
                    A(sgate[:, q, :], ps[:, q, 0:T], ACT.Silu).then_inc(ffn_silu, 1)
            norm(3)

            def take(j):
                which, m = j // KC, j % KC
                act.wait_ge(pr_mm, j + 1)
                if which == 2:
                    act.wait_ge(rk_mm, m + 1)
                own.done(A((k_a, r_a, v_a)[which][:, m, PAD:TP], ps[:, j % 4, 0:T], ACT.Copy), pr_ev)

            def square(m):
                act.wait_ge(kk_ok, m + 1)
                own.done(A(v_a[:, m, PAD:TP], kk_a[:, m, PAD:TP], ACT.Square), kk_sq)

            for j in range(KC):
                take(j)
                if j >= 1:
                    square(j - 1)
            square(KC - 1)
            act.wait_ge(pads_zero, 3)
            act.wait_ge(mix_used, 1)
            own.done(A(th_w[0:HD, :], ps[0:HD, 0, 0:T], ACT.Tanh), lora_h)
            act.wait_ge(mix_used, 2)
            own.done(A(th_a[HD:P, :], ps[HD:P, 1, 0:T], ACT.Copy), lora_h)
            act.wait_ge(kk_ev, PAIRS)
            own.done(A(r_a[:, :, PAD:TP], r_a[:, :, PAD:TP], ACT.Sqrt), kk_nrm)
            act.wait_ge(mix_used, 3)
            own.done(A(sg_a, ps[:, 2, 0:T], ACT.Sigmoid), lora_h)
            own.done(A(sg_b[0:GLORA - P, :], ps[0:GLORA - P, 3, 0:T], ACT.Sigmoid), lora_h)
            for j in range(3 * KC):
                which, m = j // KC, j % KC
                act.wait_ge(l2_mm, j + 1)
                bank = ps[:, 4 + j % 4, 0:T]
                if which == 0:
                    own.done(A(w_a[:, m, PAD:TP], bank, ACT.Sigmoid, bias=par[:, m, R_W0:R_W0 + 1]), l2_ev)
                elif which == 1:
                    own.done(A(b_a[:, m, PAD:TP], bank, ACT.Sigmoid, bias=par[:, m, R_A0:R_A0 + 1]), l2_ev)
                else:
                    own.done(A(g_a[:, m, :], bank[:, META:T], ACT.Copy), l2_ev)

            def decays(m):
                act.wait_ge(cum_ok, m + 1)
                if m >= 1:
                    act.wait_ge(dec_done, m)
                A(expo[:, 0, :], cum[:, m % 2, :], ACT.Exp, scale=-DECAY)
                A(expo[:, 1, :], cum[:, m % 2, :], ACT.Exp, scale=DECAY)
                own.done(A(expo[:, 2, :], w_a[:, m, :], ACT.Exp, scale=-DECAY), dec_exp)

            act.wait_ge(kk_done, 1)
            for j in range(KC, 3 * KC):
                take(j)
                if 10 <= j < 18:
                    decays(j - 10)
                if 13 <= j < 21:
                    act.wait_ge(rk_mm, j - 12)
                    own.done(A(bonus[:, j - 13, :], ps[:, 4 + (j - 13) % 4, META:T], ACT.Copy), rk_ev)

            act.wait_ge(work_zero, 4)
            act.wait_ge(dec_done, PAIRS)
            act.sem_inc(ot_ev, 1)

            def removals_b(c):
                for h in range(2):
                    rows = slice(h * CH, (h + 1) * CH)
                    last = A(Bt[rows, :, rows], b_a[rows, :, bass.ds(c * CH, CH)], ACT.Copy)
                last.then_inc(bd_b, 1)

            def evict(made, n, b, dst, h, evicted):
                act.wait_ge(made, n)
                A(dst[:, 4 * h:4 * h + 4, :], ps[:, 4 * h + b, :].rearrange("p (a b) -> p a b", a=4), ACT.Copy)\
                    .then_inc(evicted, 1)

            def chunk(c, first=False, last_=False):
                for n, dst in enumerate((Vs,) if last_ else (Bs, Ks, Vs)):
                    for h in range(2):
                        evict(tr_mm, c * 6 + (2 * n + h + 1), 2 if last_ else n, dst, h, tr_ev)
                if not last_:
                    removals_b(c + 1)
                for made, b, dst, evicted in ((rhs_mm, 1, RHS, rhs_ev), (u_mm, 2, U, u_ev)):
                    for h in range(2):
                        evict(made, c * 2 + (h + 1), b, dst, h, evicted)
                if first:
                    return
                for h in range(2):
                    act.wait_ge(ot_mm, c * 2 + (h + 1 - 2))
                    for e in range(2):
                        rows = slice(e * CH, (e + 1) * CH)
                        A(w_a[rows, 4 * h:4 * h + 4, bass.ds(c * CH, CH)],
                          ps[rows, 4 * h + 1, :].rearrange("p (a b) -> p a b", a=4)[:, :, rows], ACT.Copy).then_inc(ot_ev, 1)

            removals_b(0)
            chunk(0, first=True)
            with act.Fori(1, NCH - 1) as c:
                chunk(c)
            chunk(NCH - 1, last_=True)

            for b in range(4):
                act.wait_ge(ht_mm, b + 1)
                t, half = b // 2, b % 2
                own.done(A(acc[:, t, half * 512:(half + 1) * 512], ps[:, b, :], ACT.Copy), ht_cp)
            for m in range(PAIRS):
                act.wait_ge(gn_x, m + 1)
                own.done(A(gn_sq[:, m, :], w_a[:, m, CH:TP], ACT.Square), gn_sqd)
            for m in range(PAIRS):
                act.wait_ge(gn_var, m + 1)
                own.done(A(gn_std[:, m, :], ps[:, m % 4, 0:SEQ], ACT.Sqrt, bias=eps_gn, scale=1.0 / HD), gn_sd)
            for t in range(2):
                act.wait_ge(acc_ok, 2 * t + 2)
                own.done(A(utok[:, t, :], acc[:, t, :], ACT.Square, accum_out=normcol[:, 2, t:t + 1]), n4_ss)
                own.settle()
                own.done(A(rcol[:, 6, t:t + 1], normcol[:, 2, t:t + 1], ACT.Sqrt, bias=epsD, scale=1.0 / D), n4_std)
            for m in range(AHEAD):
                act.wait_ge(raw_in[m], 16)
                A(wsplit[:, m, 0, :], raw_w[:, m, :], ACT.Copy).then_inc(w_hi, 1)
            for n in range(4):
                t, half = n // 2, n % 2
                act.wait_ge(utT_mm, n + 1)
                own.done(A(utT[:, 4 * half:4 * half + 4, t * P:(t + 1) * P], ps[:, 4 + n, :].rearrange("p (a b) -> p a b", a=4),
                           ACT.Copy), utT_cp)
            act.wait_ge(lg_sub, 1)
            own.done(A(route[:, 2, :, 0:EXPERTS], route[:, 1, :, 0:EXPERTS], ACT.Exp), lg_exp)

            act.sem_inc(e_silu, 2)
            act.sem_inc(ye_ev, 1)
            act.wait_ge(npass_ok, 1)
            n = act.value_load(npass_i[0:1, 0:1], min_val=1, max_val=2)

            def highs(it, a, b):
                for m in range(a, b):
                    act.wait_ge(raw_in[m % NRAW], it * (16 * NHALF // NRAW) + 16 * (m // NRAW + 1))
                    act.wait_ge(w_used, it * NHALF + (m + 1))
                    A(wsplit[:, m % NRING, 0, :], raw_w[:, m % NRAW, :], ACT.Copy).then_inc(w_hi, 1)

            def tokens(j, made):
                for half in range(2):
                    act.wait_ge(xg_mm, made + (half + 1))
                    A(xsplit[:, j, 0, 4 * half:4 * half + 4, :], ps[:, 5 - half, :].rearrange("p (a b) -> p a b", a=4),
                      ACT.Copy).then_inc(xg_hi, 1)

            with act.Fori(0, n) as pas:
                tokens(0, pas * (TURNS * 4 + 2))
                with act.Fori(0, TURNS) as i:
                    it = pas * TURNS + i
                    tables = it * 2 + pas

                    def made(n_):
                        act.wait_ge(w_used, it * NHALF + (2 * n_ + 2 + NRING))

                    def hidden(q):
                        act.wait_ge(et_mm, it * NB2 + (q + 1))
                        A(hsplit[:, q % 2, 0, :, :], ps[:, 4, :].rearrange("p (a b) -> p a b", a=QB), ACT.Copy).then_inc(et_hi, 1)

                    highs(it, AHEAD, NRING)
                    for n_, (kind, q) in enumerate(TILES):
                        if kind == 0:
                            made(n_)
                            act.wait_ge(e_h, it * NB2 + (q + 1))
                            A(silu[:, q % 2, :], ps[:, q % 2, :], ACT.Silu).then_inc(e_silu, 1)
                            if q:
                                hidden(q - 1)
                        if (kind, q) == (2, NB2 - 1):
                            hidden(q)
                            tokens(0, tables * 2 + 4)
                        highs(it, *SPLITS[n_])
                        if (kind, q) == (2, XQ - 1):
                            tokens(1, tables * 2 + 2)
                        if kind == 2 and q % FB == FB - 1:
                            made(n_)
                            A(ye, ps[:, 6:8, :].rearrange("p a b -> p (a b)"), ACT.Copy).then_inc(ye_ev, 1)

        @block.vector
        def _(dve):
            v = nc.vector
            own = Own(dve)
            own.done(v.memset(route[:, :, :, :], 0.0), dve_own)
            own.done(v.memset(ranks[:, :, :], -1.0), dve_own)
            own.done(v.memset(normcol[:, 0, 0:1], EPS), dve_own)
            own.done(v.memset(normcol[:, 0, 1:2], HD * EPS), dve_own)
            own.done(v.memset(normcol[:, 1, 0:1], GN_EPS), dve_own)
            dve.wait_ge(in_tr, 5)
            own.done(v.tensor_copy(hT[:, :, 0:META], ps[:, 4, 0:KC * META].rearrange("p (k t) -> p k t", k=KC)), in_rest)
            dve.wait_ge(in_tr, 6)
            own.done(v.tensor_copy(par[:, :, :], ps[:, 5, 0:KC * NROW].rearrange("p (k t) -> p k t", k=KC)), in_rest)
            own.settle()
            own.done(v.tensor_scalar(one_minus_ka[:, :], par[:, :, R_KA], -1.0, 1.0, ALU.mult, ALU.add), dve_own)

            def rms(n):
                dve.wait_ge(norm_std, n)
                own.done(v.reciprocal(rstd, std), dve_own)
                own.settle()

            def normed_chunk(n, k):
                row = (R_MIXN, R_FFNN, R_MIXN + 1)[n - 1]
                own.done(v.scalar_tensor_tensor(uT[:, k, 1:T + 1], hT[:, k, :], par[:, k, row:row + 1], rstd,
                                                ALU.mult, ALU.mult), norm_u)

            def norm(n):
                rms(n)
                for k in range(KC):
                    normed_chunk(n, k)

            norm(1)
            dve.wait_ge(in_tr, 7)
            own.done(v.tensor_copy(sink[:, :], ps[:, 6, 0:HEADS]), in_rest)
            dve.wait_ge(kz_zero, 1)
            dve.wait_ge(ld_small, 16 * 5)
            own.done(v.memset(scores[:, :, :, :], 0.0), dve_own)
            own.done(v.memset(stat[:, :, :, :], 0.0), dve_own)
            own.settle()
            def head_norm(i):
                m = QK[i]
                dve.wait_ge(qk_std, i + 1)
                rs = rstd2[:, i % 2, :]
                own.done(v.reciprocal(rs, rs), dve_own)
                own.settle()
                if m < KC:
                    last = v.scalar_tensor_tensor(qT[:, m, :], raw[:, i % 2, :], qgain[:, 0:1], rs, ALU.mult, ALU.mult)
                else:
                    for h in range(2):
                        rows = slice(h * HD, (h + 1) * HD)
                        last = v.scalar_tensor_tensor(kz[rows, m - KC, h, :], raw[rows, i % 2, :], kgain[rows, 0:1],
                                                      rs[rows, :], ALU.mult, ALU.mult)
                own.done(last, qk_n)

            for i in range(KC + KVH - 1):
                head_norm(i)

            def masked(c):
                b = c % 2
                dve.wait_ge(sc_mm, c + 1)
                if c >= 2:
                    dve.wait_ge(pt_mm, c - 1)
                o1, o2, o0 = [scores[:, b, :, o:o + n] for o, n in SEG]
                m1, m2, m0 = [attmask[:, o:o + n].unsqueeze(1).to_broadcast([P, 2, n]) for o, n in SEG]
                v.tensor_tensor(o1, ps[:, 0, 0:288].rearrange("p (h k) -> p h k", h=2), m1, ALU.add)
                v.tensor_tensor(o0[0:META], ps[0:META, 0, 288:320].rearrange("p (h k) -> p h k", h=2), m0[0:META], ALU.add)
                own.done(v.tensor_tensor(o2, ps[:, 1:3, 0:T], m2, ALU.add), sc_rd)
                own.settle()
                st = stat[:, b, :, :].rearrange("p a (h s) -> p a h s", h=2)
                for s_, o in enumerate((o1, o2, o0)):
                    last = v.tensor_reduce(st[:, 0, :, s_], o, AX, ALU.max)
                own.done(last, dve_own)
                own.settle()
                sk = sink[:, 2 * c:2 * c + 2].unsqueeze(2).to_broadcast([P, 2, 3])
                own.done(v.tensor_tensor(st[:, 0], st[:, 0], sk, ALU.max), dve_own)
                own.settle()
                own.done(v.tensor_scalar(st[:, 1], st[:, 0], -1.0, None, ALU.mult), dve_own)
                own.settle()
                own.done(v.tensor_tensor(st[:, 3], st[:, 1], sk, ALU.add), sc_max)

            def normed(c):
                b = c % 2
                dve.wait_ge(sc_exp, c + 1)
                own.done(v.tensor_tensor(stat[:, b, 5, :], stat[:, b, 2, :], stat[:, b, 4, :], ALU.add), dve_own)
                own.settle()
                own.done(v.reciprocal(stat[:, b, 6, :], stat[:, b, 5, :]), dve_own)
                own.settle()
                st = stat[:, b, 6, :].rearrange("p (h s) -> p h s", h=2)
                for s_, (o, n) in enumerate(SEG):
                    w = scores[:, b, :, o:o + n]
                    last = v.tensor_tensor(w, w, st[:, :, s_:s_ + 1].to_broadcast([P, 2, n]), ALU.mult)
                own.done(last, p_ok)

            def copies(c):
                dve.wait_ge(pt_mm, c + 1)
                if c >= 2:
                    dve.wait_ge(pv_mm, c - 1)
                b = c % 2
                v.tensor_copy(pT[:, b, 512:768], ps[:, 4, 0:256])
                v.tensor_copy(pT[0:META, b, 1280:1312], ps[0:META, 4, 256:288])
                own.done(v.tensor_copy(pT[0:META, b, 768:1280], ps[0:META, 5, :]), pt_d)

            dve.wait_ge(consts_ok, 1)
            masked(0)
            head_norm(KC + KVH - 1)
            normed(0)
            masked(1)
            for c in range(PAIRS):
                copies(c)
                if c + 1 < PAIRS:
                    normed(c + 1)
                if c + 2 < PAIRS:
                    masked(c + 2)
            for m in range(KC):
                dve.wait_ge(wo_mm, m + 1)
                own.done(v.tensor_tensor(hT[:, m, :], hT[:, m, :], ps[:, m % 4, 0:T], ALU.add), wo_add)
            norm(2)

            dve.sem_inc(ffn_mul, QB)
            with dve.Fori(0, FB) as f:
                for q in range(QB):
                    dve.wait_ge(up_mm, f * QB + (q + 1))
                    dve.wait_ge(ffn_silu, f * QB + (q + 1 + QB))
                    v.tensor_tensor(hid[:, bass.ds(f * QB + q, 1), :], sgate[:, q:q + 1, :], ps[:, 4 + q:5 + q, 0:T],
                                    ALU.mult).then_inc(ffn_mul, 1)
            for k in range(KC):
                dve.wait_ge(down_q, k + 1)
                own.done(v.tensor_tensor(hT[:, k, :], hT[:, k, :], ps[:, k, 0:T], ALU.add), down_add)
            own.settle()

            def mix(k, buf, i):
                return v.scalar_tensor_tensor(xm[buf][:, k, :], xx[:, k, :], par[:, k, R_MIX + i:R_MIX + i + 1],
                                              uT[:, k, 1:T + 1], ALU.mult, ALU.add)

            rms(3)
            for k in range(KC + 2):
                if k < KC:
                    normed_chunk(3, k)
                if 1 <= k <= KC:
                    dve.wait_ge(norm_u, 2 * KC + k)
                    own.done(v.tensor_tensor(xx[:, k - 1, :], uT[:, k - 1, 0:T], uT[:, k - 1, 1:T + 1], ALU.subtract), xx_ok)
                if k >= 2:
                    dve.wait_ge(xx_ok, k - 1)
                    own.done(mix(k - 2, 0, 2), mixk_ok)

            def mixes(buf, i, free=None, n=0):
                if free is not None:
                    dve.wait_ge(free, n)
                for k in range(KC):
                    last = mix(k, buf, i)
                own.done(last, mix_ok)

            def kk_floor(m):
                dve.wait_ge(kk_ss, m + 1)
                own.done(v.tensor_scalar(r_a[:, m, PAD:TP], ps[:, 4 + m % 4, 0:T], 1e-24, None, ALU.max), kk_ev)

            mixes(1, 1)
            for m in range(PAIRS):
                dve.wait_ge(pr_ev, m + 1)
                own.done(v.tensor_scalar(kk_a[:, m, PAD:TP], k_a[:, m, PAD:TP], par[:, m, R_KK:R_KK + 1], None, ALU.mult), kk_ok)
            mixes(0, 4, pr_mm, KC)
            for m in range(4):
                kk_floor(m)
            mixes(1, 5, mix_used, 1)
            for m in range(4, PAIRS):
                kk_floor(m)
            mixes(0, 0, mix_used, 2)
            mixes(1, 3, mix_used, 3)
            dve.wait_ge(l2_ev, 2 * KC)
            for m in range(PAIRS):
                last = v.tensor_scalar(v_a[:, m, PAD:TP], b_a[:, m, PAD:TP], par[:, m, R_KA:R_KA + 1],
                                       one_minus_ka[:, m:m + 1], ALU.mult, ALU.add)
            own.done(last, dve_own)
            own.settle()
            own.done(v.tensor_tensor(k_a[:, :, PAD:TP], k_a[:, :, PAD:TP], v_a[:, :, PAD:TP], ALU.mult), dve_own)
            dve.wait_ge(kk_nrm, 1)
            own.done(v.reciprocal(r_a[:, :, PAD:TP], r_a[:, :, PAD:TP]), dve_own)
            own.settle()
            own.done(v.tensor_tensor(kk_a[:, :, PAD:TP], kk_a[:, :, PAD:TP], r_a[:, :, PAD:TP], ALU.mult), kk_done)
            own.settle()
            own.done(v.tensor_tensor(b_a[:, :, PAD:TP], b_a[:, :, PAD:TP], kk_a[:, :, PAD:TP], ALU.mult), dve_own)
            own.settle()
            dve.wait_ge(pads_zero, 3)
            for m in range(PAIRS):
                dve.wait_ge(pr_ev, KC + 1 + m)
                own.done(v.scalar_tensor_tensor(v_a[:, m, PAD:TP], r_a[:, m, PAD:TP], par[:, m, R_RK:R_RK + 1],
                                                k_a[:, m, PAD:TP], ALU.mult, ALU.mult), rk_ok)
                own.done(v.tensor_tensor_scan(cum[:, m % 2, :], reset[:, :], w_a[:, m, :], 0.0, ALU.mult, ALU.add), dve_own)
                own.settle()
                dve.wait_ge(rk_ok, m + 1)
                own.done(v.tensor_tensor(w_a[:, m, :], cum[:, m % 2, :], w_a[:, m, :], ALU.subtract), cum_ok)
                dve.wait_ge(dec_exp, m + 1)
                v.tensor_tensor(r_a[:, m, :], r_a[:, m, :], expo[:, 0, :], ALU.mult)
                v.tensor_copy(chunkdecay[:, m, :], expo[:, 0, :].rearrange("p (c i) -> p c i", c=NCH)[:, :, CH - 1])
                v.tensor_tensor(b_a[:, m, :], b_a[:, m, :], expo[:, 1, :], ALU.mult)
                v.tensor_tensor(k_a[:, m, :], k_a[:, m, :], expo[:, 1, :], ALU.mult)
                own.done(v.scalar_tensor_tensor(kk_a[:, m, :], kk_a[:, m, :], -1.0, expo[:, 2, :], ALU.mult, ALU.mult), dec_done)

            bc = lambda m_: m_.unsqueeze(1).to_broadcast([P, 4, P])
            halves = [slice(4 * h, 4 * h + 4) for h in range(2)]

            def removals_receptances(c):
                for src, j in ((kk_a, 0), (r_a, 1)):
                    for h in range(2):
                        rows = slice(h * CH, (h + 1) * CH)
                        last = v.tensor_copy(ARt[rows, :, j, rows], src[rows, :, bass.ds(c * CH, CH)])
                last.then_inc(bd_ar, 1)

            def chunk(c, first=False, last_=False):
                less = {k: 0 if first else n for k, n in LESS.items()}
                for n in range(4):
                    dst, h = (NA, KA)[n // 2], n % 2
                    w = P if first else 2 * P
                    dve.wait_ge(ap_mm, c * 4 + (n + 1))
                    for q in range(2):
                        last = v.tensor_tensor(
                            dst[:, 4 * h + 2 * q:4 * h + 2 * q + 2, :, :].rearrange("p a b c -> p a (b c)")[:, :, 0:w],
                            ps[:, 4 * h + 2 * (n // 2) + q, :].rearrange("p (a b) -> p a b", a=2)[:, :, 0:w],
                            causal[:, :, :].rearrange("p b c -> p (b c)")[:, 0:w].unsqueeze(1).to_broadcast([P, 2, w]), ALU.mult)
                    last.then_inc(ap_ev, 1)
                dve.wait_ge(ap_ev, c * 4 + 4)
                for hs in halves:
                    last = v.tensor_tensor(XT[:, hs, :], NA[:, hs, 0, :], bc(level1T[:, :]), ALU.mult)
                last.then_inc(rec_own, 1)
                dve.wait_ge(rec_own, c * 12 + (1 - less["rec"]))
                for hs in halves:
                    last = v.tensor_tensor(XT[:, hs, :], XT[:, hs, :], bc(ident[:, :]), ALU.add)
                last.then_inc(rec_own, 1)
                dve.wait_ge(rec_own, c * 12 + (2 - less["rec"]))
                for hs in halves:
                    v.transpose(X[:, hs, :].rearrange("p a b -> p (a b)"), XT[:, hs, :].rearrange("p a b -> p (a b)"))\
                        .then_inc(x_ok, 1)
                levels = NLV0 if first else NLV
                for l in range(levels):
                    for h, hs in enumerate(halves):
                        dve.wait_ge(y_mm, c * 10 + (2 * l + h + 1 - less["y"]))
                        v.tensor_tensor(Y[:, hs, :], ps[:, 4 * h + 3, :].rearrange("p (a b) -> p a b", a=4),
                                        bc(levelmask[:, l, :]), ALU.mult).then_inc(y_ev, 1)
                    for h, hs in enumerate(halves):
                        dve.wait_ge(x_mm, c * 10 + (2 * l + h + 1 - less["y"]))
                        b = ps[:, 4 * h, :].rearrange("p (a b) -> p a b", a=4)
                        if l < levels - 1:
                            v.tensor_tensor(X[:, hs, :], X[:, hs, :], b, ALU.add).then_inc(rec_own, 1)
                            dve.wait_ge(rec_own, c * 12 + (3 + 2 * l + h - less["rec"]))
                            v.transpose(XT[:, hs, :].rearrange("p a b -> p (a b)"), X[:, hs, :].rearrange("p a b -> p (a b)"))\
                                .then_inc(x_ok, 1)
                        else:
                            v.tensor_tensor(XT[:, hs, :], XT[:, hs, :], b, ALU.add).then_inc(x_ok, 1)
                if last_:
                    return
                if first:
                    dve.wait_ge(rhs_mm, 2)
                else:
                    dve.wait_ge(ot_mm, c * 2 + (2 - 2))
                removals_receptances(c + 1)
                for h, hs in enumerate(halves):
                    new = ps[:, 4 * h + 3, :].rearrange("p (a b) -> p a b", a=4)
                    decay = chunkdecay[:, hs, bass.ds(c, 1)].to_broadcast([P, 4, P])
                    dve.wait_ge(s_mm, c * 2 + (h + 1))
                    if first:
                        v.tensor_tensor(S[:, hs, :], new, decay, ALU.mult).then_inc(s_ok, 1)
                        continue
                    v.tensor_tensor(S[:, hs, :], S[:, hs, :], new, ALU.add).then_inc(rec_own, 1)
                    dve.wait_ge(rec_own, c * 12 + (11 + h - less["rec"]))
                    v.tensor_tensor(S[:, hs, :], S[:, hs, :], decay, ALU.mult).then_inc(s_ok, 1)

            dve.wait_ge(work_zero, 4)
            dve.wait_ge(dec_done, PAIRS)
            removals_receptances(0)
            for m in range(PAIRS):
                dve.wait_ge(rk_ev, m + 1)
                dve.wait_ge(pr_ev, 2 * KC + 1 + m)
                own.done(v.tensor_tensor(bonus[:, m, :], bonus[:, m, :], v_a[:, m, CH:TP], ALU.mult), dve_own)
            own.settle()
            chunk(0, first=True)
            with dve.Fori(1, NCH - 1) as c:
                chunk(c)
            chunk(NCH - 1, last_=True)

            dve.sem_inc(w_lo, NRAW)
            for m in range(PAIRS):
                dve.wait_ge(gn_mm, m + 1)
                o = w_a[:, m, CH:TP]
                own.done(v.scalar_tensor_tensor(o, ps[:, 4 + m % 4, 0:SEQ], -1.0 / HD, o, ALU.mult, ALU.add), gn_x)
            for m in range(PAIRS):
                dve.wait_ge(gn_sd, m + 1)
                own.done(v.reciprocal(gn_std[:, m, :], gn_std[:, m, :]), dve_own)
                own.settle()
                o = w_a[:, m, CH:TP]
                own.done(v.scalar_tensor_tensor(o, o, par[:, m, R_GNW:R_GNW + 1], gn_std[:, m, :], ALU.mult, ALU.mult), dve_own)
                own.settle()
                own.done(v.scalar_tensor_tensor(o, o, par[:, m, R_GNB:R_GNB + 1], bonus[:, m, :], ALU.add, ALU.add), dve_own)
                own.settle()
                own.done(v.tensor_tensor(o, o, g_a[:, m, :], ALU.mult), y_ok)
            for n in range(4):
                t, h = n // 2, n % 2
                dve.wait_ge(wo2_mm, n + 1)
                a_ = acc[:, t, h * 512:(h + 1) * 512]
                dve.wait_ge(ht_cp, 4)
                own.done(v.tensor_tensor(a_, a_, ps[:, n, :], ALU.add), acc_ok)
            dve.wait_ge(ld_gain, 16)
            for t in range(2):
                dve.wait_ge(n4_std, t + 1)
                own.done(v.reciprocal(rcol[:, 7, t:t + 1], rcol[:, 6, t:t + 1]), dve_own)
                own.settle()
                for half in range(2):
                    cs = slice(half * BLK, (half + 1) * BLK)
                    own.done(v.scalar_tensor_tensor(utok[:, t, cs], acc[:, t, cs], rcol[:, 7, t:t + 1], gainrow[:, cs],
                                                    ALU.mult, ALU.mult), utok_ok)
            v.memset(ye, 0.0)
            for m in range(AHEAD):
                dve.wait_ge(w_hi, m + 1)
                v.tensor_tensor(wsplit[:, m, 1, :], raw_w[:, m, :], wsplit[:, m, 0, :].bitcast(F32), ALU.subtract)\
                    .then_inc(w_lo, 1)

            col = lambda n: rcol[:, n, :]
            wide = lambda n: rcol[:, n, :].unsqueeze(2).to_broadcast([P, 2, EXPERTS])
            rt = lambda n: route[:, n, :, 0:EXPERTS]

            def step(ins, s_=dve_own):
                own.done(ins, s_)
                own.settle()

            dve.wait_ge(lg_mm, 1)
            step(v.tensor_copy(rt(3), ps[:, 0, 0:16].rearrange("p (t e) -> p t e", t=2)))
            step(v.tensor_reduce(col(0), rt(3), AX, ALU.max))
            step(v.tensor_tensor(rt(1), rt(3), wide(0), ALU.subtract), lg_sub)
            dve.wait_ge(lg_exp, 1)
            step(v.tensor_reduce(col(1), rt(2), AX, ALU.add))
            step(v.reciprocal(col(2), col(1)))
            step(v.tensor_tensor(rt(3), rt(2), wide(2), ALU.mult))
            for n, src, best in ((0, 3, 3), (1, 7, 4)):
                step(v.tensor_reduce(col(best), rt(src), AX, ALU.max))
                step(v.tensor_tensor(rt(4), rt(src), wide(best), ALU.is_equal))
                step(v.scalar_tensor_tensor(rt(5), rt(4), -8.0, expno8[:, :, :], ALU.mult, ALU.add))
                step(v.tensor_reduce(col(5), rt(5), AX, ALU.min))
                step(v.tensor_tensor(rt(8 + n), expno[:, :, :], wide(5), ALU.is_equal))
                if n == 0:
                    step(v.scalar_tensor_tensor(rt(7), rt(8), -2.0, rt(3), ALU.mult, ALU.add))
            step(v.tensor_tensor(rt(0), rt(8), rt(9), ALU.add), mask_ok)
            step(v.tensor_tensor(rt(6), rt(3), rt(0), ALU.mult))
            step(v.tensor_reduce(col(1), rt(6), AX, ALU.add))
            step(v.reciprocal(col(2), col(1)))
            step(v.tensor_tensor(rt(10), rt(6), wide(2), ALU.mult))
            dve.wait_ge(rank_mm, 1)
            step(v.tensor_copy(ranks[:, :, 0:EXPERTS], ps[:, 1, 0:24].rearrange("p (t e) -> p t e", t=3)))
            step(v.tensor_reduce(rcol[:, 0, 0:1], ranks[:, 2, 0:EXPERTS], AX, ALU.max))
            step(v.tensor_scalar(npass_i[:, :], rcol[:, 0, 0:1], float(P), 1.0, ALU.is_gt, ALU.add), npass_ok)

            dve.sem_inc(e_h, 2)
            dve.sem_inc(et_ev, 1)
            dve.sem_inc(es_add, 1)
            n = dve.value_load(npass_i[0:1, 0:1], min_val=1, max_val=2)
            chosen, gate = route[:, 0, :, :], route[:, 10, :, :]

            def choose(j, expert):
                e = bass.ds(expert, 1)
                for t in range(2):
                    v.tensor_scalar(sel[:, j, t, :], slotno[:, :], ranks[:, t, e], chosen[:, t, e], ALU.is_equal, ALU.mult)
                    last = v.tensor_scalar(selg[:, j, t, :], slotno[:, :], ranks[:, t, e], gate[:, t, e],
                                           ALU.is_equal, ALU.mult)
                last.then_inc(sel_ok, 1)

            def lows(it, a, b):
                for m in range(a, b):
                    dve.wait_ge(w_hi, it * NHALF + (m + 1))
                    v.tensor_tensor(wsplit[:, m % NRING, 1, :], raw_w[:, m % NRAW, :],
                                    wsplit[:, m % NRING, 0, :].bitcast(F32), ALU.subtract).then_inc(w_lo, 1)

            def tokens(j, made):
                for half in range(2):
                    dve.wait_ge(xg_hi, made + (half + 1))
                    ks = slice(4 * half, 4 * half + 4)
                    v.tensor_tensor(xsplit[:, j, 1, ks, :], ps[:, 5 - half, :].rearrange("p (a b) -> p a b", a=4),
                                    xsplit[:, j, 0, ks, :].bitcast(F32), ALU.subtract).then_inc(xg_ev, 1)

            def gate_rows(j, made):
                dve.wait_ge(st_mm, made)
                v.tensor_copy(selT[:, j, :, :], ps[:, 5, 0:256].rearrange("p (a b) -> p a b", a=2)).then_inc(st_ev, 1)

            def collect(o, made):
                dve.wait_ge(es_mm, made)
                t, h = o // 2, o % 2
                a_ = acc[:, t, h * BLK:(h + 1) * BLK]
                v.tensor_tensor(a_, a_, ps[:, 5, :], ALU.add).then_inc(es_add, 1)

            with dve.Fori(0, n) as pas:
                choose(0, 0)
                v.memset(selT[:, 1, :, :], 0.0)
                tokens(0, pas * (TURNS * 4 + 2))
                gate_rows(0, pas * (TURNS * 2 + 1) + 1)
                with dve.Fori(0, TURNS) as i:
                    it = pas * TURNS + i
                    tables = it * 2 + pas
                    adds = it * 8 + pas * 4

                    def hidden_lo(q):
                        dve.wait_ge(et_hi, it * NB2 + (q + 1))
                        v.tensor_tensor(hsplit[:, q % 2, 1, :, :], ps[:, 4, :].rearrange("p (a b) -> p a b", a=QB),
                                        hsplit[:, q % 2, 0, :, :].bitcast(F32), ALU.subtract).then_inc(et_ev, 1)

                    lows(it, AHEAD, NRING)
                    for n_, (kind, q) in enumerate(TILES):
                        if kind == 0:
                            if q == XQ + 1:
                                gate_rows(1, tables + 2)
                            if q in LATE:
                                _, o, n0 = LATE[q]
                                collect(o, adds + (n0 + 1))
                            if q:
                                hidden_lo(q - 1)
                        elif kind == 1:
                            dve.wait_ge(w_used, it * NHALF + (2 * n_ + 2 + NRING))
                            dve.wait_ge(e_silu, it * NB2 + (q + 3))
                            v.tensor_tensor(hbuf[:, q % 2, :], silu[:, q % 2, :], ps[:, 2 + q % 2, :], ALU.mult).then_inc(e_h, 1)
                            if q in LATE:
                                collect(o + 1, adds + (n0 + 2))
                            if q == 3:
                                choose(1, 2 * i + 1)
                            if q == FB + 3:
                                choose(0, 2 * i + 2)
                        if (kind, q) == (2, NB2 - 1):
                            hidden_lo(q)
                            tokens(0, tables * 2 + 4)
                            gate_rows(0, tables + 3)
                        lows(it, *SPLITS[n_])
                        if (kind, q) == (2, XQ - 1):
                            tokens(1, tables * 2 + 2)
                turns = pas * TURNS + TURNS
                for o in range(4):
                    collect(o, turns * 8 + pas * 4 + (o + 1))
                v.tensor_scalar(ranks[:, 0:2, :], ranks[:, 0:2, :], -float(P), None, ALU.add).then_inc(rec_own, 1)
                dve.wait_ge(rec_own, pas + (12 * NCH - LESS["rec"] - 2 + 1))
                dve.wait_ge(es_add, turns * 8 + pas * 4 + 5)
            dve.sem_inc(acc_done, 1)


_INS = ['x', 'meta_tokens', 'mixer_norm', 'ffn_norm', 'attn_w_qkv', 'attn_q_norm', 'attn_k_norm', 'attn_sinks',
        'attn_w_o', 'rwkv_mix', 'rwkv_w0', 'rwkv_w1', 'rwkv_w2', 'rwkv_a0', 'rwkv_a1', 'rwkv_a2', 'rwkv_g1', 'rwkv_g2',
        'rwkv_k_k', 'rwkv_k_a', 'rwkv_r_k', 'rwkv_w_r', 'rwkv_w_k', 'rwkv_w_v', 'rwkv_w_o', 'rwkv_gn_w', 'rwkv_gn_b',
        'ffn_w_gate', 'ffn_w_up', 'ffn_w_down', 'moe_router', 'moe_w_gate', 'moe_w_up', 'moe_w_down']


def kernel(**inputs):
    import numpy as _np
    import concourse.bacc as _bacc
    from concourse import mybir as _mybir
    from concourse.bass_utils import run_bass_kernel_spmd as _run

    nc = _bacc.Bacc("TRN2", target_bir_lowering=False, num_devices=1)
    arrays, args = {}, []
    for name in _INS:
        a = _np.ascontiguousarray(inputs[name])
        arrays[f"in_{name}"] = a
        args.append(nc.dram_tensor(f"in_{name}", a.shape, _mybir.dt.from_np(a.dtype), kind="ExternalInput").ap())
    args.append(nc.dram_tensor("out_0", (1, SEQ, D), _mybir.dt.float32, kind="ExternalOutput").ap())
    build(nc, *args)
    r = _run(nc, [arrays], core_ids=[0])
    return r.results[0]["out_0"]
```
